# Optimizing a Trainium2 kernel written in Bass

```python
import jax, jax.numpy as jnp
from jax import lax
import numpy as np

D_MODEL = 1024
BATCH = 1
SEQ = 512
DEPTH = 2
DEC_BATCH = 8
DEC_SEQ = 1
PAST_LEN = 2048
PAGE_SIZE = 128

N_A_LAYERS = DEPTH // 2
N_B_LAYERS = DEPTH - N_A_LAYERS
D_FF = 2816
HG_HEADS = 8
HG_DK = D_MODEL // HG_HEADS
HG_DV = D_MODEL // HG_HEADS
HG_CHUNK = 64
MLA_HEADS = 8
QK_NOPE = 128
QK_ROPE = 64
V_HEAD = 128
KV_RANK = 256
Q_RANK = 384
ROPE_THETA = 10000.0
Q_BLOCK = 128
EPS = 1e-6
SM_SCALE = (QK_NOPE + QK_ROPE) ** -0.5

kernel_name = 'hgrn2_mla_yoco_macaron_step'

def rmsnorm(x, g):
    xf = x.astype(jnp.float32)
    xf = xf * lax.rsqrt(jnp.mean(xf * xf, axis=-1, keepdims=True) + EPS)
    return xf.astype(x.dtype) * g

def rope(x, pos):
    half = QK_ROPE // 2
    inv_freq = ROPE_THETA ** (-2.0 * jnp.arange(half, dtype=jnp.float32) / QK_ROPE)
    ang = pos.astype(jnp.float32)[:, None] * inv_freq[None, :]
    ang = ang.reshape((ang.shape[0],) + (1,) * (x.ndim - 3) + (half,))
    cos, sin = jnp.cos(ang), jnp.sin(ang)
    xf = x.astype(jnp.float32)
    x1, x2 = xf[..., :half], xf[..., half:]
    return jnp.concatenate([x1 * cos - x2 * sin, x2 * cos + x1 * sin], axis=-1).astype(x.dtype)

def swiglu(h, w_gu, w_down):
    a, b = jnp.split(h @ w_gu, 2, axis=-1)
    return (jax.nn.silu(a) * b) @ w_down

def gla_chunked(q, k, v, logg):
    Bn, T, H, DK = q.shape
    DV = v.shape[-1]
    C = HG_CHUNK
    n = T // C

    def to_chunks(a):
        return a.reshape(Bn, n, C, H, a.shape[-1]).transpose(1, 0, 3, 2, 4)

    causal = jnp.tril(jnp.ones((C, C), dtype=bool))[:, :, None]

    def step(S, inp):
        qc, kc, vc, gc = inp
        b = jnp.cumsum(gc, axis=2)
        o_inter = jnp.einsum('bhtk,bhkv->bhtv', qc * jnp.exp(b), S)
        diff = b[:, :, :, None, :] - b[:, :, None, :, :]
        decay = jnp.exp(jnp.where(causal, diff, -jnp.inf))
        attn = jnp.einsum('bhtk,bhsk,bhtsk->bhts', qc, kc, decay)
        o = o_inter + jnp.einsum('bhts,bhsv->bhtv', attn, vc)
        b_last = b[:, :, -1:, :]
        S = jnp.exp(b_last[:, :, 0, :, None]) * S + jnp.einsum('bhsk,bhsv->bhkv', kc * jnp.exp(b_last - b), vc)
        return S, o

    S0 = jnp.zeros((Bn, H, DK, DV), jnp.float32)
    S, o = lax.scan(step, S0, (to_chunks(q), to_chunks(k), to_chunks(v), to_chunks(logg)))
    return o.transpose(1, 0, 3, 2, 4).reshape(Bn, T, H, DV), S

def gla_tokens(q, k, v, logg, S0):
    def step(S, inp):
        qt, kt, vt, gt = inp
        S = jnp.exp(gt)[..., None] * S + kt[..., :, None] * vt[..., None, :]
        return S, jnp.einsum('bhk,bhkv->bhv', qt, S)

    tm = lambda a: a.transpose(1, 0, 2, 3)
    S, o = lax.scan(step, S0, (tm(q), tm(k), tm(v), tm(logg)))
    return tm(o), S

def hgrn_layer(h, mix, a, lb, w_in, g_out, w_out):
    Bn, T, _ = h.shape
    q, f, i, g = jnp.split(h @ w_in, 4, axis=-1)
    ff = f.astype(jnp.float32)
    log_forget = jnp.logaddexp(jnp.log(lb), jnp.log1p(-lb) + jax.nn.log_sigmoid(ff))
    k = (1.0 - lb) * jax.nn.sigmoid(-ff)
    heads = lambda t: t.reshape(Bn, T, HG_HEADS, -1).astype(jnp.float32)
    o, S = mix(a, heads(jax.nn.silu(q)), heads(k), heads(i), heads(log_forget))
    o = rmsnorm(o, g_out.reshape(HG_HEADS, HG_DV)).reshape(Bn, T, -1).astype(h.dtype)
    return (o * jax.nn.silu(g)) @ w_out, S

def shared_kv(x, sc, pos, kv_w_ada, kv_b_ada, kv_g_norm, kv_w_down, kv_g_latent):
    shift, scale = jnp.split(sc @ kv_w_ada + kv_b_ada, 2, axis=-1)
    h = rmsnorm(x, kv_g_norm) * (1 + scale[:, None]) + shift[:, None]
    z = h @ kv_w_down
    return rmsnorm(z[..., :KV_RANK], kv_g_latent), rope(z[..., KV_RANK:], pos)

def attend_prompt(q_lat, q_rope, ckv, krope):
    Bn, S, H, R = q_lat.shape
    nb = S // Q_BLOCK

    def blocks(a):
        return a.reshape(Bn, nb, Q_BLOCK, H, a.shape[-1]).transpose(1, 0, 2, 3, 4)

    kpos = jnp.arange(S)

    def one_block(args):
        ql, qr, start = args
        s = jnp.einsum('bqhr,bkr->bhqk', ql, ckv) + jnp.einsum('bqhd,bkd->bhqk', qr, krope)
        qpos = start + jnp.arange(Q_BLOCK)
        s = jnp.where(kpos[None, :] <= qpos[:, None], s.astype(jnp.float32) * SM_SCALE, -jnp.inf)
        p = jax.nn.softmax(s, axis=-1).astype(ckv.dtype)
        return jnp.einsum('bhqk,bkr->bqhr', p, ckv)

    out = lax.map(one_block, (blocks(q_lat), blocks(q_rope), jnp.arange(nb) * Q_BLOCK))
    return out.transpose(1, 0, 2, 3, 4).reshape(Bn, S, H, R)

def attend_paged(q_lat, q_rope, ckv_new, krope_new, cache_ckv, cache_krope, page_table):
    T = q_lat.shape[1]
    R = ckv_new.shape[-1]
    causal = jnp.tril(jnp.ones((T, T), dtype=bool))[None]

    def one_seq(args):
        ql, qr, cn, kn, pages = args
        past_c = cache_ckv[pages].reshape(-1, R)
        past_k = cache_krope[pages].reshape(-1, QK_ROPE)
        s_past = jnp.einsum('thr,lr->htl', ql, past_c) + jnp.einsum('thd,ld->htl', qr, past_k)
        s_new = jnp.einsum('thr,ur->htu', ql, cn) + jnp.einsum('thd,ud->htu', qr, kn)
        s_new = jnp.where(causal, s_new.astype(jnp.float32) * SM_SCALE, -jnp.inf)
        s = jnp.concatenate([s_past.astype(jnp.float32) * SM_SCALE, s_new], axis=-1)
        p = jax.nn.softmax(s, axis=-1).astype(cn.dtype)
        L = past_c.shape[0]
        return jnp.einsum('htl,lr->thr', p[..., :L], past_c) + jnp.einsum('htu,ur->thr', p[..., L:], cn)

    return lax.map(one_seq, (q_lat, q_rope, ckv_new, krope_new, page_table))

def mla_layer(h, pos, attend, ckv, krope, w_dq, g_q, w_uq, w_uk, w_uv, w_out):
    Bn, T, _ = h.shape
    qc = rmsnorm(h @ w_dq, g_q)
    q = jnp.einsum('btr,rhd->bthd', qc, w_uq)
    q_lat = jnp.einsum('bthn,rhn->bthr', q[..., :QK_NOPE], w_uk)
    q_rope = rope(q[..., QK_NOPE:], pos)
    o_lat = attend(q_lat, q_rope, ckv, krope)
    o = jnp.einsum('bthr,rhv->bthv', o_lat, w_uv).reshape(Bn, T, -1)
    return o @ w_out

def trunk(x, c, pos, mix, attend, w_ada, b_ada, g_norm, w_ffn_gu, w_ffn_down, hg_w_in, hg_lb, hg_g_out,
          hg_w_out, kv_w_ada, kv_b_ada, kv_g_norm, kv_w_down, kv_g_latent, kv_w_uk, kv_w_uv, q_w_down,
          q_g_norm, q_w_up, attn_w_out, g_final):
    Bn, T, D = x.shape
    sc = jax.nn.silu(c)
    lb_all = jnp.cumsum(jax.nn.softmax(hg_lb.astype(jnp.float32), axis=0), axis=0)
    states = []
    ckv = krope = None
    for l in range(DEPTH):
        if l == N_A_LAYERS:
            ckv, krope = shared_kv(x, sc, pos, kv_w_ada, kv_b_ada, kv_g_norm, kv_w_down, kv_g_latent)
        mods = (sc @ w_ada[l] + b_ada[l]).reshape(Bn, 3, 3, D)[:, :, :, None, :]

        def mod(y, j):
            return rmsnorm(y, g_norm[l, j]) * (1 + mods[:, j, 1]) + mods[:, j, 0]

        x = x + 0.5 * mods[:, 0, 2] * swiglu(mod(x, 0), w_ffn_gu[l, 0], w_ffn_down[l, 0])
        h = mod(x, 1)
        if l < N_A_LAYERS:
            y, S = hgrn_layer(h, mix, l, lb_all[l], hg_w_in[l], hg_g_out[l], hg_w_out[l])
            states.append(S)
        else:
            b = l - N_A_LAYERS
            y = mla_layer(h, pos, attend, ckv, krope, q_w_down[b], q_g_norm[b], q_w_up[b], kv_w_uk, kv_w_uv,
                          attn_w_out[b])
        x = x + mods[:, 1, 2] * y
        x = x + 0.5 * mods[:, 2, 2] * swiglu(mod(x, 2), w_ffn_gu[l, 1], w_ffn_down[l, 1])
    return rmsnorm(x, g_final), jnp.stack(states), ckv, krope

def setup_inputs(seed: int = 0) -> dict:
    key = jax.random.key(seed)
    ks = iter(jax.random.split(key, 40))
    D = D_MODEL
    n_pages = PAST_LEN // PAGE_SIZE
    n_pool = (DEC_BATCH * n_pages * 5) // 4

    def nrm(shape, scale):
        return scale * jax.random.normal(next(ks), shape, jnp.float32)

    def gain(shape):
        return 1.0 + nrm(shape, 0.02)

    page_table = jax.random.permutation(next(ks), n_pool)[: DEC_BATCH * n_pages]
    page_table = page_table.reshape(DEC_BATCH, n_pages).astype(jnp.int32)
    return {
        'x_prompt': nrm((BATCH, SEQ, D), 1.0),
        'x_sample': nrm((DEC_BATCH, DEC_SEQ, D), 1.0),
        'c_prompt': nrm((BATCH, D), 1.0),
        'c_sample': nrm((DEC_BATCH, D), 1.0),
        'state_hgrn': nrm((N_A_LAYERS, DEC_BATCH, HG_HEADS, HG_DK, HG_DV), 0.5),
        'cache_ckv': nrm((n_pool, PAGE_SIZE, KV_RANK), 1.0),
        'cache_krope': nrm((n_pool, PAGE_SIZE, QK_ROPE), 1.0),
        'page_table': page_table,
        'w_ada': nrm((DEPTH, D, 9 * D), 0.5 * D ** -0.5),
        'b_ada': nrm((DEPTH, 9 * D), 0.02),
        'g_norm': gain((DEPTH, 3, D)),
        'w_ffn_gu': nrm((DEPTH, 2, D, 2 * D_FF), D ** -0.5),
        'w_ffn_down': nrm((DEPTH, 2, D_FF, D), D_FF ** -0.5),
        'hg_w_in': nrm((N_A_LAYERS, D, 4 * D), D ** -0.5),
        'hg_lb': nrm((N_A_LAYERS + 1, D), 0.5),
        'hg_g_out': gain((N_A_LAYERS, D)),
        'hg_w_out': nrm((N_A_LAYERS, D, D), D ** -0.5),
        'kv_w_ada': nrm((D, 2 * D), 0.5 * D ** -0.5),
        'kv_b_ada': nrm((2 * D,), 0.02),
        'kv_g_norm': gain((D,)),
        'kv_w_down': nrm((D, KV_RANK + QK_ROPE), D ** -0.5),
        'kv_g_latent': gain((KV_RANK,)),
        'kv_w_uk': nrm((KV_RANK, MLA_HEADS, QK_NOPE), KV_RANK ** -0.5),
        'kv_w_uv': nrm((KV_RANK, MLA_HEADS, V_HEAD), KV_RANK ** -0.5),
        'q_w_down': nrm((N_B_LAYERS, D, Q_RANK), D ** -0.5),
        'q_g_norm': gain((N_B_LAYERS, Q_RANK)),
        'q_w_up': nrm((N_B_LAYERS, Q_RANK, MLA_HEADS, QK_NOPE + QK_ROPE), Q_RANK ** -0.5),
        'attn_w_out': nrm((N_B_LAYERS, MLA_HEADS * V_HEAD, D), (MLA_HEADS * V_HEAD) ** -0.5),
        'g_final': gain((D,)),
    }

def reference(x_prompt, x_sample, c_prompt, c_sample, state_hgrn, cache_ckv, cache_krope, page_table, w_ada,
              b_ada, g_norm, w_ffn_gu, w_ffn_down, hg_w_in, hg_lb, hg_g_out, hg_w_out, kv_w_ada, kv_b_ada,
              kv_g_norm, kv_w_down, kv_g_latent, kv_w_uk, kv_w_uv, q_w_down, q_g_norm, q_w_up, attn_w_out,
              g_final):
    pos_prompt = jnp.arange(SEQ)
    pos_sample = PAST_LEN + jnp.arange(DEC_SEQ)

    def prompt_mix(a, q, k, v, g):
        return gla_chunked(q, k, v, g)

    def sample_mix(a, q, k, v, g):
        return gla_tokens(q, k, v, g, state_hgrn[a].astype(jnp.float32))

    def sample_attend(ql, qr, cn, kn):
        return attend_paged(ql, qr, cn, kn, cache_ckv, cache_krope, page_table)

    y_prompt, st_prompt, ckv_prompt, krope_prompt = trunk(
        x_prompt, c_prompt, pos_prompt, prompt_mix, attend_prompt, w_ada, b_ada, g_norm, w_ffn_gu, w_ffn_down,
        hg_w_in, hg_lb, hg_g_out, hg_w_out, kv_w_ada, kv_b_ada, kv_g_norm, kv_w_down, kv_g_latent, kv_w_uk,
        kv_w_uv, q_w_down, q_g_norm, q_w_up, attn_w_out, g_final)
    y_sample, st_sample, ckv_sample, krope_sample = trunk(
        x_sample, c_sample, pos_sample, sample_mix, sample_attend, w_ada, b_ada, g_norm, w_ffn_gu, w_ffn_down,
        hg_w_in, hg_lb, hg_g_out, hg_w_out, kv_w_ada, kv_b_ada, kv_g_norm, kv_w_down, kv_g_latent, kv_w_uk,
        kv_w_uv, q_w_down, q_g_norm, q_w_up, attn_w_out, g_final)
    return (y_prompt, y_sample, st_prompt.astype(state_hgrn.dtype), st_sample.astype(state_hgrn.dtype),
            ckv_prompt, krope_prompt, ckv_sample, krope_sample)


_drawn_inputs = setup_inputs


def setup_inputs(seed=0):
    import zlib

    import numpy as np

    out = dict(_drawn_inputs(seed))
    spreads = {}
    factors = {'cache_ckv': 5.157,
     'cache_krope': 8.0,
     'g_norm': 3.114,
     'hg_g_out': 8.0,
     'kv_g_norm': 8.438,
     'kv_g_latent': 8.012,
     'q_g_norm': 8.0,
     'g_final': 2.732,
     'kv_b_ada': 2.759}
    for name, (base, spread) in spreads.items():
        noise = np.random.default_rng([zlib.crc32(name.encode()), seed]).standard_normal(out[name].shape)
        drawn = base * np.exp(spread * noise) if base else spread * noise
        out[name] = __import__('jax').numpy.asarray(drawn.astype(out[name].dtype))
    for name, factor in factors.items():
        out[name] = (out[name] * factor).astype(out[name].dtype)
    return out
```

```python
from contextlib import ExitStack, contextmanager

import concourse.bass as bass
from concourse import mybir

F32 = mybir.dt.float32
F32R = mybir.dt.float32r
U32 = mybir.dt.uint32
I32 = mybir.dt.int32
ALU = mybir.AluOpType
ACT = mybir.ActivationFunctionType
AX_X = mybir.AxisListType.X

P = 128
D = 1024
KD = D // P
NP = 512
NS = 8
NT = NP + NS
HT = NT // 2
DFF = 2816
MF = DFF // P
MFA = 12
MFB = MF - MFA
H = 8
KV = 256
RK = KV // P
RQ = 384
QK = RQ // P
ROPE = 64
PAST = 2048
PAGE = 128
NPG = PAST // PAGE
SEQS = 1 + NS
EPS = 1e-6
SM_SCALE = (P + ROPE) ** -0.5
RAW = 4
SLOT = 2048
LAND = 64
ADA_W = 256
ADA_L = 9 * D // ADA_W
C_L0, C_KV, C_L1 = 0, 72, 88
NMOD = 160
V_NORM, V_FINAL, V_KVN, V_LAT, V_Q, V_HG, V_LB = 0, 48, 56, 64, 66, 69, 77
NVEC = 93
NEG = -3.0e38
K_ID, K_ROT, K_CAUS, K_COMB, K_NEW, K_END = 0, 128, 256, 384, 400, 464
ADA_FIRST = 14
ADA_FFN = MF
ADA_TAIL = ADA_L - ADA_FFN - H
SLOTS = 2 * ADA_L + H + 4 * (MF + 16) + 2 * H + 2 + 2 + 12 + 1 + 2 * 4


class Tally:

    def __init__(self):
        self.n, self.per, self.i = {}, {}, None

    def add(self, key, by=1):
        self.n[key] = self.n.get(key, 0) + by

    def at(self, key, extra=0, times=1):
        v = self.n.get(key, 0) * times + extra
        if self.i is not None and self.per.get(key, 0):
            return self.i * (self.per[key] * times) + v
        return v

    @contextmanager
    def loop(self, eng, count, per):
        before = dict(self.n)
        with eng.Fori(0, count) as i:
            self.i, self.per = i, per
            yield i
        self.i = None
        for k in list(self.n):
            step = self.n[k] - before.get(k, 0)
            assert step == per.get(k, 0), (k, step, per.get(k, 0))
            self.n[k] = before.get(k, 0) + count * step
        self.per = {}


def hgrn_events(project):
    t = (lambda a, n: [("tiles", a, n)]) if project else (lambda a, n: [])
    ada = (lambda j: [("ada", j, 0)]) if project else (lambda j: [])
    comb = (lambda j: [("comb", j, 0)]) if project else (lambda j: [])
    g = lambda kind, j=0: [(kind, j, 0)]
    return (g("vt") + t(0, 3) + g("level", 0) + t(3, 3) + g("level", 1) + t(6, 3) + g("level", 2) + t(9, 3)
            + g("level", 3) + t(12, 2) + g("outer", 0) + t(14, 2) + ada(0) + g("level", 4) + t(16, 2) + comb(0)
            + g("level", 5) + t(18, 2) + g("outer", 1) + t(20, 2) + g("level", 6) + t(22, 2) + g("level", 7)
            + t(24, 2) + g("kt") + t(26, 2) + g("state") + t(28, 2) + g("out") + t(30, 2) + ada(1)
            + g("outs") + comb(1))


def project_events():
    return [("tiles", 0, 16), ("ada", 0, 0), ("tiles", 16, 8), ("comb", 0, 0), ("tiles", 24, 8), ("ada", 1, 0),
            ("comb", 1, 0)]


def build(nc, a, y_prompt, y_sample, st_prompt, st_sample, ckv_prompt, kr_prompt, ckv_sample, kr_sample):
    ctx = ExitStack()
    with ctx:
        at = [(nc.sbuf_base + 63) // 64 * 64]

        def place(name, shape, dt=F32, where=None):
            words = 1
            for s in shape[1:]:
                words *= s
            off = at[0] if where is None else where
            if where is None:
                at[0] += (4 * words + 63) // 64 * 64
            return nc.alloc_sbuf_tensor_at(name, list(shape), dt, offset=off)

        def group(first, *parts):
            out, off = [], first
            for name, shape, dt in parts:
                words = 1
                for s in shape[1:]:
                    words *= s
                out.append(place(name, shape, dt, off))
                off += (4 * words + 63) // 64 * 64
            return out, off

        def sem(name):
            return ctx.enter_context(nc.semaphore(name))

        x = place("x", [P, KD, NT])
        hn_hi = place("hn_hi", [P, KD, NT], F32R)
        hn_lo = place("hn_lo", [P, KD, NT], F32R)
        raw = place("raw", [P, RAW, SLOT])
        w_hi = place("w_hi", [P, 2, SLOT], F32R)
        w_lo = place("w_lo", [P, 2, SLOT], F32R)
        mods = place("mods", [P, NMOD, SEQS])
        bias = place("bias", [P, NMOD])
        vec = place("vec", [P, NVEC])
        amod = place("amod", [P, KD, SEQS])
        gate = place("gate", [P, KD * SEQS])
        sc18 = place("sc18", [P, KD, 2 * SEQS], F32R)
        cst = place("cst", [P, K_END])
        ident = cst[:, K_ID:K_ID + P]
        rot = cst[:, K_ROT:K_ROT + P]
        causal = cst[:, K_CAUS:K_CAUS + P]
        comb = cst[0:2 * SEQS, K_COMB:K_COMB + SEQS]
        newmask = cst[0:H, K_NEW:K_NEW + 64]
        ident_r = place("ident_r", [P, P], F32R)
        ones = place("ones", [P, P])
        eps = place("eps", [P, 1])
        low = place("low", [P, 2, H])
        rows = place("rows", [2 * SEQS, ADA_W])
        t9 = place("t9", [P, 2, SEQS])
        pt_sb = place("pt_sb", [1, NS * NPG], I32)
        tabs = at[0]
        cossin = place("cossin", [P, 2, NT])
        lmask = place("lmask", [P, 8, P], U32, tabs)
        lat = at[0]
        ck_hi = place("ck_hi", [P, RK, NT], F32R)
        ck_lo = place("ck_lo", [P, RK, NT], F32R)
        kr2 = place("kr2", [P, NT])
        ckn = place("ckn", [NS, KV + ROPE])
        ql = place("ql", [P, RK, NS, H])
        qrs = place("qrs", [ROPE, NS, H])
        qsamp = place("qsamp", [P, 2, RK + 1, H])
        cnew = place("cnew", [P, RK, NS])
        scr = at[0]
        sq = place("sq", [P, 2, NT])
        root = place("root", [P, NT])
        rstd = place("rstd", [P, NT])
        tn = place("tn", [P, 2, NT])
        tt = place("tt", [P, 2, NT])
        ar = at[0]
        end = nc.sbuf_usable_end
        (xr, xs, cr, vrow, brow0, brow1, scf), e0 = group(
            ar, ("xr", [P, 4, D], F32), ("xs", [NS, D], F32), ("cr", [SEQS, D], F32), ("vrow", [NVEC, P], F32),
            ("brow0", [C_L1, P], F32), ("brow1", [NMOD - C_L1, P], F32), ("scf", [P, KD, SEQS], F32))
        (hid_hi, hid_lo), e1 = group(ar, ("hid_hi", [P, MFA, NT], F32R), ("hid_lo", [P, MFA, NT], F32R))
        (sg, hf), e2 = group(scr, ("sg", [P, 2, NT], F32), ("hf", [P, NT], F32))
        (og, gg, qs, fg, kk, vv), e3 = group(
            ar, ("og", [P, H, NT], F32), ("gg", [P, H, NT], F32), ("qs", [P, 2, NT], F32), ("fg", [P, 2, NT], F32),
            ("kk", [P, 2, NT], F32), ("vv", [P, 2, NT], F32))
        (sgq, sgg, s1, s2, attn, vn, kn_n, tot), e4 = group(
            scr, ("sgq", [P, NT], F32), ("sgg", [P, NT], F32), ("s1", [P, NT], F32), ("s2", [P, NT], F32),
            ("attn", [P, NP], F32), ("vn", [P, 4, P], F32), ("kn_n", [P, 4, P], F32), ("tot", [P, NP], F32))
        (ss,), e5 = group(lat, ("ss", [P, 2, NS, P], F32))
        (kvo, st), e6 = group(e5, ("kvo", [P, 4, P], F32), ("st", [P, 4, P], F32))
        (z, zr, nat), e7 = group(ar, ("z", [P, QK, NT], F32), ("zr", [P, NT], F32), ("nat", [P, 2, KV + ROPE], F32))
        (qz, qc_hi, qc_lo, qn, qrz, qr, kn, vh, ukt), e8 = group(
            ar, ("qz", [P, QK, NT], F32), ("qc_hi", [P, QK, NT], F32R), ("qc_lo", [P, QK, NT], F32R),
            ("qn", [P, 2, NT], F32), ("qrz", [P, NT], F32), ("qr", [P, 2, NT], F32), ("kn", [P, 2, NP], F32),
            ("vh", [P, 4, 2 * P], F32), ("ukt", [P, 2, RK, P], F32))
        (pp, ppt, mx, nb, rsum, rinv, tn_m), e9 = group(
            scr, ("pp", [P, 2, NP], F32), ("ppt", [P, 2, NP], F32), ("mx", [P, 32], F32), ("nb", [P, 32], F32),
            ("rsum", [P, 32], F32), ("rinv", [P, 32], F32), ("tn_m", [P, NT], F32))
        (pg, pgk, ct0, ol, ol_hi, ol_lo, ols), e10 = group(
            ar, ("pg", [P, 2, NPG, KV], F32), ("pgk", [P, 2, NPG, ROPE], F32), ("ct0", [P, 3, 512], F32),
            ("ol", [H, KV], F32), ("ol_hi", [P, RK, NS, H], F32R), ("ol_lo", [P, RK, NS, H], F32R),
            ("ols", [P, RK, NS, H], F32))
        (srow, ct1, pts, smx), e11 = group(
            scr, ("srow", [H, PAST + NS], F32), ("ct1", [P, 3, 512], F32), ("pts", [P, NPG + 1, H], F32),
            ("smx", [H, 4], F32))
        cts = [ct0, ct1]
        (yt, ynat, yns), e12 = group(ar, ("yt", [P, KD, NT], F32), ("ynat", [P, 2, D], F32), ("yns", [NS, D], F32))
        assert max(e0, e1, e3, e7, e8, e10, e12) <= end, (ar, end, e0, e1, e3, e7, e8, e10, e12)
        assert max(e2, e4, e9, e11) <= ar and e6 <= scr, (ar, scr, e2, e4, e9, e11, e6)

        ps = ctx.enter_context(nc.psum_tensor("ps", [P, 8, 512], F32))
        pair = [ps[:, 2 * b:2 * b + 2, 0:HT] for b in range(3)]

        def two(ap):
            return ap.rearrange("p (h n) -> p h n", h=2)

        s_in = sem("inputs_landed")
        s_xin = sem("x_landed")
        s_tab = sem("rotary_tables_landed")
        s_pt = sem("page_table_landed")
        landed = [sem(f"weights_landed{r}") for r in range(RAW)]
        hi_done = sem("hi_half_written")
        split_done = sem("lo_half_written")
        slot_used = sem("slot_multiplied")
        start_t = sem("start_transposed")
        start_c = sem("start_copied")
        sc_done = sem("silu_c_split")
        low_ready = sem("bound_logits_ready")
        low_done = sem("bounds_made")
        x_t = sem("x_transposed")
        x_placed = sem("x_placed")
        rows_copied = sem("ada_rows_copied")
        comb_done = sem("ada_rows_combined")
        mods_added = sem("mods_added")
        chain = sem("vector_step")
        sq_done = sem("squares_made")
        stats_done = sem("squares_summed")
        root_done = sem("root_taken")
        tn_done = sem("normed_chunk")
        aff_done = sem("modulated_chunk")
        hn_done = sem("hn_chunk_split")
        gate_done = sem("gate_chunk_multiplied")
        gate_read = sem("gate_chunk_read")
        up_read = sem("up_chunk_read")
        hid_done = sem("hidden_chunk_split")
        res_done = sem("residual_chunk_multiplied")
        x_upd = sem("x_chunk_updated")
        proj_mid = sem("first_chunk_of_slot_multiplied")
        act_part = sem("sigmoids_taken")
        q_read = sem("q_chunk_read")
        f_read = sem("f_chunk_read")
        i_read = sem("i_chunk_read")
        g_read = sem("g_chunk_read")
        fk_done = sem("forget_and_key_made")
        att_done = [sem(f"att_bank_multiplied{j}") for j in range(2)]
        att_read = [sem(f"att_bank_read{j}") for j in range(2)]
        level_ready = sem("level_operands_ready")
        st_done = sem("states_made")
        st_out = sem("prompt_state_stored")
        st_free = sem("prompt_state_buffer_free")
        ss_in = [sem(f"sample_states_landed{j}") for j in range(2)]
        ss_done = sem("sample_states_updated")
        outs_read = sem("sample_outputs_read")
        ss_out = [sem(f"sample_states_stored{j}") for j in range(2)]
        z_read = sem("latent_chunk_read")
        z_done = sem("latent_chunk_multiplied")
        lat_done = sem("latent_normed")
        rope_done = sem("rope_applied")
        nat_t = sem("rows_transposed")
        nat_read = sem("rows_copied")
        nat_out = [sem(f"rows_stored{j}") for j in range(2)]
        small_out = sem("sample_rows_stored")
        q_done = sem("query_piece_multiplied")
        q_copied = sem("query_piece_copied")
        nb_done = sem("row_maxima_ready")
        p_done = sem("weights_normalised")
        pt_t = sem("weights_transposed")
        pt_copied = sem("weights_t_copied")
        o_done = sem("head_values_summed")
        o_read = sem("head_values_split")
        pages_in = [sem(f"pages_landed{j}") for j in range(2)]
        pages_used = sem("pages_multiplied")
        ct_t = sem("pages_transposed")
        ct_copied_a = sem("latent_pages_copied")
        ct_copied_d = sem("rope_pages_copied")
        sc_mul = sem("page_scores_multiplied")
        sc_copied = sem("page_scores_copied")
        smax_done = sem("sample_maxima_ready")
        exp_done = sem("sample_weights_ready")
        pts_t = sem("sample_weights_transposed")
        pts_copied = sem("sample_weights_t_copied")
        pv_done = sem("sample_values_summed")
        ol_done = sem("sample_values_scaled")
        olt_done = sem("sample_values_transposed")
        ols_done = sem("sample_values_placed")
        os_split = sem("sample_heads_split")
        qs_ready = sem("sequence_queries_ready")
        new_mul = sem("new_score_multiplied")
        olsplit = sem("sample_values_split")
        y_done = sem("y_chunk_made")
        y_t = sem("y_transposed")
        y_copied = sem("y_copied")
        y_out = [sem(f"y_stored{j}") for j in range(2)]

        ada_v = [a["w_ada"][l].rearrange("(k p) n -> p k n", p=P) for l in range(2)]
        kvada_v = a["kv_w_ada"].rearrange("(k p) n -> p k n", p=P)
        gu_v = {(l, j): a["w_ffn_gu"][l, j].rearrange("(k p) (g f) -> p k g f", p=P, g=2)
                for l in range(2) for j in range(2)}
        dn_v = {(l, j): a["w_ffn_down"][l, j].rearrange("(k p) n -> p k n", p=P) for l in range(2) for j in range(2)}
        hg_v = a["hg_w_in"][0].rearrange("(k p) (g f) -> p k g f", p=P, g=4)
        hgo_v = a["hg_w_out"][0].rearrange("(k p) n -> p k n", p=P)
        kvd_v = a["kv_w_down"].rearrange("(k p) n -> p k n", p=P)
        qd_v = a["q_w_down"][0].rearrange("(k p) n -> p k n", p=P)
        qu_v = a["q_w_up"][0].rearrange("(k p) h n -> p k h n", p=P)
        uk_v = a["kv_w_uk"].rearrange("(k p) h n -> p k (h n)", p=P)
        uv_v = a["kv_w_uv"].rearrange("(k p) h n -> p k (h n)", p=P)
        ao_v = a["attn_w_out"][0].rearrange("(k p) n -> p k n", p=P)
        st_in_v = a["state_hgrn"][0].rearrange("b h k v -> h k b v")
        st_s_v = st_sample[0].rearrange("b h k v -> h k b v")
        st_p_v = st_prompt[0, 0]

        block = ctx.enter_context(nc.Block())

        @block.sync
        def _(sp):
            T = Tally()

            def slot(loads):
                k = T.n.get("slot", 0)
                r = k % RAW
                if k >= RAW:
                    sp.wait_ge(split_done, T.at("slot", 2 - 2 * RAW, 2))
                for dst, src in loads(raw[:, r, :]):
                    sp.dma_start(dst, src).then_inc(landed[r], LAND // len(loads(raw[:, r, :])))
                T.add("slot")

            def columns(view, col, width, k0=0, kn=KD):
                h = (kn + 1) // 2

                def loads(w):
                    d = w[:, 0:kn * width].rearrange("p (k n) -> p k n", k=kn)
                    return [(d[:, 0:h, :], view[:, k0:k0 + h, bass.ds(col, width)]),
                            (d[:, h:kn, :], view[:, k0 + h:k0 + kn, bass.ds(col, width)])]
                return slot(loads)

            def gate_up(view, m):
                def loads(w):
                    d = w.rearrange("p (k g n) -> p k g n", k=KD, g=2)
                    return [(d[:, :, g, :], view[:, :, g, bass.ds(m * P, P)]) for g in range(2)]
                return slot(loads)

            def ada_run(view, first, n):
                for j in range(min(4, n)):
                    columns(view, (first + j) * ADA_W, ADA_W)
                full = max(0, n - 4) // 4
                if full:
                    with T.loop(sp, full, {"slot": 4}) as i:
                        for j in range(4):
                            columns(view, i * (4 * ADA_W) + (first + 4 + j) * ADA_W, ADA_W)
                for j in range(4 + 4 * full, n):
                    columns(view, (first + j) * ADA_W, ADA_W)

            def ffn(l, j, ada=None):
                for m0, mn, kn in ((0, MFA, MFA // 2), (MFA, MFB, MFB // 2)):
                    if ada is not None:
                        view, first = ada
                        with T.loop(sp, mn // 2, {"slot": 4}) as i:
                            for q in range(2):
                                gate_up(gu_v[l, j], i * 2 + (m0 + q))
                                columns(view, i * (2 * ADA_W) + (first + m0 + q) * ADA_W, ADA_W)
                    else:
                        with T.loop(sp, mn // 4, {"slot": 4}) as i:
                            for q in range(4):
                                gate_up(gu_v[l, j], i * 4 + (m0 + q))
                        for q in range(mn // 4 * 4, mn):
                            gate_up(gu_v[l, j], m0 + q)
                    with T.loop(sp, 2, {"slot": 4}) as i:
                        for q in range(2):
                            for s in range(2):
                                columns(dn_v[l, j], i * 512 + q * 256, 256, m0 + s * kn, kn)

            def hgrn_project(h):
                def loads(w, g0=0):
                    d = w.rearrange("p (k g n) -> p k g n", k=KD, g=2)
                    return [(d[:, :, g, :], hg_v[:, :, g0 + g, bass.ds(h * P, P)]) for g in range(2)]
                slot(loads)
                columns(kvada_v, h * ADA_W, ADA_W)
                slot(lambda w: loads(w, 2))
                columns(ada_v[1], h * ADA_W, ADA_W)

            ada_run(ada_v[0], 0, ADA_FIRST)
            ffn(0, 0, (ada_v[0], ADA_FIRST))
            hgrn_project(0)
            with T.loop(sp, 3, {"slot": 8}) as i:
                for q in range(2):
                    hgrn_project(i * 2 + (q + 1))
            hgrn_project(7)
            for j in range(ADA_TAIL):
                columns(ada_v[1], (H + j) * ADA_W, ADA_W)
            for m in range(4):
                columns(hgo_v, m * 256, 256)
            ffn(0, 1, (ada_v[1], H + ADA_TAIL))
            columns(kvd_v, 0, 256)
            slot(lambda w: [(w[:, 0:KD * P].rearrange("p (k n) -> p k n", k=KD)[:, :, s * ROPE:(s + 1) * ROPE],
                             kvd_v[:, :, KV:KV + ROPE]) for s in range(2)])
            ffn(1, 0)
            columns(qd_v, 0, 256)
            columns(qd_v, 256, 128)
            for hp in range(4):
                def loads(w, hp=hp):
                    d = w[:, 0:QK * 384].rearrange("p (k n) -> p k n", k=QK)
                    out = []
                    for s in range(2):
                        out.append((d[:, :, s * P:(s + 1) * P], qu_v[:, :, 2 * hp + s, 0:P]))
                        out.append((d[:, :, 256 + s * ROPE:256 + (s + 1) * ROPE], qu_v[:, :, 2 * hp + s, P:P + ROPE]))
                    return out
                slot(loads)
                columns(uk_v, hp * 256, 256, 0, RK)
                columns(uv_v, hp * 256, 256, 0, RK)
            columns(uv_v, 0, D, 0, RK)
            columns(ao_v, 0, 256)
            columns(ao_v, 256, 256)
            sp.wait_ge(s_pt, 16)
            sp.wait_ge(o_read, H)
            ckv_pages = a["cache_ckv"].rearrange("n p r -> p n r")
            kr_pages = a["cache_krope"].rearrange("n p r -> p n r")
            top = a["cache_ckv"].shape[0] - 1
            with T.loop(sp, NS // 2, {"seq": 2}) as i:
                for q in range(2):
                    sp.wait_ge(pages_used, T.at("seq", 1))
                    for p in range(NPG):
                        v = sp.value_load(pt_sb[0:1, bass.ds(i * (2 * NPG) + (q * NPG + p), 1)], min_val=0, max_val=top)
                        sp.dma_start(pg[:, q, p, :], ckv_pages[:, bass.ds(v, 1), :].rearrange("p a r -> p (a r)")
                                     ).then_inc(pages_in[q], 16)
                        sp.dma_start(pgk[:, q, p, :], kr_pages[:, bass.ds(v, 1), :].rearrange("p a r -> p (a r)")
                                     ).then_inc(pages_in[q], 16)
                    T.add("seq")
            columns(ao_v, 512, 256)
            columns(ao_v, 768, 256)
            ffn(1, 1)

        @block.gpsimd
        def _(pool):
            T = Tally()
            pool.sem_inc(pages_used, 2)
            pool.sem_inc(st_free, 1)
            pool.dma_start(cst[:], a["consts"]).then_inc(s_in, 16)
            pool.dma_start(cr[0:1, :], a["c_prompt"]).then_inc(s_in, 16)
            pool.dma_start(cr[1:SEQS, :], a["c_sample"]).then_inc(s_in, 16)
            rows_of = lambda v: v.rearrange("(c p) -> c p", p=P)
            pool.dma_start(brow0[0:72, :], rows_of(a["b_ada"][0])).then_inc(s_in, 16)
            pool.dma_start(brow0[72:88, :], rows_of(a["kv_b_ada"])).then_inc(s_in, 16)
            pool.dma_start(brow1[:], rows_of(a["b_ada"][1])).then_inc(s_in, 16)
            pool.dma_start(vrow[V_NORM:V_FINAL, :], a["g_norm"].rearrange("l j (c p) -> (l j c) p", p=P)).then_inc(s_in, 16)
            pool.dma_start(vrow[V_FINAL:V_KVN, :], rows_of(a["g_final"])).then_inc(s_in, 16)
            pool.dma_start(vrow[V_KVN:V_LAT, :], rows_of(a["kv_g_norm"])).then_inc(s_in, 16)
            pool.dma_start(vrow[V_LAT:V_Q, :], rows_of(a["kv_g_latent"])).then_inc(s_in, 16)
            pool.dma_start(vrow[V_Q:V_HG, :], rows_of(a["q_g_norm"][0])).then_inc(s_in, 16)
            pool.dma_start(vrow[V_HG:V_LB, :], rows_of(a["hg_g_out"][0])).then_inc(s_in, 16)
            pool.dma_start(vrow[V_LB:NVEC, :], a["hg_lb"].rearrange("l (c p) -> (l c) p", p=P)).then_inc(s_in, 16)
            for t in range(4):
                pool.dma_start(xr[:, t, :], a["x_prompt"][0, t * P:(t + 1) * P, :]).then_inc(s_xin, 16)
            pool.dma_start(xs[:], a["x_sample"].rearrange("b s d -> (b s) d")).then_inc(s_xin, 16)
            pool.dma_start(lmask[:], a["level_masks"]).then_inc(s_tab, 16)
            pool.dma_start(pt_sb[:], a["page_table"].rearrange("b n -> (b n)").rearrange("(a n) -> a n", a=1)
                           ).then_inc(s_pt, 16)

            def head_in(h, q):
                pool.dma_start(ss[:, q, :, :], st_in_v[bass.ds(h, 1)].rearrange("a k b v -> k (a b) v")
                               ).then_inc(ss_in[q], 16)

            def head_out(h, q):
                pool.wait_ge(st_done, T.at("head", 1))
                pool.nop(nofuse=True)
                pool.dma_start(st_p_v[bass.ds(h, 1)].rearrange("a k v -> (a k) v"), st[:, 3, :]).then_inc(st_out, 16)
                pool.wait_ge(ss_done, T.at("head", 3, 2))
                pool.nop(nofuse=True)
                pool.dma_start(st_s_v[bass.ds(h, 1)].rearrange("a k b v -> k (a b) v"), ss[:, q, :, :]
                               ).then_inc(ss_out[q], 16)
                pool.wait_ge(st_out, T.at("head", 16, 16))
                pool.sem_inc(st_free, 1)
                pool.wait_ge(ss_out[q], T.at(f"head{q}", 16, 16))
                pool.wait_ge(outs_read, T.at("head", 1))
                pool.nop(nofuse=True)
                T.add("head")
                T.add(f"head{q}")

            head_in(0, 0)
            head_in(1, 1)
            with T.loop(pool, 3, {"head": 2, "head0": 1, "head1": 1}) as i:
                for q in range(2):
                    head_out(i * 2 + q, q)
                    head_in(i * 2 + (q + 2), q)
            head_out(6, 0)
            head_out(7, 1)
            pool.dma_start(cossin[:], a["rotary"]).then_inc(s_tab, 16)
            for t in range(4):
                pool.wait_ge(nat_read, t + 1)
                pool.dma_start(ckv_prompt[0, t * P:(t + 1) * P, :], nat[:, t % 2, 0:KV]).then_inc(nat_out[t % 2], 16)
                pool.dma_start(kr_prompt[0, t * P:(t + 1) * P, :], nat[:, t % 2, KV:]).then_inc(nat_out[t % 2], 16)
            pool.wait_ge(nat_read, 5)
            pool.dma_start(ckv_sample.rearrange("b s r -> (b s) r"), ckn[:, 0:KV]).then_inc(small_out, 16)
            pool.dma_start(kr_sample.rearrange("b s r -> (b s) r"), ckn[:, KV:]).then_inc(small_out, 16)
            for t in range(4):
                pool.wait_ge(y_copied, 2 * t + 2)
                pool.dma_start(y_prompt[0, t * P:(t + 1) * P, :], ynat[:, t % 2, :]).then_inc(y_out[t % 2], 16)
            pool.wait_ge(y_copied, 10)
            pool.dma_start(y_sample.rearrange("b s d -> (b s) d"), yns[:]).then_inc(small_out, 16)
            pool.wait_ge(st_out, 16 * H)
            pool.wait_ge(small_out, 48)
            for j in range(2):
                pool.wait_ge(ss_out[j], 16 * 4)
                pool.wait_ge(nat_out[j], 64)
                pool.wait_ge(y_out[j], 32)

        @block.tensor
        def _(pe):
            T = Tally()

            def halves(n=2):
                pe.wait_ge(split_done, T.at("slot", n, 2))

            def slabs(kn, width):
                b = T.n.get("slot", 0) % 2
                return (w_hi[:, b, 0:kn * width].rearrange("p (k n) -> p k n", k=kn),
                        w_lo[:, b, 0:kn * width].rearrange("p (k n) -> p k n", k=kn))

            def tile(out, wh, wl, xh, xl, start, stop):
                for t in range(2):
                    c = slice(t * HT, (t + 1) * HT)
                    pe.matmul(out[:, t, :], wh, xh[:, c], start=start, stop=False)
                    pe.matmul(out[:, t, :], wh, xl[:, c], start=False, stop=False)
                    mm = pe.matmul(out[:, t, :], wl, xh[:, c], start=False, stop=stop)
                return mm

            def chunk(out, hi, lo, col, xh, xl, kn, fresh=False, two_halves=False):
                for k in range(kn):
                    if fresh:
                        pe.wait_ge(hn_done, T.at("hn", k + 1))
                    if two_halves and k == 4:
                        halves(2)
                    mm = tile(out, hi[:, k, col:col + P], lo[:, k, col:col + P], xh[:, k, :], xl[:, k, :],
                              k == 0, k == kn - 1)
                return mm

            def ada():
                hi, lo = slabs(KD, ADA_W)
                if T.n.get("ada", 0) or T.i is not None:
                    pe.wait_ge(rows_copied, T.at("ada"))
                for half in range(2):
                    halves(1 + half)
                    for k in range(4 * half, 4 * half + 4):
                        pe.matmul(ps[0:18, 6, 0:ADA_W], sc18[:, k, :], hi[:, k, :], start=(k == 0), stop=False)
                        mm = pe.matmul(ps[0:18, 6, 0:ADA_W], sc18[:, k, :], lo[:, k, :], start=False, stop=(k == 7))
                mm.then_inc(slot_used, 1)
                T.add("slot")
                T.add("ada")

            def ada_comb():
                pe.wait_ge(rows_copied, T.at("ada"))
                if T.n.get("comb", 0) or T.i is not None:
                    pe.wait_ge(mods_added, T.at("comb"))
                for j in range(2):
                    mm = pe.matmul(ps[:, 7, j * SEQS:(j + 1) * SEQS], rows[:, j * P:(j + 1) * P], comb,
                                   start=True, stop=True)
                mm.then_inc(comb_done, 1)
                T.add("comb")

            def ada_run(n):
                for j in range(min(4, n)):
                    ada()
                    ada_comb()
                full = max(0, n - 4) // 4
                if full:
                    with T.loop(pe, full, {"slot": 4, "ada": 4, "comb": 4}):
                        for j in range(4):
                            ada()
                            ada_comb()
                for j in range(4 + 4 * full, n):
                    ada()
                    ada_comb()

            def sum_squares(n, out=2):
                for c in range(n):
                    pe.wait_ge(sq_done, T.at("sq", c + 1))
                    for t in range(2):
                        mm = pe.matmul(pair[out][:, t, :], ones[:], sq[:, c % 2, t * HT:(t + 1) * HT],
                                       start=(c == 0), stop=(c == n - 1))
                    mm.then_inc(stats_done, 1)
                T.add("sq", n)
                T.add("root")

            def hidden(fresh=False, combine=False):
                hi, lo = slabs(KD, 2 * P)
                halves(1)
                pe.wait_ge(gate_read, T.at("up", 1))
                chunk(pair[0], hi, lo, 0, hn_hi, hn_lo, KD, fresh, True).then_inc(gate_done, 1)
                if combine:
                    ada_comb()
                pe.wait_ge(up_read, T.at("up", 1))
                chunk(pair[1], hi, lo, P, hn_hi, hn_lo, KD).then_inc(slot_used, 1)
                if fresh:
                    T.add("hn", KD)
                T.add("up")
                T.add("slot")

            def down(kn):
                with T.loop(pe, 2, {"slot": 4, "res": 4}):
                    for q in range(2):
                        for s in range(2):
                            hi, lo = slabs(kn, 256)
                            halves()
                            for m in range(2):
                                if s == 0:
                                    pe.wait_ge(x_upd, T.at("res", m + 1))
                                for k in range(kn):
                                    c = slice(m * P, (m + 1) * P)
                                    mm = tile(pair[m], hi[:, k, c], lo[:, k, c], hid_hi[:, s * kn + k, :],
                                              hid_lo[:, s * kn + k, :], s == 0 and k == 0, s == 1 and k == kn - 1)
                                if s == 1 and m == 0:
                                    mm.then_inc(res_done, 1)
                            mm.then_inc(slot_used, 1)
                            T.add("slot")
                        T.add("res", 2)

            def ffn(with_ada):
                for half, mn in ((0, MFA), (1, MFB)):
                    pe.wait_ge(x_upd, T.at("res", 2))
                    by_hand = 2 if with_ada else mn % 4 or 4
                    for m in range(by_hand):
                        hidden(half == 0 and m == 0, with_ada and (half or m))
                        if with_ada:
                            ada()
                    if with_ada:
                        with T.loop(pe, (mn - 2) // 2, {"slot": 4, "up": 2, "ada": 2, "comb": 2}):
                            for q in range(2):
                                hidden(False, True)
                                ada()
                    else:
                        with T.loop(pe, (mn - by_hand) // 4, {"slot": 4, "up": 4}):
                            for q in range(4):
                                hidden()
                    T.add("hid", mn)
                    pe.wait_ge(hid_done, T.at("hid"))
                    down(mn // 2)
                if with_ada:
                    ada_comb()

            def out_projection(fresh):
                for s in range(4):
                    hi, lo = slabs(KD, 256)
                    halves(1)
                    for m in range(2):
                        pe.wait_ge(x_upd, T.at("res", m + 1))
                        mm = chunk(pair[m], hi, lo, m * P, hn_hi, hn_lo, KD, fresh and s == 0 and m == 0, m == 0)
                        mm.then_inc(slot_used if m else res_done, 1)
                        if fresh and s == 0 and m == 0:
                            T.add("hn", KD)
                    T.add("slot")
                    T.add("res", 2)

            def hgrn_step(events, q, first):
                def att():
                    b = T.n.get("att", 0) % 2
                    pe.wait_ge(att_read[b], T.at(f"att{b}", 1))
                    T.add("att")
                    T.add(f"att{b}")
                    return ps[:, 4 + b, :], att_done[b]

                for kind, j, n in events:
                    if kind == "tiles":
                        for idx in range(j, j + n):
                            c, k = divmod(idx, KD)
                            hi, lo = slabs(KD, 2 * P)
                            if k == 0:
                                if c == 0:
                                    halves(1)
                                    if not first:
                                        pe.wait_ge(i_read, T.at("proj"))
                                elif c == 1:
                                    if not first:
                                        pe.wait_ge(g_read, T.at("proj"))
                                elif c == 2:
                                    halves(1)
                                    pe.wait_ge(q_read, T.at("proj", 1))
                                else:
                                    pe.wait_ge(f_read, T.at("proj", 1))
                            if k == 4 and c % 2 == 0:
                                halves(2)
                            if first and c == 0:
                                pe.wait_ge(hn_done, T.at("hn", k + 1))
                            col = (c % 2) * P
                            mm = tile(pair[c % 2], hi[:, k, col:col + P], lo[:, k, col:col + P], hn_hi[:, k, :],
                                      hn_lo[:, k, :], k == 0, k == 7)
                            if k == 7:
                                mm.then_inc(slot_used if c % 2 else proj_mid, 1)
                                if c % 2:
                                    T.add("slot")
                                if c == 3:
                                    T.add("proj")
                                if first and c == 0:
                                    T.add("hn", KD)
                    elif kind == "ada":
                        ada()
                    elif kind == "comb":
                        ada_comb()
                    elif kind == "vt":
                        out, done = att()
                        pe.wait_ge(i_read, T.at("head", 1))
                        pe.wait_ge(fk_done, T.at("head", 1))
                        pe.wait_ge(q_read, T.at("head", 1))
                        for c in range(4):
                            mm = pe.transpose(out[:, c * P:(c + 1) * P], vv[:, q, c * P:(c + 1) * P], ident)
                        mm.then_inc(done, 1)
                    elif kind == "level":
                        if j:
                            pe.wait_ge(level_ready, T.at("level", j))
                        out, done = att()
                        for c in range(4):
                            s = slice(c * P, (c + 1) * P)
                            mm = pe.matmul(out[:, s], kk[:, q, s], qs[:, q, s], start=True, stop=True)
                        mm.then_inc(done, 1)
                    elif kind == "outer":
                        out, done = att()
                        for b in range(4):
                            v = vv[:, q, NP + 4 * j + b:NP + 4 * j + b + 1].broadcast_to([P, P])
                            mm = pe.matmul(out[:, b * P:(b + 1) * P], v, ident, start=True, stop=True)
                        mm.then_inc(done, 1)
                    elif kind == "kt":
                        pe.wait_ge(level_ready, T.at("level", 8))
                        T.add("level", 8)
                        out, done = att()
                        for c in range(4):
                            mm = pe.transpose(out[:, c * P:(c + 1) * P], kk[:, q, c * P:(c + 1) * P], ident)
                        mm.then_inc(done, 1)
                    elif kind == "state":
                        out, done = att()
                        other = T.n["att"] % 2
                        pe.wait_ge(att_read[other], T.at(f"att{other}", 1))
                        for c in range(4):
                            mm = pe.matmul(out[:, c * P:(c + 1) * P], kn_n[:, c, :], vn[:, c, :], start=True, stop=True)
                        mm.then_inc(done, 1)
                    elif kind == "out":
                        out, done = att()
                        for c in range(4):
                            s = slice(c * P, (c + 1) * P)
                            if c == 1:
                                pe.wait_ge(st_done, T.at("head", 1))
                            mm = pe.matmul(out[:, s], vn[:, c, :], attn[:, s], start=True, stop=(c == 0))
                            if c:
                                mm = pe.matmul(out[:, s], st[:, c - 1, :], qs[:, q, s], start=False, stop=True)
                        mm.then_inc(done, 1)
                    elif kind == "outs":
                        out, done = att()
                        pe.wait_ge(ss_done, T.at("head", 3, 2))
                        for b in range(NS):
                            mm = pe.matmul(out[:, b:b + 1], ss[:, q, b, :], qs[:, q, NP + b:NP + b + 1],
                                           start=True, stop=True)
                        mm.then_inc(done, 1)
                        T.add("head")

            def hgrn_norm():
                for h in range(H):
                    pe.wait_ge(sq_done, T.at("sq", h + 1))
                    if h >= 2:
                        pe.wait_ge(root_done, T.at("root", h - 1))
                    for t in range(2):
                        mm = pe.matmul(pair[h % 2][:, t, :], ones[:], sq[:, h % 2, t * HT:(t + 1) * HT],
                                       start=True, stop=True)
                    mm.then_inc(stats_done, 1)
                    if h < ADA_TAIL:
                        ada()
                        ada_comb()
                T.add("sq", H)
                T.add("root", H)
                pe.wait_ge(root_done, T.at("root"))

            pe.wait_ge(s_in, 16 * 13)
            for c in range(KD):
                pe.transpose(ps[:, 4, c * SEQS:(c + 1) * SEQS], cr[:, c * P:(c + 1) * P], ident[0:SEQS, 0:SEQS])
            pe.transpose(ps[:, 5, 0:NVEC], vrow[:], ident[0:NVEC, 0:NVEC])
            pe.transpose(ps[:, 5, 128:128 + C_L1], brow0[:], ident[0:C_L1, 0:C_L1])
            pe.transpose(ps[:, 5, 256:256 + NMOD - C_L1], brow1[:], ident[0:NMOD - C_L1, 0:NMOD - C_L1]
                         ).then_inc(start_t, 1)
            pe.wait_ge(s_xin, 16 * 5)
            for c in range(KD):
                if c >= 4:
                    pe.wait_ge(x_placed, c - 3)
                for t in range(4):
                    mm = pe.transpose(ps[:, c % 4, t * P:(t + 1) * P], xr[:, t, c * P:(c + 1) * P], ident)
                mm.then_inc(x_t, 1)
            for c in range(KD):
                mm = pe.transpose(ps[:, 7, c * NS:(c + 1) * NS], xs[:, c * P:(c + 1) * P], ident[0:NS, 0:NS])
            mm.then_inc(x_t, 1)
            pe.wait_ge(x_placed, KD + 1)
            pe.wait_ge(sc_done, 1)
            ada_run(ADA_FIRST)
            sum_squares(KD)
            ffn(True)
            sum_squares(KD)
            hgrn_step(project_events(), 1, True)
            per = {"slot": 8, "ada": 4, "comb": 4, "proj": 2, "att": 30, "att0": 15, "att1": 15, "level": 16, "head": 2}
            with T.loop(pe, 3, per):
                for q in range(2):
                    hgrn_step(hgrn_events(True), q, False)
            hgrn_step(hgrn_events(True), 0, False)
            hgrn_step(hgrn_events(False), 1, False)
            hgrn_norm()
            out_projection(True)
            sum_squares(KD)
            ffn(True)

            sum_squares(KD)
            hi, lo = slabs(KD, 256)
            halves(1)
            for m in range(2):
                chunk(pair[m], hi, lo, m * P, hn_hi, hn_lo, KD, m == 0, m == 0).then_inc(slot_used if m else z_done, 1)
            T.add("hn", KD)
            T.add("slot")
            hi, lo = slabs(KD, P)
            halves()
            pe.wait_ge(z_read, 1)
            chunk(pair[0], hi, lo, 0, hn_hi, hn_lo, KD).then_inc(slot_used, 1)
            T.add("slot")
            pe.wait_ge(z_read, 2)
            sum_squares(RK, 1)
            pe.wait_ge(z_read, 3)
            for t in range(2):
                mm = pe.matmul(pair[0][:, t, :], rot, zr[:, t * HT:(t + 1) * HT], start=True, stop=True)
            mm.then_inc(z_done, 1)
            pe.wait_ge(lat_done, 1)
            pe.wait_ge(rope_done, 1)
            for t in range(5):
                b = 6 + t % 2
                if t >= 2:
                    pe.wait_ge(nat_read, t - 1)
                s, n = (slice(t * P, (t + 1) * P), P) if t < 4 else (slice(NP, NT), NS)
                for r in range(RK):
                    pe.transpose(ps[0:n, b, r * P:(r + 1) * P], z[:, r, s], ident)
                pe.transpose(ps[0:n, b, KV:KV + ROPE], kr2[0:ROPE, s], ident[0:ROPE, 0:ROPE]).then_inc(nat_t, 1)

            sum_squares(KD)
            ffn(False)

            sum_squares(KD)
            for s, n in ((0, 2), (1, 1)):
                hi, lo = slabs(KD, 256 if s == 0 else P)
                halves(1 if s == 0 else 2)
                for m in range(n):
                    if s:
                        pe.wait_ge(z_read, 4)
                    mm = chunk(pair[m], hi, lo, m * P, hn_hi, hn_lo, KD, s == 0 and m == 0, s == 0 and m == 0)
                    mm.then_inc(slot_used if m == n - 1 else z_done, 1)
                    if s == 0 and m == 0:
                        T.add("hn", KD)
                T.add("slot")
            pe.wait_ge(z_read, 5)
            sum_squares(QK, 1)
            pe.wait_ge(lat_done, 2)
            for hp in range(4):
                hi, lo = slabs(QK, 384)
                halves()
                if hp:
                    pe.wait_ge(o_read, 2 * hp - 1)
                chunk(pair[0], hi, lo, 0, qc_hi, qc_lo, QK).then_inc(q_done, 1)
                if hp:
                    pe.wait_ge(o_read, 2 * hp)
                chunk(pair[1], hi, lo, P, qc_hi, qc_lo, QK).then_inc(q_done, 1)
                pe.wait_ge(q_copied, 6 * hp + 1)
                chunk(pair[0], hi, lo, 2 * P, qc_hi, qc_lo, QK).then_inc(slot_used, 1)
                T.add("slot")
                pe.wait_ge(q_copied, 6 * hp + 3)
                for t in range(2):
                    mm = pe.matmul(pair[1][:, t, :], rot, qrz[:, t * HT:(t + 1) * HT], start=True, stop=True)
                mm.then_inc(q_done, 1)
                hi, lo = slabs(RK, 256)
                halves()
                for s in range(2):
                    for r in range(RK):
                        wh, wl = hi[:, r, s * P:(s + 1) * P], lo[:, r, s * P:(s + 1) * P]
                        pe.matmul(ps[:, s, :], wh, ck_hi[:, r, 0:NP], start=(r == 0), stop=False)
                        pe.matmul(ps[:, s, :], wh, ck_lo[:, r, 0:NP], start=False, stop=False)
                        mm = pe.matmul(ps[:, s, :], wl, ck_hi[:, r, 0:NP], start=False, stop=(r == 1))
                mm.then_inc(q_done, 1)
                b = T.n.get("att", 0) % 2
                pe.wait_ge(att_read[b], T.at(f"att{b}", 1))
                for s in range(2):
                    for r in range(RK):
                        o = ps[:, 4 + b, (2 * s + r) * P:(2 * s + r + 1) * P]
                        pe.matmul(o, hi[:, r, s * P:(s + 1) * P], ident_r[:], start=True, stop=False)
                        mm = pe.matmul(o, lo[:, r, s * P:(s + 1) * P], ident_r[:], start=False, stop=True)
                mm.then_inc(att_done[b], 1)
                T.add("att")
                T.add(f"att{b}")
                b = T.n["att"] % 2
                pe.wait_ge(att_read[b], T.at(f"att{b}", 1))
                pe.wait_ge(q_copied, 6 * hp + 5)
                pe.wait_ge(rope_done, hp + 2)
                for s in range(2):
                    for r in range(RK):
                        mm = pe.matmul(ps[:, 4 + b, (2 * s + r) * NS:(2 * s + r + 1) * NS], ukt[:, s, r, :],
                                       qn[:, s, NP:NT], start=True, stop=True)
                mm.then_inc(slot_used, 1)
                T.add("slot")
                pe.matmul(ps[0:ROPE, 4 + b, 4 * NS:5 * NS], ident[:, ROPE:P], qr[:, 1, NP:NT], start=True, stop=True
                          ).then_inc(att_done[b], 1)
                T.add("att")
                T.add(f"att{b}")
                hi, lo = slabs(RK, 256)
                halves()
                for c in range(4):
                    o = ps[:, 2 + c // 2, (c % 2) * 256:(c % 2) * 256 + 256]
                    for r in range(RK):
                        th, tl = ck_hi[:, r, c * P:(c + 1) * P], ck_lo[:, r, c * P:(c + 1) * P]
                        pe.matmul(o, th, hi[:, r, :], start=(r == 0), stop=False)
                        pe.matmul(o, tl, hi[:, r, :], start=False, stop=False)
                        mm = pe.matmul(o, th, lo[:, r, :], start=False, stop=(r == 1))
                mm.then_inc(slot_used, 1)
                T.add("slot")
                pe.wait_ge(q_copied, 6 * hp + 6)
                units = [(s, t) for s in range(2) for t in range(4)]
                for u in range(len(units) + 2):
                    if u < 8:
                        s, t = units[u]
                        n = (t + 1) * P
                        b = T.n["att"] % 2
                        pe.wait_ge(att_read[b], T.at(f"att{b}", 1))
                        pe.matmul(ps[:, 4 + b, 0:n], qn[:, s, t * P:(t + 1) * P], kn[:, s, 0:n], start=True, stop=False)
                        pe.matmul(ps[:, 4 + b, 0:n], qr[:, s, t * P:(t + 1) * P], kr2[:, 0:n], start=False, stop=True
                                  ).then_inc(att_done[b], 1)
                        T.add("att")
                        T.add(f"att{b}")
                    if 1 <= u <= 8:
                        s, t = units[u - 1]
                        w = 8 * hp + u - 1
                        pe.wait_ge(p_done, w + 1)
                        if w >= 2:
                            pe.wait_ge(pt_copied, w - 1)
                        for c in range(t + 1):
                            mm = pe.transpose(ps[:, 6 + w % 2, c * P:(c + 1) * P], pp[:, w % 2, c * P:(c + 1) * P], ident)
                        mm.then_inc(pt_t, 1)
                    if u >= 2:
                        s, t = units[u - 2]
                        w = 8 * hp + u - 2
                        pe.wait_ge(pt_copied, w + 1)
                        for c in range(t + 1):
                            mm = pe.matmul(ps[:, 2 * s, t * P:(t + 1) * P], vh[:, c, s * P:(s + 1) * P],
                                           ppt[:, w % 2, c * P:(c + 1) * P], start=(c == 0), stop=(c == t))
                        if t == 3:
                            mm.then_inc(o_done, 1)

            pe.wait_ge(o_read, H)
            per = {"seq": 2, "seq0": 1, "seq1": 1, "ct": 8}
            with T.loop(pe, NS // 2, per):
                for q in range(2):
                    def turn(g, q=q):
                        b = 4 * (g % 2)
                        pe.wait_ge(ct_copied_a, T.at("ct", g + 1))
                        pe.wait_ge(ct_copied_d, T.at("ct", g + 1))
                        for p in range(4):
                            for r in range(RK):
                                pe.transpose(ps[:, b + r, p * P:(p + 1) * P], pg[:, q, 4 * g + p, r * P:(r + 1) * P], ident)
                            mm = pe.transpose(ps[0:ROPE, b + 2, p * P:(p + 1) * P], pgk[:, q, 4 * g + p, :], ident)
                        mm.then_inc(ct_t, 1)

                    def scores(g, q=q):
                        pe.wait_ge(ct_copied_a, T.at("ct", g + 3))
                        pe.wait_ge(ct_copied_d, T.at("ct", g + 3))
                        if g >= 2:
                            pe.wait_ge(sc_copied, T.at("ct", g - 1))
                        o = ps[0:H, 3 + 4 * (g % 2), :]
                        for r in range(RK):
                            pe.matmul(o, qsamp[:, q, r, :], cts[g % 2][:, r, :], start=(r == 0), stop=False)
                        pe.matmul(o, qsamp[0:ROPE, q, 2, :], cts[g % 2][0:ROPE, 2, :], start=False, stop=True
                                  ).then_inc(sc_mul, 1)

                    pe.wait_ge(pages_in[q], T.at(f"seq{q}", 2 * NPG * 16, 2 * NPG * 16))
                    turn(0)
                    turn(1)
                    pe.wait_ge(qs_ready, T.at("seq", 1))
                    scores(0)
                    turn(2)
                    pe.wait_ge(ols_done, T.at("seq", 1))
                    scores(1)
                    turn(3)
                    scores(2)
                    scores(3)
                    T.add("ct", 4)
                    pe.wait_ge(sc_copied, T.at("ct", -1))
                    for r in range(RK):
                        pe.matmul(ps[0:H, 3, 0:NS], qsamp[:, q, r, :], cnew[:, r, :], start=(r == 0), stop=False)
                    pe.matmul(ps[0:H, 3, 0:NS], qsamp[0:ROPE, q, 2, :], kr2[0:ROPE, NP:NT], start=False, stop=True
                              ).then_inc(new_mul, 1)
                    pe.wait_ge(exp_done, T.at("seq", 1))
                    pe.wait_ge(sc_copied, T.at("ct"))
                    pe.nop(nofuse=True)
                    for p in range(NPG):
                        pe.transpose(ps[:, 7, p * H:(p + 1) * H], srow[:, p * P:(p + 1) * P], ident[0:H, 0:H])
                    pe.transpose(ps[0:NS, 7, NPG * H:(NPG + 1) * H], srow[:, PAST:PAST + NS], ident[0:H, 0:H]
                                 ).then_inc(pts_t, 1)
                    pe.wait_ge(pts_copied, T.at("seq", 1))
                    for p in range(NPG):
                        pe.matmul(ps[0:H, 3, 0:KV], pts[:, p, :], pg[:, q, p, :], start=(p == 0), stop=False)
                    pe.matmul(ps[0:H, 3, 0:KV], pts[0:NS, NPG, :], ckn[:, 0:KV], start=False, stop=True
                              ).then_inc(pages_used, 1)
                    pe.wait_ge(ol_done, T.at("seq", 1))
                    pe.nop(nofuse=True)
                    for r in range(RK):
                        mm = pe.transpose(ps[:, 7, r * H:(r + 1) * H], ol[:, r * P:(r + 1) * P], ident[0:H, 0:H])
                    mm.then_inc(olt_done, 1)
                    T.add("seq")
                    T.add(f"seq{q}")
            pe.wait_ge(olsplit, 1)
            halves()
            hi, lo = slabs(RK, D)
            for h in range(H):
                o = ps[:, 0, h * NS:(h + 1) * NS]
                for r in range(RK):
                    wh, wl = hi[:, r, h * P:(h + 1) * P], lo[:, r, h * P:(h + 1) * P]
                    pe.matmul(o, wh, ol_hi[:, r, :, h], start=(r == 0), stop=False)
                    pe.matmul(o, wh, ol_lo[:, r, :, h], start=False, stop=False)
                    mm = pe.matmul(o, wl, ol_hi[:, r, :, h], start=False, stop=(r == 1))
            mm.then_inc(slot_used, 1)
            T.add("slot")
            pe.wait_ge(os_split, 1)
            out_projection(False)
            sum_squares(KD)
            ffn(False)

            sum_squares(KD)
            pe.wait_ge(y_done, KD)
            for t in range(5):
                s, n = (slice(t * P, (t + 1) * P), P) if t < 4 else (slice(NP, NT), NS)
                for half in range(2):
                    w = 2 * t + half
                    if w >= 4:
                        pe.wait_ge(y_copied, w - 3)
                    for c in range(4):
                        mm = pe.transpose(ps[0:n, 4 + w % 4, c * P:(c + 1) * P], yt[:, 4 * half + c, s], ident)
                    mm.then_inc(y_t, 1)


        @block.scalar
        def _(act):
            T = Tally()

            def split_hi():
                k = T.n.get("split", 0)
                if k == SLOTS:
                    return
                r, b = k % RAW, k % 2
                turns = LAND * (k // RAW + 1)
                if T.i is not None:
                    turns = T.i * (LAND * T.per["split"] // RAW) + turns
                act.wait_ge(landed[r], turns)
                if k >= 2:
                    act.wait_ge(slot_used, T.at("split", -1))
                for half in range(2):
                    c = slice(half * SLOT // 2, (half + 1) * SLOT // 2)
                    act.activation(w_hi[:, b, c], raw[:, r, c], ACT.Copy).then_inc(hi_done, 1)
                T.add("split")

            def ada():
                split_hi()
                act.wait_ge(slot_used, T.at("slot", 1))
                if T.n.get("ada", 0):
                    act.wait_ge(comb_done, T.at("ada"))
                act.activation(rows[:], ps[0:2 * SEQS, 6, 0:ADA_W], ACT.Copy).then_inc(rows_copied, 1)
                T.add("slot")
                T.add("ada")

            def ada_run(n):
                for j in range(min(4, n)):
                    ada()
                full = max(0, n - 4) // 4
                if full:
                    with T.loop(act, full, {"slot": 4, "split": 4, "ada": 4}):
                        for j in range(4):
                            ada()
                for j in range(4 + 4 * full, n):
                    ada()

            def squares(n, source):
                for c in range(n):
                    src = source(c)
                    if T.n.get("sq", 0) + c >= 2:
                        act.wait_ge(stats_done, T.at("sq", c - 1))
                    act.activation(sq[:, c % 2, :], src, ACT.Square).then_inc(sq_done, 1)
                T.add("sq", n)

            def take_root(n, out=2):
                act.wait_ge(stats_done, T.at("sq"))
                act.activation(two(root[:]), pair[out], ACT.Sqrt, scale=1.0 / (n * P), bias=eps[:, 0:1]
                               ).then_inc(root_done, 1)

            def x_chunk(first):
                def source(c):
                    if first:
                        act.wait_ge(x_placed, KD + 1)
                    else:
                        act.wait_ge(x_upd, T.at("res", 3 + c - KD))
                    return x[:, c, :]
                return source

            def norm(base, first=False):
                squares(KD, x_chunk(first))
                take_root(KD)
                for c in range(KD):
                    act.wait_ge(tn_done, T.at("hn", c + 1))
                    if c >= 2:
                        act.wait_ge(hn_done, T.at("hnd", c - 1))
                    act.activation(tt[:, c % 2, 0:NP], tn[:, c % 2, 0:NP], ACT.Identity, scale=amod[:, c, 0:1],
                                   bias=mods[:, base + c, 0:1]).then_inc(aff_done, 1)
                T.add("hn", KD)
                T.add("hnd", KD)

            def hidden():
                split_hi()
                act.wait_ge(gate_done, T.at("up", 1))
                if T.n.get("up", 0) >= 2:
                    act.wait_ge(up_read, T.at("up"))
                act.activation(two(sg[:, T.n.get("up", 0) % 2, :]), pair[0], ACT.Silu).then_inc(gate_read, 1)
                T.add("up")
                T.add("slot")

            def down(last=False):
                if last:
                    for _ in range(8):
                        split_hi()
                    T.add("slot", 8)
                else:
                    with T.loop(act, 2, {"slot": 4, "split": 4}):
                        for _ in range(4):
                            split_hi()
                            T.add("slot")

            def ffn(with_ada, last=False):
                for half, mn in ((0, MFA), (1, MFB)):
                    by_hand = 2 if with_ada else mn % 4 or 4
                    for m in range(by_hand):
                        hidden()
                        if with_ada:
                            ada()
                    if with_ada:
                        with T.loop(act, (mn - 2) // 2, {"slot": 4, "split": 4, "up": 2, "ada": 2}):
                            for q in range(2):
                                hidden()
                                ada()
                    else:
                        with T.loop(act, (mn - by_hand) // 4, {"slot": 4, "split": 4, "up": 4}):
                            for q in range(4):
                                hidden()
                    down(last and half == 1)
                T.add("res", 2 * KD)

            def out_projection():
                for _ in range(4):
                    split_hi()
                    T.add("slot")
                T.add("res", KD)

            def hgrn_step(events, q, h):
                def att():
                    b = T.n.get("att", 0) % 2
                    T.add("att")
                    T.add(f"att{b}")
                    return ps[:, 4 + b, :], att_done[b], T.at(f"att{b}"), att_read[b]

                for kind, j, n in events:
                    if kind == "tiles":
                        if j % 16 == 0:
                            split_hi()
                        for c in range(4):
                            if not j < 8 * (c + 1) <= j + n:
                                continue
                            if c == 0:
                                act.wait_ge(proj_mid, T.at("proj", 1, 2))
                                act.activation(two(sgq[:]), pair[0], ACT.Sigmoid).then_inc(act_part, 1)
                            elif c == 1:
                                act.wait_ge(slot_used, T.at("slot", 1))
                                act.activation(two(s1[:]), pair[1], ACT.Sigmoid)
                                act.activation(two(s2[:]), pair[1], ACT.Sigmoid, scale=-1.0).then_inc(f_read, 1)
                                T.add("slot")
                            elif c == 2:
                                act.wait_ge(proj_mid, T.at("proj", 2, 2))
                                act.activation(two(vv[:, 1 - q, :]), pair[0], ACT.Copy).then_inc(i_read, 1)
                            else:
                                act.wait_ge(slot_used, T.at("slot", 1))
                                act.activation(two(sgg[:]), pair[1], ACT.Sigmoid).then_inc(act_part, 1)
                                T.add("slot")
                                T.add("proj")
                    elif kind == "ada":
                        ada()
                    elif kind == "vt":
                        src, done, count, read = att()
                        act.wait_ge(done, count)
                        act.activation(vn[:].rearrange("p c k -> p (c k)"), src, ACT.Copy).then_inc(read, 1)
                    elif kind == "kt":
                        src, done, count, read = att()
                        act.wait_ge(done, count)
                        act.activation(kn_n[:].rearrange("p c k -> p (c k)"), src, ACT.Copy).then_inc(read, 1)
                    elif kind == "outer":
                        src, done, count, read = att()
                        act.wait_ge(done, count)
                        act.wait_ge(ss_done, T.at("head", j + 1, 2))
                        for b in range(4):
                            t = NP + 4 * j + b
                            mm = act.activation(kvo[:, b, :], src[:, b * P:(b + 1) * P], ACT.Copy, scale=kk[:, q, t:t + 1])
                        mm.then_inc(read, 1)
                    elif kind == "out":
                        src, done, count, read = att()
                        act.wait_ge(done, count)
                        act.activation(og[:, bass.ds(h, 1), 0:NP], src.unsqueeze(1), ACT.Copy).then_inc(read, 1)
                    elif kind == "outs":
                        src, done, count, read = att()
                        act.wait_ge(done, count)
                        act.activation(og[:, bass.ds(h, 1), NP:NT], src[:, 0:NS].unsqueeze(1), ACT.Copy).then_inc(read, 1)
                        b0 = (T.n["att"] - 1) % 2
                        act.wait_ge(read, T.at(f"att{b0}", 1))
                        act.sem_inc(outs_read, 1)
                        T.add("head")
                    elif kind in ("level", "state"):
                        att()

            def hgrn_norm():
                act.wait_ge(att_read[0], T.at("att0", 1))
                act.wait_ge(att_read[1], T.at("att1", 1))
                for h in range(H + 1):
                    if h < H:
                        if T.n.get("sq", 0) >= 2:
                            act.wait_ge(stats_done, T.at("sq", -1))
                        act.activation(sq[:, h % 2, :], og[:, h, :], ACT.Square).then_inc(sq_done, 1)
                        T.add("sq")
                    if h < ADA_TAIL:
                        pass
                    if h >= 1:
                        g = h - 1
                        act.wait_ge(stats_done, T.at("sq", 0 if h == H else -1))
                        if g >= 2:
                            act.wait_ge(hn_done, T.at("hnd", g - 1))
                        act.activation(two(tt[:, g % 2, :]), pair[g % 2], ACT.Sqrt, scale=1.0 / P, bias=eps[:, 0:1]
                                       ).then_inc(root_done, 1)
                    if h < ADA_TAIL:
                        ada()
                T.add("hnd", H)

            act.sem_inc(gate_read, 1)
            act.sem_inc(ct_copied_a, 2)
            for j in range(2):
                act.sem_inc(att_read[j], 1)
            split_hi()
            act.wait_ge(start_t, 1)
            act.activation(scf[:].rearrange("p k s -> p (k s)"), ps[:, 4, 0:KD * SEQS], ACT.Silu).then_inc(start_c, 1)
            act.activation(vec[:], ps[:, 5, 0:NVEC], ACT.Copy).then_inc(start_c, 1)
            act.activation(bias[:, 0:C_L1], ps[:, 5, 128:128 + C_L1], ACT.Copy).then_inc(start_c, 1)
            act.activation(bias[:, C_L1:NMOD], ps[:, 5, 256:256 + NMOD - C_L1], ACT.Copy).then_inc(start_c, 1)
            act.wait_ge(low_ready, 1)
            act.activation(low[:, 1, :], low[:, 0, :], ACT.Sigmoid, scale=-1.0).then_inc(low_done, 1)
            act.wait_ge(low_done, 1)
            act.activation(low[:, 0, :], low[:, 0, :], ACT.Sigmoid).then_inc(low_done, 1)
            ada_run(ADA_FIRST)
            norm(C_L0, True)
            ffn(True)
            norm(C_L0 + 24)
            hgrn_step(project_events(), 1, 0)
            per = {"slot": 8, "split": 8, "ada": 4, "proj": 2, "att": 30, "att0": 15, "att1": 15, "head": 2}
            with T.loop(act, 3, per) as i:
                for q in range(2):
                    hgrn_step(hgrn_events(True), q, i * 2 + q)
            hgrn_step(hgrn_events(True), 0, 6)
            hgrn_step(hgrn_events(False), 1, 7)
            hgrn_norm()
            out_projection()
            norm(C_L0 + 48)
            ffn(True)

            norm(C_KV)
            split_hi()
            act.wait_ge(z_done, 1)
            act.activation(two(z[:, 0, :]), pair[0], ACT.Copy).then_inc(z_read, 1)
            act.wait_ge(slot_used, T.at("slot", 1))
            act.activation(two(z[:, 1, :]), pair[1], ACT.Copy).then_inc(z_read, 1)
            T.add("slot")
            split_hi()
            act.wait_ge(slot_used, T.at("slot", 1))
            act.activation(two(zr[:]), pair[0], ACT.Copy).then_inc(z_read, 1)
            T.add("slot")
            act.wait_ge(z_read, 2)
            squares(RK, lambda c: z[:, c, :])
            take_root(RK, 1)
            for t in range(5):
                act.wait_ge(nat_t, t + 1)
                if t in (2, 3):
                    act.wait_ge(nat_out[t % 2], 32)
                n = P if t < 4 else NS
                dst = nat[:, t % 2, :] if t < 4 else ckn[:]
                act.activation(dst, ps[0:n, 6 + t % 2, 0:KV + ROPE], ACT.Copy).then_inc(nat_read, 1)
            norm(C_L1)
            ffn(False)

            norm(C_L1 + 24)
            split_hi()
            act.wait_ge(z_done, 3)
            act.activation(two(qz[:, 0, :]), pair[0], ACT.Copy).then_inc(z_read, 1)
            act.wait_ge(slot_used, T.at("slot", 1))
            act.activation(two(qz[:, 1, :]), pair[1], ACT.Copy).then_inc(z_read, 1)
            T.add("slot")
            split_hi()
            act.wait_ge(slot_used, T.at("slot", 1))
            act.activation(two(qz[:, 2, :]), pair[0], ACT.Copy).then_inc(z_read, 1)
            T.add("slot")
            act.wait_ge(z_read, 6)
            squares(QK, lambda c: qz[:, c, :])
            take_root(QK, 1)

            def att():
                b = T.n.get("att", 0) % 2
                T.add("att")
                T.add(f"att{b}")
                return ps[:, 4 + b, :], att_done[b], T.at(f"att{b}"), att_read[b]

            for hp in range(4):
                split_hi()
                act.wait_ge(q_done, 4 * hp + 1)
                if hp:
                    act.wait_ge(o_done, 2 * hp)
                act.activation(two(qn[:, 0, :]), pair[0], ACT.Copy).then_inc(q_copied, 1)
                act.wait_ge(q_done, 4 * hp + 2)
                act.activation(two(qn[:, 1, :]), pair[1], ACT.Copy).then_inc(q_copied, 1)
                act.wait_ge(slot_used, T.at("slot", 1))
                if hp:
                    act.wait_ge(rope_done, hp + 1)
                act.activation(two(qrz[:]), pair[0], ACT.Copy).then_inc(q_copied, 1)
                T.add("slot")
                split_hi()
                act.wait_ge(q_done, 4 * hp + 4)
                act.activation(kn[:], ps[:, 0:2, :], ACT.Copy).then_inc(q_copied, 1)
                src, done, count, read = att()
                act.wait_ge(done, count)
                act.activation(ukt[:].rearrange("p s r k -> p (s r k)"), src, ACT.Copy).then_inc(q_copied, 1)
                act.wait_ge(q_copied, 6 * hp + 5)
                act.sem_inc(read, 1)
                att()
                T.add("slot")
                split_hi()
                act.wait_ge(slot_used, T.at("slot", 1))
                act.activation(vh[:].rearrange("p (a c) n -> p a (c n)", a=2), ps[:, 2:4, :], ACT.Copy).then_inc(q_copied, 1)
                T.add("slot")
                for u in range(9):
                    if u < 8:
                        w = 8 * hp + u
                        n = (u % 4 + 1) * P
                        src, done, count, read = att()
                        act.wait_ge(nb_done, w + 1)
                        act.activation(pp[:, w % 2, 0:n], src[:, 0:n], ACT.Exp, bias=nb[:, w:w + 1], scale=SM_SCALE,
                                       accum_out=rsum[:, w:w + 1]).then_inc(read, 1)
                    if u >= 1:
                        w = 8 * hp + u - 1
                        n = ((u - 1) % 4 + 1) * P
                        act.wait_ge(pt_t, w + 1)
                        act.activation(ppt[:, w % 2, 0:n], ps[:, 6 + w % 2, 0:n], ACT.Copy).then_inc(pt_copied, 1)

            split_hi()
            per = {"seq": 2, "ct": 8}
            with T.loop(act, NS // 2, per):
                for q in range(2):
                    def copy_pages(g):
                        b = 4 * (g % 2)
                        act.wait_ge(ct_t, T.at("ct", g + 1))
                        act.activation(cts[g % 2][:, 0:2, :], ps[:, b:b + 2, :], ACT.Copy).then_inc(ct_copied_a, 1)

                    def copy_scores(g):
                        act.wait_ge(sc_mul, T.at("ct", g + 1))
                        act.activation(srow[:, g * 512:(g + 1) * 512], ps[0:H, 3 + 4 * (g % 2), :], ACT.Copy
                                       ).then_inc(sc_copied, 1)

                    copy_pages(0)
                    copy_pages(1)
                    copy_scores(0)
                    copy_pages(2)
                    copy_scores(1)
                    copy_pages(3)
                    copy_scores(2)
                    copy_scores(3)
                    T.add("ct", 4)
                    act.wait_ge(smax_done, T.at("seq", 1))
                    act.activation(srow[:], srow[:], ACT.Exp, bias=smx[:, 1:2], scale=SM_SCALE, accum_out=smx[:, 2:3]
                                   ).then_inc(exp_done, 1)
                    act.wait_ge(pts_t, T.at("seq", 1))
                    act.activation(pts[:, 0:NPG, :].rearrange("p a h -> p (a h)"), ps[:, 7, 0:NPG * H], ACT.Copy)
                    act.activation(pts[0:NS, NPG, :], ps[0:NS, 7, NPG * H:(NPG + 1) * H], ACT.Copy).then_inc(pts_copied, 1)
                    T.add("seq")
            T.add("slot")
            out_projection()
            norm(C_L1 + 48)
            ffn(False, True)

            squares(KD, x_chunk(False))
            take_root(KD)
            for w in range(10):
                t, half = divmod(w, 2)
                act.wait_ge(y_t, w + 1)
                if t in (2, 3) and half == 0:
                    act.wait_ge(y_out[t % 2], 16)
                n = P if t < 4 else NS
                dst = ynat[:, t % 2, half * 512:(half + 1) * 512] if t < 4 else yns[:, half * 512:(half + 1) * 512]
                act.activation(dst, ps[0:n, 4 + w % 4, :], ACT.Copy).then_inc(y_copied, 1)

        @block.vector
        def _(dve):
            T = Tally()

            def link(ins):
                ins.then_inc(chain, 1)
                T.add("chain")
                dve.wait_ge(chain, T.at("chain"))

            def split_lo():
                k = T.n.get("split", 0)
                if k == SLOTS:
                    return
                r, b = k % RAW, k % 2
                for half in range(2):
                    c = slice(half * SLOT // 2, (half + 1) * SLOT // 2)
                    dve.wait_ge(hi_done, T.at("split", half + 1, 2))
                    dve.tensor_tensor(w_lo[:, b, c], raw[:, r, c], w_hi[:, b, c], ALU.subtract).then_inc(split_done, 1)
                T.add("split")

            def add_mods(col):
                dve.wait_ge(comb_done, T.at("comb", 1))
                dve.tensor_tensor(mods[:, bass.ds(col, 2), :], ps[:, 7, 0:2 * SEQS].rearrange("p (c s) -> p c s", c=2),
                                  bias[:, bass.ds(col, 2)].unsqueeze(2).broadcast_to([P, 2, SEQS]), ALU.add
                                  ).then_inc(mods_added, 1)
                T.add("comb")

            def ada(col):
                split_lo()
                T.add("slot")
                add_mods(col)

            def ada_run(first, n):
                for j in range(min(4, n)):
                    ada(2 * (first + j))
                full = max(0, n - 4) // 4
                if full:
                    with T.loop(dve, full, {"slot": 4, "split": 4, "comb": 4}) as i:
                        for j in range(4):
                            ada(i * 8 + 2 * (first + 4 + j))
                for j in range(4 + 4 * full, n):
                    ada(2 * (first + j))

            def split_act(src, hi, lo, done=None):
                link(dve.tensor_copy(hi, src))
                ins = dve.tensor_tensor(lo, src, hi, ALU.subtract)
                if done is not None:
                    ins.then_inc(done, 1)

            def norm(base, gain, gate_base, factor):
                dve.wait_ge(mods_added, T.at("comb"))
                dve.scalar_tensor_tensor(amod[:], mods[:, base + KD:base + 2 * KD, :], 1.0,
                                         vec[:, gain:gain + KD].unsqueeze(2).broadcast_to([P, KD, SEQS]), ALU.add, ALU.mult)
                if gate_base is not None:
                    if T.n.get("res", 0):
                        dve.wait_ge(x_upd, T.at("res", 2, 2))
                    dve.tensor_scalar(gate[:], mods[:, gate_base:gate_base + KD, :].rearrange("p c s -> p (c s)"),
                                      factor, None, ALU.mult)
                dve.wait_ge(root_done, T.at("root", 1))
                T.add("root")
                link(dve.reciprocal(rstd[:], root[:]))

                def finish(c):
                    b = c % 2
                    dve.wait_ge(tn_done, T.at("hn", c + 1))
                    link(dve.tensor_tensor(t9[:, 0, 0:NS], tn[:, b, NP:NT], amod[:, c, 1:SEQS], ALU.mult))
                    link(dve.tensor_tensor(tt[:, b, NP:NT], t9[:, 0, 0:NS], mods[:, base + c, 1:SEQS], ALU.add))
                    dve.wait_ge(aff_done, T.at("hn", c + 1))
                    split_act(tt[:, b, :], hn_hi[:, c, :], hn_lo[:, c, :], hn_done)

                for c in range(KD + 1):
                    if c < KD:
                        if c >= 2:
                            dve.wait_ge(aff_done, T.at("hn", c - 1))
                        dve.tensor_tensor(tn[:, c % 2, :], x[:, c, :], rstd[:], ALU.mult).then_inc(tn_done, 1)
                    if c:
                        finish(c - 1)
                T.add("hn", KD)

            def hidden(m, col=None):
                split_lo()
                if col is not None:
                    add_mods(col)
                dve.wait_ge(slot_used, T.at("slot", 1))
                dve.wait_ge(gate_read, T.at("up", 2))
                if T.n.get("up", 0):
                    dve.wait_ge(hid_done, T.at("up"))
                dve.tensor_tensor(two(hf[:]), pair[1], two(sg[:, T.n.get("up", 0) % 2, :]), ALU.mult).then_inc(up_read, 1)
                dve.wait_ge(up_read, T.at("up", 2))
                split_act(hf[:].unsqueeze(1), hid_hi[:, bass.ds(m, 1), :], hid_lo[:, bass.ds(m, 1), :], hid_done)
                T.add("up")
                T.add("slot")

            def residual(c, m):
                if m == 0:
                    dve.wait_ge(res_done, T.at("res", 1))
                else:
                    dve.wait_ge(slot_used, T.at("slot", 1))
                xc = x[:, bass.ds(c, 1), :]
                g0 = gate[:, bass.ds(c * SEQS, 1)]
                link(dve.tensor_tensor(t9[:, m, 0:NS], pair[m][:, 1, HT - NS:HT], gate[:, bass.ds(c * SEQS + 1, NS)],
                                       ALU.mult))
                for lo, hi, t in ((0, HT, 0), (HT, NP, 1)):
                    dve.scalar_tensor_tensor(xc[:, :, lo:hi], pair[m][:, t, 0:hi - lo].unsqueeze(1), g0,
                                             xc[:, :, lo:hi], ALU.mult, ALU.add)
                dve.tensor_tensor(xc[:, :, NP:NT], xc[:, :, NP:NT], t9[:, m, 0:NS].unsqueeze(1), ALU.add
                                  ).then_inc(x_upd, 1)

            def down(last=False):
                def body(i):
                    for q in range(2):
                        split_lo()
                        T.add("slot")
                        split_lo()
                        for m in range(2):
                            residual(i * 4 + (2 * q + m), m)
                        T.add("slot")
                        T.add("res")
                if last:
                    for i in range(2):
                        body(i)
                else:
                    with T.loop(dve, 2, {"slot": 4, "split": 4, "res": 2, "chain": 4}) as i:
                        body(i)

            def ffn(col=None, last=False):
                done = 0
                for half, mn in ((0, MFA), (1, MFB)):
                    by_hand = 2 if col is not None else mn % 4 or 4
                    for m in range(by_hand):
                        if col is not None:
                            pending = col + 2 * (done - 1) if done else None
                            hidden(m, pending)
                            split_lo()
                            T.add("slot")
                            done += 1
                        else:
                            hidden(m)
                    if col is not None:
                        with T.loop(dve, (mn - 2) // 2, {"slot": 4, "split": 4, "up": 2, "comb": 2, "chain": 2}) as i:
                            for q in range(2):
                                hidden(i * 2 + (2 + q), i * 4 + (col + 2 * (done - 1 + q)))
                                split_lo()
                                T.add("slot")
                        done += mn - 2
                    else:
                        with T.loop(dve, (mn - by_hand) // 4, {"slot": 4, "split": 4, "up": 4, "chain": 4}) as i:
                            for q in range(4):
                                hidden(i * 4 + (by_hand + q))
                    down(last and half == 1)
                if col is not None:
                    add_mods(col + 2 * (done - 1))

            def out_projection():
                for s in range(4):
                    split_lo()
                    for m in range(2):
                        residual(2 * s + m, m)
                    T.add("slot")
                    T.add("res")

            def hgrn_step(events, q, h, hnext, ada_cols):
                def att():
                    b = T.n.get("att", 0) % 2
                    T.add("att")
                    T.add(f"att{b}")
                    return ps[:, 4 + b, :], att_done[b], T.at(f"att{b}"), att_read[b]

                for kind, j, n in events:
                    if kind == "tiles":
                        if j % 16 == 0:
                            split_lo()
                        for c in range(4):
                            if not j < 8 * (c + 1) <= j + n:
                                continue
                            if c == 0:
                                dve.wait_ge(act_part, T.at("proj", 1, 2))
                                dve.tensor_tensor(two(qs[:, 1 - q, :]), pair[0], two(sgq[:]), ALU.mult).then_inc(q_read, 1)
                            elif c == 1:
                                dve.wait_ge(f_read, T.at("proj", 1))
                                lb, ub = low[:, 0, bass.ds(hnext, 1)], low[:, 1, bass.ds(hnext, 1)]
                                dve.tensor_scalar(fg[:, 1 - q, :], s1[:], ub, lb, ALU.mult, ALU.add)
                                dve.tensor_scalar(kk[:, 1 - q, :], s2[:], ub, None, ALU.mult).then_inc(fk_done, 1)
                                T.add("slot")
                            elif c == 3:
                                dve.wait_ge(act_part, T.at("proj", 2, 2))
                                dve.tensor_tensor(gg[:, bass.ds(hnext, 1), :].rearrange("p a (h n) -> p (a h) n", h=2),
                                                  pair[1], two(sgg[:]), ALU.mult).then_inc(g_read, 1)
                                T.add("slot")
                                T.add("proj")
                    elif kind == "ada":
                        split_lo()
                        T.add("slot")
                    elif kind == "comb":
                        add_mods(ada_cols[j])
                    elif kind == "level":
                        src, done, count, read = att()
                        dve.wait_ge(done, count)
                        qh, kh, fh = qs[:, q, 0:NP], kk[:, q, 0:NP], fg[:, q, 0:NP]
                        if j == 0:
                            link(dve.memset(attn[:], 0.0))
                            dve.tensor_tensor(qh, qh, fh, ALU.mult).then_inc(level_ready, 1)
                        else:
                            m = 2 ** (j - 1)
                            blocks = NP // (2 * m)
                            t_in = fh if j == 1 else tot[:, NP - 4 * blocks:NP - 2 * blocks]
                            t_in = t_in.rearrange("p (b t) -> p b t", t=2)
                            kb = kh.rearrange("p (b t m) -> p b t m", t=2, m=m)
                            qb = qh.rearrange("p (b t m) -> p b t m", t=2, m=m)
                            link(dve.tensor_tensor(tot[:, NP - 2 * blocks:NP - blocks], t_in[:, :, 0], t_in[:, :, 1],
                                                   ALU.mult))
                            dve.tensor_tensor(kb[:, :, 0, :], kb[:, :, 0, :], t_in[:, :, 1:2].broadcast_to([P, blocks, m]),
                                              ALU.mult)
                            dve.tensor_tensor(qb[:, :, 1, :], qb[:, :, 1, :], t_in[:, :, 0:1].broadcast_to([P, blocks, m]),
                                              ALU.mult).then_inc(level_ready, 1)
                        dve.copy_predicated(attn[:].rearrange("p (c t) -> p c t", c=4),
                                            lmask[:, j, :].unsqueeze(1).broadcast_to([P, 4, P]),
                                            src.rearrange("p (c t) -> p c t", c=4)).then_inc(read, 1)
                    elif kind == "state":
                        src, done, count, read = att()
                        dve.wait_ge(done, count)
                        dve.wait_ge(st_free, T.at("head", 1))
                        link(dve.tensor_copy(st[:, 0, :], src[:, 0:P]))
                        for c in range(1, 4):
                            ins = dve.scalar_tensor_tensor(st[:, c, :], st[:, c - 1, :], tot[:, NP - 8 + c:NP - 7 + c],
                                                           src[:, c * P:(c + 1) * P], ALU.mult, ALU.add)
                            if c < 3:
                                link(ins)
                        ins.then_inc(st_done, 1)
                        dve.wait_ge(st_done, T.at("head", 1))
                        dve.sem_inc(read, 1)
                    elif kind == "outer":
                        src, done, count, read = att()
                        b0 = (T.n["att"] - 1) % 2
                        dve.wait_ge(read, T.at(f"att{b0}", 1))
                        if j == 0:
                            dve.wait_ge(ss_in[q], T.at(f"head{q}", 16, 16))
                        for b in range(4):
                            t = 4 * j + b
                            ins = dve.scalar_tensor_tensor(ss[:, q, t, :], ss[:, q, t, :], fg[:, q, NP + t:NP + t + 1],
                                                           kvo[:, b, :], ALU.mult, ALU.add)
                        ins.then_inc(ss_done, 1)
                    elif kind in ("vt", "kt", "out", "outs"):
                        att()
                        if kind == "outs":
                            T.add("head")
                            T.add(f"head{q}")

            def hgrn_norm():
                for h in range(H + 1):
                    if h < ADA_TAIL:
                        split_lo()
                        T.add("slot")
                    if h >= 1:
                        g = h - 1
                        dve.wait_ge(root_done, T.at("root", g + 1))
                        link(dve.reciprocal(rstd[:], tt[:, g % 2, :]))
                        link(dve.tensor_tensor(tn[:, 0, :], og[:, g, :], rstd[:], ALU.mult))
                        link(dve.scalar_tensor_tensor(tn[:, 1, :], tn[:, 0, :], vec[:, V_HG + g:V_HG + g + 1],
                                                      gg[:, g, :], ALU.mult, ALU.mult))
                        split_act(tn[:, 1, :], hn_hi[:, g, :], hn_lo[:, g, :], hn_done)
                    if h < ADA_TAIL:
                        add_mods(C_L1 + 2 * (H + h))
                T.add("root", H)

            def small_norm(chunks, n, gain, hi, lo):
                dve.wait_ge(root_done, T.at("root", 1))
                T.add("root")
                link(dve.reciprocal(rstd[:], root[:]))
                for c in range(n):
                    link(dve.scalar_tensor_tensor(chunks[:, c, :], chunks[:, c, :], vec[:, gain + c:gain + c + 1],
                                                  rstd[:], ALU.mult, ALU.mult))
                    split_act(chunks[:, c, :], hi[:, c, :], lo[:, c, :])

            dve.sem_inc(up_read, 1)
            dve.sem_inc(x_upd, 2)
            dve.sem_inc(ss_done, 1)
            dve.sem_inc(ct_copied_d, 2)
            dve.sem_inc(ols_done, 1)
            dve.memset(ones[:], 1.0)
            dve.memset(eps[:], EPS)
            split_lo()
            dve.wait_ge(s_in, 16 * 13)
            dve.tensor_copy(ident_r[:], ident)
            dve.wait_ge(start_c, 1)
            scv = scf[:]
            link(dve.tensor_copy(sc18[:, :, 0:SEQS], scv))
            dve.tensor_tensor(sc18[:, :, SEQS:], scv, sc18[:, :, 0:SEQS], ALU.subtract).then_inc(sc_done, 1)
            dve.wait_ge(start_c, 2)
            dve.tensor_tensor(low[:, 0, :], vec[:, V_LB:V_LB + H], vec[:, V_LB + H:V_LB + 2 * H], ALU.subtract
                              ).then_inc(low_ready, 1)
            for c in range(KD):
                dve.wait_ge(x_t, c + 1)
                dve.tensor_copy(x[:, c, 0:NP], ps[:, c % 4, :]).then_inc(x_placed, 1)
            dve.wait_ge(x_t, KD + 1)
            dve.tensor_copy(x[:, :, NP:NT], ps[:, 7, 0:KD * NS].rearrange("p (c s) -> p c s", c=KD)).then_inc(x_placed, 1)
            dve.wait_ge(start_c, 4)
            dve.wait_ge(s_tab, 16)
            ada_run(0, ADA_FIRST)
            norm(C_L0, V_NORM, C_L0 + 16, 0.5)
            ffn(C_L0 + 2 * ADA_FIRST)
            norm(C_L0 + 24, V_NORM + 8, C_L0 + 40, 1.0)
            hgrn_step(project_events(), 1, None, 0, (C_KV, C_L1))
            per = {"slot": 8, "split": 8, "comb": 4, "proj": 2, "att": 30, "att0": 15, "att1": 15, "head": 2,
                   "head0": 1, "head1": 1, "chain": 22}
            with T.loop(dve, 3, per) as i:
                for q in range(2):
                    hgrn_step(hgrn_events(True), q, i * 2 + q, i * 2 + (q + 1),
                              (i * 4 + (C_KV + 2 + 2 * q), i * 4 + (C_L1 + 2 + 2 * q)))
            hgrn_step(hgrn_events(True), 0, 6, 7, (C_KV + 14, C_L1 + 14))
            hgrn_step(hgrn_events(False), 1, 7, None, None)
            hgrn_norm()
            out_projection()
            norm(C_L0 + 48, V_NORM + 16, C_L0 + 64, 0.5)
            ffn(C_L1 + 2 * (H + ADA_TAIL))

            norm(C_KV, V_KVN, None, None)
            split_lo()
            T.add("slot")
            split_lo()
            T.add("slot")
            dve.wait_ge(st_out, 16 * H)
            for j in range(2):
                dve.wait_ge(ss_out[j], 16 * H // 2)
            small_norm(z, RK, V_LAT, ck_hi, ck_lo)
            dve.tensor_copy(cnew[:], z[:, 0:RK, NP:NT]).then_inc(lat_done, 1)
            dve.wait_ge(s_tab, 32)
            cos, sin = cossin[:, 0, :], cossin[:, 1, :]
            dve.wait_ge(z_read, 3)
            dve.tensor_tensor(kr2[:], zr[:], cos, ALU.mult)
            dve.wait_ge(z_done, 2)
            link(dve.tensor_tensor(two(tn[:, 0, :]), pair[0], two(sin), ALU.mult))
            dve.tensor_tensor(kr2[:], kr2[:], tn[:, 0, :], ALU.add).then_inc(rope_done, 1)
            norm(C_L1, V_NORM + 24, C_L1 + 16, 0.5)
            for j in range(2):
                dve.wait_ge(nat_out[j], 64)
            ffn()

            norm(C_L1 + 24, V_NORM + 32, C_L1 + 40, 1.0)
            split_lo()
            T.add("slot")
            split_lo()
            T.add("slot")
            link(dve.memset(qr[:], 0.0))
            small_norm(qz, QK, V_Q, qc_hi, qc_lo)
            dve.memset(t9[:, 1, 0:1], 0.0).then_inc(lat_done, 1)

            def att():
                b = T.n.get("att", 0) % 2
                T.add("att")
                T.add(f"att{b}")
                return ps[:, 4 + b, :], att_done[b], T.at(f"att{b}"), att_read[b]

            for hp in range(4):
                split_lo()
                T.add("slot")
                dve.wait_ge(q_copied, 6 * hp + 3)
                dve.wait_ge(q_done, 4 * hp + 3)
                for s in range(2):
                    rp = slice(s * ROPE, (s + 1) * ROPE)
                    dve.tensor_tensor(qr[rp, s, :], qrz[rp, :], cos[rp, :], ALU.mult)
                link(dve.tensor_tensor(two(tn_m[:]), pair[1], two(sin), ALU.mult))
                for s in range(2):
                    rp = slice(s * ROPE, (s + 1) * ROPE)
                    ins = dve.tensor_tensor(qr[rp, s, :], qr[rp, s, :], tn_m[rp, :], ALU.add)
                ins.then_inc(rope_done, 1)
                split_lo()
                T.add("slot")
                att()
                src, done, count, read = att()
                dve.wait_ge(done, count)
                for s in range(2):
                    for r in range(RK):
                        dve.tensor_copy(ql[:, r, :, 2 * hp + s], src[:, (2 * s + r) * NS:(2 * s + r + 1) * NS])
                dve.tensor_copy(qrs[:, :, 2 * hp], qr[0:ROPE, 0, NP:NT])
                dve.tensor_copy(qrs[:, :, 2 * hp + 1], src[0:ROPE, 4 * NS:5 * NS]).then_inc(read, 1)
                split_lo()
                T.add("slot")
                for u in range(9):
                    if u < 8:
                        w = 8 * hp + u
                        t = u % 4
                        src, done, count, read = att()
                        dve.wait_ge(done, count)
                        diag = src[:, t * P:(t + 1) * P]
                        link(dve.tensor_tensor(diag, diag, causal, ALU.add))
                        link(dve.tensor_reduce(mx[:, w:w + 1], src[:, 0:(t + 1) * P], AX_X, ALU.max))
                        dve.tensor_scalar(nb[:, w:w + 1], mx[:, w:w + 1], -SM_SCALE, None, ALU.mult).then_inc(nb_done, 1)
                        exp_bank = read, count + 1
                    if u >= 1:
                        w = 8 * hp + u - 1
                        n = ((u - 1) % 4 + 1) * P
                        dve.wait_ge(*last_bank)
                        link(dve.reciprocal(rinv[:, w:w + 1], rsum[:, w:w + 1]))
                        dve.tensor_scalar(pp[:, w % 2, 0:n], pp[:, w % 2, 0:n], rinv[:, w:w + 1], None, ALU.mult
                                          ).then_inc(p_done, 1)
                    if u < 8:
                        last_bank = exp_bank
                    if u in (5, 8):
                        s = 0 if u == 5 else 1
                        h = 2 * hp + s
                        dve.wait_ge(o_done, h + 1)
                        link(dve.tensor_copy(hn_hi[:, h, 0:NP], ps[:, 2 * s, :]))
                        dve.tensor_tensor(hn_lo[:, h, 0:NP], ps[:, 2 * s, :], hn_hi[:, h, 0:NP], ALU.subtract
                                          ).then_inc(o_read, 1)

            split_lo()
            per = {"seq": 2, "ct": 8, "chain": 8}
            with T.loop(dve, NS // 2, per) as i:
                for q in range(2):
                    seq = i * 2 + q
                    for r in range(RK):
                        dve.tensor_copy(qsamp[:, q, r, :].unsqueeze(1), ql[:, r, bass.ds(seq, 1), :])
                    dve.tensor_copy(qsamp[0:ROPE, q, RK, :].unsqueeze(1), qrs[:, bass.ds(seq, 1), :]).then_inc(qs_ready, 1)
                    for g in range(4):
                        dve.wait_ge(ct_t, T.at("ct", g + 1))
                        dve.tensor_copy(cts[g % 2][0:ROPE, 2, :], ps[0:ROPE, 4 * (g % 2) + 2, :]).then_inc(ct_copied_d, 1)
                    T.add("ct", 4)
                    dve.wait_ge(new_mul, T.at("seq", 1))
                    link(dve.tensor_tensor(srow[:, PAST:PAST + NS], ps[0:H, 3, 0:NS], newmask[:, bass.ds(i * (2 * NS) + q * NS, NS)],
                                           ALU.add))
                    dve.wait_ge(sc_copied, T.at("ct"))
                    link(dve.tensor_reduce(smx[:, 0:1], srow[:], AX_X, ALU.max))
                    dve.tensor_scalar(smx[:, 1:2], smx[:, 0:1], -SM_SCALE, None, ALU.mult).then_inc(smax_done, 1)
                    dve.wait_ge(exp_done, T.at("seq", 1))
                    link(dve.reciprocal(smx[:, 3:4], smx[:, 2:3]))
                    dve.wait_ge(pages_used, T.at("seq", 3))
                    dve.tensor_scalar(ol[:], ps[0:H, 3, 0:KV], smx[:, 3:4], None, ALU.mult).then_inc(ol_done, 1)
                    dve.wait_ge(olt_done, T.at("seq", 1))
                    link(dve.tensor_copy(ols[:, :, bass.ds(seq, 1), :].rearrange("p r a h -> p r (a h)"),
                                         ps[:, 7, 0:RK * H].rearrange("p (r h) -> p r h", r=RK)))
                    dve.sem_inc(ols_done, 1)
                    T.add("seq")
            olf = ols[:].rearrange("p r b h -> p (r b h)")
            split_act(olf, ol_hi[:].rearrange("p r b h -> p (r b h)"), ol_lo[:].rearrange("p r b h -> p (r b h)"), olsplit)
            dve.wait_ge(slot_used, T.at("slot", 1))
            T.add("slot")
            heads = ps[:, 0, 0:H * NS].rearrange("p (h s) -> p h s", h=H)
            link(dve.tensor_copy(hn_hi[:, :, NP:NT], heads))
            dve.tensor_tensor(hn_lo[:, :, NP:NT], heads, hn_hi[:, :, NP:NT], ALU.subtract).then_inc(os_split, 1)
            out_projection()
            norm(C_L1 + 48, V_NORM + 40, C_L1 + 64, 0.5)
            ffn(last=True)

            dve.wait_ge(root_done, T.at("root", 1))
            link(dve.reciprocal(rstd[:], root[:]))
            for c in range(KD):
                dve.scalar_tensor_tensor(yt[:, c, :], x[:, c, :], vec[:, V_FINAL + c:V_FINAL + c + 1], rstd[:],
                                         ALU.mult, ALU.mult).then_inc(y_done, 1)


_INS = ["x_prompt", "x_sample", "c_prompt", "c_sample", "state_hgrn", "cache_ckv", "cache_krope", "page_table", "w_ada",
        "b_ada", "g_norm", "w_ffn_gu", "w_ffn_down", "hg_w_in", "hg_lb", "hg_g_out", "hg_w_out", "kv_w_ada",
        "kv_b_ada", "kv_g_norm", "kv_w_down", "kv_g_latent", "kv_w_uk", "kv_w_uv", "q_w_down", "q_g_norm", "q_w_up",
        "attn_w_out", "g_final"]
_OUTS = [(1, NP, D), (NS, 1, D), (1, 1, H, P, P), (1, NS, H, P, P), (1, NP, KV), (1, NP, ROPE), (NS, 1, KV),
         (NS, 1, ROPE)]


def _tables():
    import numpy as np
    c = np.zeros((P, K_END), np.float32)
    c[:, K_ID:K_ID + P] = np.eye(P)
    half = ROPE // 2
    for base in (0, ROPE):
        for n in range(half):
            c[base + n + half, K_ROT + base + n] = -1.0
            c[base + n, K_ROT + base + n + half] = 1.0
    c[:, K_CAUS:K_CAUS + P] = np.triu(np.full((P, P), NEG, np.float32), 1)
    for n in range(SEQS):
        c[n, K_COMB + n] = c[SEQS + n, K_COMB + n] = 1.0
    new = np.full((NS, NS), NEG, np.float32)
    np.fill_diagonal(new, 0.0)
    c[0:H, K_NEW:K_NEW + 64] = new.reshape(1, 64)
    masks = np.zeros((P, 8, P), np.uint32)
    for s in range(P):
        for t in range(s, P):
            masks[s, (s ^ t).bit_length(), t] = 1
    pos = np.concatenate([np.arange(NP), np.full(NS, PAST)]).astype(np.float32)
    freq = (np.float32(10000.0) ** (np.float32(-2.0) * np.arange(half, dtype=np.float32) / np.float32(ROPE))).astype(np.float32)
    ang = (pos[None, :] * np.tile(freq, 4)[:, None]).astype(np.float32)
    rotary = np.stack([np.cos(ang), np.sin(ang)], axis=1).astype(np.float32)
    return {"consts": c, "level_masks": masks, "rotary": rotary}


def kernel(**inputs):
    import numpy as _np
    import concourse.bacc as _bacc
    from concourse import mybir as _mybir
    from concourse.bass_utils import run_bass_kernel_spmd as _run

    nc = _bacc.Bacc("TRN2", target_bir_lowering=False, num_devices=1)
    arrays, aps = {}, {}
    given = {n: _np.ascontiguousarray(inputs[n]) for n in _INS}
    given.update(_tables())
    for name, a in given.items():
        arrays[f"in_{name}"] = a
        aps[name] = nc.dram_tensor(f"in_{name}", a.shape, _mybir.dt.from_np(a.dtype), kind="ExternalInput").ap()
    outs = [nc.dram_tensor(f"out_{i}", s, _mybir.dt.float32, kind="ExternalOutput").ap() for i, s in enumerate(_OUTS)]
    build(nc, aps, *outs)
    r = _run(nc, [arrays], core_ids=[0])
    return tuple(r.results[0][f"out_{i}"] for i in range(len(_OUTS)))
```

```python
from contextlib import ExitStack, contextmanager

import concourse.bass as bass
from concourse import mybir

F32 = mybir.dt.float32
F32R = mybir.dt.float32r
U32 = mybir.dt.uint32
I32 = mybir.dt.int32
ALU = mybir.AluOpType
ACT = mybir.ActivationFunctionType
AX_X = mybir.AxisListType.X

P = 128
D = 1024
KD = D // P
NP = 512
NS = 8
NT = NP + NS
HT = NT // 2
DFF = 2816
MF = DFF // P
MFA = 12
MFB = MF - MFA
H = 8
KV = 256
RK = KV // P
RQ = 384
QK = RQ // P
ROPE = 64
PAST = 2048
PAGE = 128
NPG = PAST // PAGE
SEQS = 1 + NS
EPS = 1e-6
SM_SCALE = (P + ROPE) ** -0.5
RAW = 4
AHEAD = 2
SLOT = 2048
LAND = 64
ADA_W = 256
ADA_L = 9 * D // ADA_W
C_L0, C_KV, C_L1 = 0, 72, 88
NMOD = 160
V_NORM, V_FINAL, V_KVN, V_LAT, V_Q, V_HG, V_LB = 0, 48, 56, 64, 66, 69, 77
NVEC = 93
NEG = -3.0e38
K_ID, K_ROT, K_CAUS, K_COMB, K_NEW, K_END = 0, 128, 256, 384, 400, 464
ADA_FIRST = 14
ADA_FFN = MF
ADA_TAIL = ADA_L - ADA_FFN - H


def _stream():
    def ffn(with_ada):
        out = []
        for mn in (MFA, MFB):
            out += [SLOT] * (mn * (2 if with_ada else 1)) + [mn // 2 * 256] * 8
        return out
    return ([SLOT] * ADA_FIRST + ffn(True) + [SLOT] * (4 * H + ADA_TAIL + 4) + ffn(True) + [SLOT, KD * P] + ffn(False)
            + [SLOT, KD * P] + [QK * 384, RK * 256, RK * 256] * 4 + [RK * D] + [SLOT] * 4 + ffn(False))


STREAM = _stream()
SLOTS = len(STREAM)


class Tally:

    def __init__(self):
        self.n, self.per, self.i = {}, {}, None

    def add(self, key, by=1):
        self.n[key] = self.n.get(key, 0) + by

    def at(self, key, extra=0, times=1):
        v = self.n.get(key, 0) * times + extra
        if self.i is not None and self.per.get(key, 0):
            return self.i * (self.per[key] * times) + v
        return v

    def words(self, k):
        passes = range(self.count if self.i is not None else 1)
        assert len({STREAM[k + n * self.per.get("split", 0)] for n in passes}) == 1, k
        return STREAM[k]

    @contextmanager
    def loop(self, eng, count, per):
        before = dict(self.n)
        with eng.Fori(0, count) as i:
            self.i, self.per, self.count = i, per, count
            yield i
        self.i = None
        for k in list(self.n):
            step = self.n[k] - before.get(k, 0)
            assert step == per.get(k, 0), (k, step, per.get(k, 0))
            self.n[k] = before.get(k, 0) + count * step
        self.per = {}


def hgrn_events(project):
    t = (lambda a, n: [("tiles", a, n)]) if project else (lambda a, n: [])
    ada = (lambda j: [("ada", j, 0)]) if project else (lambda j: [])
    comb = (lambda j: [("comb", j, 0)]) if project else (lambda j: [])
    g = lambda kind, j=0: [(kind, j, 0)]
    return (g("vt") + t(0, 3) + g("level", 0) + t(3, 3) + g("level", 1) + t(6, 3) + g("level", 2) + t(9, 3)
            + g("level", 3) + t(12, 2) + g("outer", 0) + t(14, 2) + ada(0) + g("level", 4) + t(16, 2) + comb(0)
            + g("level", 5) + t(18, 2) + g("outer", 1) + t(20, 2) + g("level", 6) + t(22, 2) + g("level", 7)
            + t(24, 2) + g("kt") + t(26, 2) + g("state") + t(28, 2) + g("out") + t(30, 2) + ada(1)
            + g("outs") + comb(1))


def last_events():
    events, out, h = hgrn_events(False), [], 0
    for e in events:
        out.append(e)
        if e[0] in ("level", "outer") and h < H - 1:
            out.append(("norm", h, 0))
            h += 1
    return out + [("norm", n, 0) for n in range(h, H + 1)]


def project_events():
    return [("fresh", 0, 16), ("ada", 0, 0), ("tiles", 16, 8), ("comb", 0, 0), ("tiles", 24, 8), ("ada", 1, 0),
            ("comb", 1, 0)]


def build(nc, a, y_prompt, y_sample, st_prompt, st_sample, ckv_prompt, kr_prompt, ckv_sample, kr_sample):
    ctx = ExitStack()
    with ctx:
        at = [(nc.sbuf_base + 63) // 64 * 64]

        def place(name, shape, dt=F32, where=None):
            words = 1
            for s in shape[1:]:
                words *= s
            off = at[0] if where is None else where
            if where is None:
                at[0] += (4 * words + 63) // 64 * 64
            return nc.alloc_sbuf_tensor_at(name, list(shape), dt, offset=off)

        def group(first, *parts):
            out, off = [], first
            for name, shape, dt in parts:
                words = 1
                for s in shape[1:]:
                    words *= s
                out.append(place(name, shape, dt, off))
                off += (4 * words + 63) // 64 * 64
            return out, off

        def sem(name):
            return ctx.enter_context(nc.semaphore(name))

        x = place("x", [P, KD, NT])
        hn_hi = place("hn_hi", [P, KD, NT], F32R)
        hn_lo = place("hn_lo", [P, KD, NT], F32R)
        raw = [place(f"raw{r}", [P, SLOT]) for r in range(RAW)]
        w_lo = [place(f"w_lo{r}", [P, SLOT], F32R, at[0] - 4 * SLOT * (RAW - r)) for r in range(RAW)]
        w_hi = place("w_hi", [P, RAW, SLOT], F32R)
        mods = place("mods", [P, NMOD, SEQS])
        bias = place("bias", [P, NMOD])
        vec = place("vec", [P, NVEC])
        amod = place("amod", [P, KD, SEQS])
        gate = place("gate", [P, KD * SEQS])
        sc18 = place("sc18", [P, KD, 2 * SEQS], F32R)
        cst = place("cst", [P, K_END])
        ident = cst[:, K_ID:K_ID + P]
        rot = cst[:, K_ROT:K_ROT + P]
        causal = cst[:, K_CAUS:K_CAUS + P]
        comb = cst[0:2 * SEQS, K_COMB:K_COMB + SEQS]
        newmask = cst[0:H, K_NEW:K_NEW + 64]
        ident_r = place("ident_r", [P, P], F32R)
        ones = place("ones", [P, P])
        eps = place("eps", [P, 1])
        low = place("low", [P, 2, H])
        rows = place("rows", [2 * SEQS, ADA_W])
        t9 = place("t9", [P, 2, SEQS])
        ts = place("ts", [P, KD, NS])
        pt_sb = place("pt_sb", [1, NS * NPG], I32)
        tabs = at[0]
        cossin = place("cossin", [P, 2, NT])
        lmask = place("lmask", [P, 8, P], U32, tabs)
        lat = at[0]
        ck_hi = place("ck_hi", [P, RK, NT], F32R)
        ck_lo = place("ck_lo", [P, RK, NT], F32R)
        kr2 = place("kr2", [P, NT])
        ckn = place("ckn", [NS, KV + ROPE])
        ql = place("ql", [P, RK, NS, H])
        qrs = place("qrs", [ROPE, NS, H])
        qsamp = place("qsamp", [P, 2, RK + 1, H])
        cnew = place("cnew", [P, RK, NS])
        scr = at[0]
        sq = place("sq", [P, 2, NT])
        root = place("root", [P, NT])
        rstd = place("rstd", [P, NT])
        tn = place("tn", [P, 2, NT])
        tt = place("tt", [P, 2, NT])
        ar = at[0]
        end = nc.sbuf_usable_end
        (xr, xs, cr, vrow, brow0, brow1, scf), e0 = group(
            ar, ("xr", [P, 4, D], F32), ("xs", [NS, D], F32), ("cr", [SEQS, D], F32), ("vrow", [NVEC, P], F32),
            ("brow0", [C_L1, P], F32), ("brow1", [NMOD - C_L1, P], F32), ("scf", [P, KD, SEQS], F32))
        (hid_hi, hid_lo), e1 = group(ar, ("hid_hi", [P, MFA, NT], F32R), ("hid_lo", [P, MFA, NT], F32R))
        (sg, hf), e2 = group(scr, ("sg", [P, 2, NT], F32), ("hf", [P, NT], F32))
        (og, gg, qs, fg, kk, vv), e3 = group(
            ar, ("og", [P, H, NT], F32), ("gg", [P, H, NT], F32), ("qs", [P, 2, NT], F32), ("fg", [P, 2, NT], F32),
            ("kk", [P, 2, NT], F32), ("vv", [P, 2, NT], F32))
        (sgq, sgg, s1, s2, attn, vn, kn_n, tot), e4 = group(
            scr, ("sgq", [P, NT], F32), ("sgg", [P, NT], F32), ("s1", [P, NT], F32), ("s2", [P, NT], F32),
            ("attn", [P, NP], F32), ("vn", [P, 4, P], F32), ("kn_n", [P, 4, P], F32), ("tot", [P, NP], F32))
        norm_root, norm_t = [kk[:, 0, :], vv[:, 0, :]], [qs[:, 0, :], fg[:, 0, :]]
        (ss,), e5 = group(lat, ("ss", [P, 2, NS, P], F32))
        (kvo, st), e6 = group(e5, ("kvo", [P, 4, P], F32), ("st", [P, 4, P], F32))
        (z, zr, nat), e7 = group(ar, ("z", [P, QK, NT], F32), ("zr", [P, NT], F32), ("nat", [P, 2, KV + ROPE], F32))
        (qz,), _ = group(ar, ("qz", [P, QK, NT], F32))
        pages_end = ar + 4 * NPG * KV
        (qc_hi, qc_lo, qn, qrz, qr, kn, vh, ukt), e8 = group(
            pages_end, ("qc_hi", [P, QK, NT], F32R), ("qc_lo", [P, QK, NT], F32R),
            ("qn", [P, 2, NT], F32), ("qrz", [P, NT], F32), ("qr", [P, 2, NT], F32), ("kn", [P, 2, NP], F32),
            ("vh", [P, 4, 2 * P], F32), ("ukt", [P, 2, RK, P], F32))
        (pp, ppt, mx, nb, rsum, rinv), e9 = group(
            scr, ("pp", [P, 3, NP], F32), ("ppt", [P, 2, NP], F32), ("mx", [P, 32], F32), ("nb", [P, 32], F32),
            ("rsum", [P, 32], F32), ("rinv", [P, 32], F32))
        tn_m = place("tn_m", [P, NT], F32, scr)
        (pg0, pg1, pgk1, ct0, ct1, ol), e10 = group(
            ar, ("pg0", [P, NPG, KV], F32), ("pg1", [P, NPG, KV], F32), ("pgk1", [P, NPG, ROPE], F32),
            ("ct0", [P, 3, 512], F32), ("ct1", [P, 3, 512], F32), ("ol", [H, KV], F32))
        (srow, pts, smx, ol_hi, ol_lo, ols), e11 = group(
            scr, ("srow", [H, PAST + NS], F32), ("pts", [P, NPG + 1, H], F32), ("smx", [H, 8], F32),
            ("ol_hi", [P, RK, NS, H], F32R), ("ol_lo", [P, RK, NS, H], F32R), ("ols", [P, RK, NS, H], F32))
        (pgk0,), e13 = group(max(e9, e11), ("pgk0", [P, NPG, ROPE], F32))
        pg, pgk = [pg0, pg1], [pgk0, pgk1]
        cts = [ct0, ct1]
        (yt, ynat, yns), e12 = group(ar, ("yt", [P, KD, NT], F32), ("ynat", [P, 2, D], F32), ("yns", [NS, D], F32))
        assert max(e0, e1, e3, e7, e8, e10, e12) <= end, (ar, end, e0, e1, e3, e7, e8, e10, e12)
        assert max(e2, e4, e13) <= ar and e6 <= scr, (ar, scr, e2, e4, e9, e11, e6)

        ps = ctx.enter_context(nc.psum_tensor("ps", [P, 8, 512], F32))
        pair = [ps[:, 2 * b:2 * b + 2, 0:HT] for b in range(3)]

        def two(ap):
            return ap.rearrange("p (h n) -> p h n", h=2)

        s_in = sem("inputs_landed")
        s_xin = sem("x_landed")
        s_tab = sem("rotary_tables_landed")
        s_pt = sem("page_table_landed")
        landed = [sem(f"weights_landed{r}") for r in range(RAW)]
        hi_done = sem("hi_half_written")
        split_done = sem("lo_half_written")
        slot_used = sem("slot_multiplied")
        start_t = sem("start_transposed")
        start_c = sem("start_copied")
        sc_done = sem("silu_c_split")
        low_ready = sem("bound_logits_ready")
        low_done = sem("bounds_made")
        x_t = sem("x_transposed")
        x_placed = sem("x_placed")
        rows_copied = sem("ada_rows_copied")
        comb_done = sem("ada_rows_combined")
        mods_added = sem("mods_added")
        chain = sem("vector_step")
        xsq_done = sem("x_squares_made")
        xsq_added = sem("x_squares_added")
        x_stats = sem("x_squares_summed")
        x_root = sem("x_root_taken")
        sq_done = sem("squares_made")
        stats_done = sem("squares_summed")
        root_done = sem("root_taken")
        tn_done = sem("normed_chunk")
        aff_done = sem("modulated_chunk")
        hn_done = sem("hn_chunk_split")
        gate_done = sem("gate_chunk_multiplied")
        gate_read = sem("gate_chunk_read")
        up_read = sem("up_chunk_read")
        hid_done = sem("hidden_chunk_split")
        res_done = sem("residual_chunk_multiplied")
        x_upd = sem("x_chunk_updated")
        proj_mid = sem("first_chunk_of_slot_multiplied")
        act_part = sem("sigmoids_taken")
        q_read = sem("q_chunk_read")
        f_read = sem("f_chunk_read")
        i_read = sem("i_chunk_read")
        g_read = sem("g_chunk_read")
        fk_done = sem("forget_and_key_made")
        att_done = [sem(f"att_bank_multiplied{j}") for j in range(2)]
        att_read = [sem(f"att_bank_read{j}") for j in range(2)]
        level_ready = sem("level_operands_ready")
        st_done = sem("states_made")
        st_out = sem("prompt_state_stored")
        st_free = sem("prompt_state_buffer_free")
        ss_in = [sem(f"sample_states_landed{j}") for j in range(2)]
        ss_done = sem("sample_states_updated")
        outs_read = sem("sample_outputs_read")
        ss_out = [sem(f"sample_states_stored{j}") for j in range(2)]
        z_read = sem("latent_chunk_read")
        z_done = sem("latent_chunk_multiplied")
        lat_done = sem("latent_normed")
        rope_done = sem("rope_applied")
        nat_t = sem("rows_transposed")
        nat_read = sem("rows_copied")
        nat_out = [sem(f"rows_stored{j}") for j in range(2)]
        small_out = sem("sample_rows_stored")
        q_done = sem("query_piece_multiplied")
        q_copied = sem("query_piece_copied")
        nb_done = sem("row_maxima_ready")
        p_done = sem("weights_normalised")
        pt_t = sem("weights_transposed")
        pt_copied = sem("weights_t_copied")
        o_done = sem("head_values_summed")
        o_read = sem("head_values_split")
        pages_in = [[sem(f"pages_landed{j}_half{k}") for k in range(2)] for j in range(2)]
        pages_used = sem("pages_multiplied")
        ct_t = sem("pages_transposed")
        ct_copied_a = sem("latent_pages_copied")
        ct_copied_d = sem("rope_pages_copied")
        sc_mul = sem("page_scores_multiplied")
        sc_copied = sem("page_scores_copied")
        smax_done = sem("sample_maxima_ready")
        exp_done = sem("sample_weights_ready")
        pts_t = sem("sample_weights_transposed")
        pts_copied = sem("sample_weights_t_copied")
        ol_done = sem("sample_values_scaled")
        olt_done = sem("sample_values_transposed")
        ols_done = sem("sample_values_placed")
        os_split = sem("sample_heads_split")
        qs_ready = sem("sequence_queries_ready")
        new_mul = sem("new_score_multiplied")
        olsplit = sem("sample_values_split")
        y_done = sem("y_chunk_made")
        y_t = sem("y_transposed")
        y_copied = sem("y_copied")
        y_out = [sem(f"y_stored{j}") for j in range(2)]

        ada_v = [a["w_ada"][l].rearrange("(k p) n -> p k n", p=P) for l in range(2)]
        kvada_v = a["kv_w_ada"].rearrange("(k p) n -> p k n", p=P)
        gu_v = {(l, j): a["w_ffn_gu"][l, j].rearrange("(k p) (g f) -> p k g f", p=P, g=2)
                for l in range(2) for j in range(2)}
        dn_v = {(l, j): a["w_ffn_down"][l, j].rearrange("(k p) n -> p k n", p=P) for l in range(2) for j in range(2)}
        hg_v = a["hg_w_in"][0].rearrange("(k p) (g f) -> p k g f", p=P, g=4)
        hgo_v = a["hg_w_out"][0].rearrange("(k p) n -> p k n", p=P)
        kvd_v = a["kv_w_down"].rearrange("(k p) n -> p k n", p=P)
        qd_v = a["q_w_down"][0].rearrange("(k p) n -> p k n", p=P)
        qu_v = a["q_w_up"][0].rearrange("(k p) h n -> p k h n", p=P)
        uk_v = a["kv_w_uk"].rearrange("(k p) h n -> p k (h n)", p=P)
        uv_v = a["kv_w_uv"].rearrange("(k p) h n -> p k (h n)", p=P)
        ao_v = a["attn_w_out"][0].rearrange("(k p) n -> p k n", p=P)
        st_in_v = a["state_hgrn"][0].rearrange("b h k v -> h k b v")
        st_s_v = st_sample[0].rearrange("b h k v -> h k b v")
        st_p_v = st_prompt[0, 0]

        block = ctx.enter_context(nc.Block())

        @block.sync
        def _(sp):
            T = Tally()

            def slot(loads):
                k = T.n.get("slot", 0)
                r = k % RAW
                if k >= RAW:
                    sp.wait_ge(slot_used, T.at("slot", 1 - RAW))
                for dst, src in loads(raw[r][:]):
                    sp.dma_start(dst, src).then_inc(landed[r], LAND // len(loads(raw[r][:])))
                T.add("slot")

            def columns(view, col, width, k0=0, kn=KD):
                h = (kn + 1) // 2

                def loads(w):
                    d = w[:, 0:kn * width].rearrange("p (k n) -> p k n", k=kn)
                    return [(d[:, 0:h, :], view[:, k0:k0 + h, bass.ds(col, width)]),
                            (d[:, h:kn, :], view[:, k0 + h:k0 + kn, bass.ds(col, width)])]
                return slot(loads)

            def gate_up(view, m):
                def loads(w):
                    d = w.rearrange("p (k g n) -> p k g n", k=KD, g=2)
                    return [(d[:, :, g, :], view[:, :, g, bass.ds(m * P, P)]) for g in range(2)]
                return slot(loads)

            def ada_run(view, first, n):
                for j in range(min(4, n)):
                    columns(view, (first + j) * ADA_W, ADA_W)
                full = max(0, n - 4) // 4
                if full:
                    with T.loop(sp, full, {"slot": 4}) as i:
                        for j in range(4):
                            columns(view, i * (4 * ADA_W) + (first + 4 + j) * ADA_W, ADA_W)
                for j in range(4 + 4 * full, n):
                    columns(view, (first + j) * ADA_W, ADA_W)

            def ffn(l, j, ada=None):
                for m0, mn, kn in ((0, MFA, MFA // 2), (MFA, MFB, MFB // 2)):
                    if ada is not None:
                        view, first = ada
                        with T.loop(sp, mn // 2, {"slot": 4}) as i:
                            for q in range(2):
                                gate_up(gu_v[l, j], i * 2 + (m0 + q))
                                columns(view, i * (2 * ADA_W) + (first + m0 + q) * ADA_W, ADA_W)
                    else:
                        with T.loop(sp, mn // 4, {"slot": 4}) as i:
                            for q in range(4):
                                gate_up(gu_v[l, j], i * 4 + (m0 + q))
                        for q in range(mn // 4 * 4, mn):
                            gate_up(gu_v[l, j], m0 + q)
                    with T.loop(sp, 2, {"slot": 4}) as i:
                        for q in range(2):
                            for s in range(2):
                                columns(dn_v[l, j], i * 512 + q * 256, 256, m0 + s * kn, kn)

            def hgrn_project(h):
                def loads(w, g0=0):
                    d = w.rearrange("p (k g n) -> p k g n", k=KD, g=2)
                    return [(d[:, :, g, :], hg_v[:, :, g0 + g, bass.ds(h * P, P)]) for g in range(2)]
                slot(loads)
                columns(kvada_v, h * ADA_W, ADA_W)
                slot(lambda w: loads(w, 2))
                columns(ada_v[1], h * ADA_W, ADA_W)

            ada_run(ada_v[0], 0, ADA_FIRST)
            ffn(0, 0, (ada_v[0], ADA_FIRST))
            hgrn_project(0)
            with T.loop(sp, 3, {"slot": 8}) as i:
                for q in range(2):
                    hgrn_project(i * 2 + (q + 1))
            hgrn_project(7)
            for j in range(ADA_TAIL):
                columns(ada_v[1], (H + j) * ADA_W, ADA_W)
            for m in range(4):
                columns(hgo_v, m * 256, 256)
            ffn(0, 1, (ada_v[1], H + ADA_TAIL))
            columns(kvd_v, 0, 256)
            slot(lambda w: [(w[:, 0:KD * P].rearrange("p (k n) -> p k n", k=KD)[:, :, s * ROPE:(s + 1) * ROPE],
                             kvd_v[:, :, KV:KV + ROPE]) for s in range(2)])
            ffn(1, 0)
            columns(qd_v, 0, 256)
            columns(qd_v, 256, 128)
            for hp in range(4):
                def loads(w, hp=hp):
                    d = w[:, 0:QK * 384].rearrange("p (k n) -> p k n", k=QK)
                    out = []
                    for s in range(2):
                        out.append((d[:, :, s * P:(s + 1) * P], qu_v[:, :, 2 * hp + s, 0:P]))
                        out.append((d[:, :, 256 + s * ROPE:256 + (s + 1) * ROPE], qu_v[:, :, 2 * hp + s, P:P + ROPE]))
                    return out
                slot(loads)
                columns(uk_v, hp * 256, 256, 0, RK)
                columns(uv_v, hp * 256, 256, 0, RK)
            ckv_pages = a["cache_ckv"].rearrange("n p r -> p n r")
            kr_pages = a["cache_krope"].rearrange("n p r -> p n r")
            top = a["cache_ckv"].shape[0] - 1

            def pages(seq, q):
                sp.wait_ge(pages_used, T.at("seq", 1))
                for p in range(NPG):
                    v = sp.value_load(pt_sb[0:1, bass.ds(seq * NPG + p, 1)], min_val=0, max_val=top)
                    sp.dma_start(pg[q][:, p, :], ckv_pages[:, bass.ds(v, 1), :].rearrange("p a r -> p (a r)")
                                 ).then_inc(pages_in[q][2 * p // NPG], 16)
                    sp.dma_start(pgk[q][:, p, :], kr_pages[:, bass.ds(v, 1), :].rearrange("p a r -> p (a r)")
                                 ).then_inc(pages_in[q][2 * p // NPG], 16)
                T.add("seq")

            sp.wait_ge(s_pt, 16)
            sp.wait_ge(lat_done, 2)
            pages(0, 0)
            columns(uv_v, 0, D, 0, RK)
            columns(ao_v, 0, 256)
            columns(ao_v, 256, 256)
            sp.wait_ge(o_read, H)
            with T.loop(sp, NS // 2 - 1, {"seq": 2}) as i:
                pages(i * 2 + 1, 1)
                pages(i * 2 + 2, 0)
            pages(NS - 1, 1)
            columns(ao_v, 512, 256)
            columns(ao_v, 768, 256)
            ffn(1, 1)

        @block.gpsimd
        def _(pool):
            T = Tally()
            pool.sem_inc(pages_used, 2)
            pool.sem_inc(st_free, 1)
            pool.dma_start(cst[:], a["consts"]).then_inc(s_in, 16)
            pool.dma_start(cr[0:1, :], a["c_prompt"]).then_inc(s_in, 16)
            pool.dma_start(cr[1:SEQS, :], a["c_sample"]).then_inc(s_in, 16)
            rows_of = lambda v: v.rearrange("(c p) -> c p", p=P)
            pool.dma_start(brow0[0:72, :], rows_of(a["b_ada"][0])).then_inc(s_in, 16)
            pool.dma_start(brow0[72:88, :], rows_of(a["kv_b_ada"])).then_inc(s_in, 16)
            pool.dma_start(brow1[:], rows_of(a["b_ada"][1])).then_inc(s_in, 16)
            pool.dma_start(vrow[V_NORM:V_FINAL, :], a["g_norm"].rearrange("l j (c p) -> (l j c) p", p=P)).then_inc(s_in, 16)
            pool.dma_start(vrow[V_FINAL:V_KVN, :], rows_of(a["g_final"])).then_inc(s_in, 16)
            pool.dma_start(vrow[V_KVN:V_LAT, :], rows_of(a["kv_g_norm"])).then_inc(s_in, 16)
            pool.dma_start(vrow[V_LAT:V_Q, :], rows_of(a["kv_g_latent"])).then_inc(s_in, 16)
            pool.dma_start(vrow[V_Q:V_HG, :], rows_of(a["q_g_norm"][0])).then_inc(s_in, 16)
            pool.dma_start(vrow[V_HG:V_LB, :], rows_of(a["hg_g_out"][0])).then_inc(s_in, 16)
            pool.dma_start(vrow[V_LB:NVEC, :], a["hg_lb"].rearrange("l (c p) -> (l c) p", p=P)).then_inc(s_in, 16)
            for t in range(4):
                pool.dma_start(xr[:, t, :], a["x_prompt"][0, t * P:(t + 1) * P, :]).then_inc(s_xin, 16)
            pool.dma_start(xs[:], a["x_sample"].rearrange("b s d -> (b s) d")).then_inc(s_xin, 16)
            pool.dma_start(lmask[:], a["level_masks"]).then_inc(s_tab, 16)
            pool.dma_start(pt_sb[:], a["page_table"].rearrange("b n -> (b n)").rearrange("(a n) -> a n", a=1)
                           ).then_inc(s_pt, 16)

            def head_in(h, q):
                pool.dma_start(ss[:, q, :, :], st_in_v[bass.ds(h, 1)].rearrange("a k b v -> k (a b) v")
                               ).then_inc(ss_in[q], 16)

            def head_out(h, q):
                pool.wait_ge(st_done, T.at("head", 1))
                pool.nop(nofuse=True)
                pool.dma_start(st_p_v[bass.ds(h, 1)].rearrange("a k v -> (a k) v"), st[:, 3, :]).then_inc(st_out, 16)
                pool.wait_ge(ss_done, T.at("head", 3, 2))
                pool.nop(nofuse=True)
                pool.dma_start(st_s_v[bass.ds(h, 1)].rearrange("a k b v -> k (a b) v"), ss[:, q, :, :]
                               ).then_inc(ss_out[q], 16)
                pool.wait_ge(st_out, T.at("head", 16, 16))
                pool.sem_inc(st_free, 1)
                pool.wait_ge(ss_out[q], T.at(f"head{q}", 16, 16))
                pool.wait_ge(outs_read, T.at("head", 1))
                pool.nop(nofuse=True)
                T.add("head")
                T.add(f"head{q}")

            head_in(0, 0)
            head_in(1, 1)
            with T.loop(pool, 3, {"head": 2, "head0": 1, "head1": 1}) as i:
                for q in range(2):
                    head_out(i * 2 + q, q)
                    head_in(i * 2 + (q + 2), q)
            head_out(6, 0)
            head_out(7, 1)
            pool.dma_start(cossin[:], a["rotary"]).then_inc(s_tab, 16)
            for t in range(4):
                pool.wait_ge(nat_read, t + 1)
                pool.dma_start(ckv_prompt[0, t * P:(t + 1) * P, :], nat[:, t % 2, 0:KV]).then_inc(nat_out[t % 2], 16)
                pool.dma_start(kr_prompt[0, t * P:(t + 1) * P, :], nat[:, t % 2, KV:]).then_inc(nat_out[t % 2], 16)
            pool.wait_ge(nat_read, 5)
            pool.dma_start(ckv_sample.rearrange("b s r -> (b s) r"), ckn[:, 0:KV]).then_inc(small_out, 16)
            pool.dma_start(kr_sample.rearrange("b s r -> (b s) r"), ckn[:, KV:]).then_inc(small_out, 16)
            for t in range(4):
                pool.wait_ge(y_copied, 2 * t + 2)
                pool.dma_start(y_prompt[0, t * P:(t + 1) * P, :], ynat[:, t % 2, :]).then_inc(y_out[t % 2], 16)
            pool.wait_ge(y_copied, 10)
            pool.dma_start(y_sample.rearrange("b s d -> (b s) d"), yns[:]).then_inc(small_out, 16)
            pool.wait_ge(st_out, 16 * H)
            pool.wait_ge(small_out, 48)
            for j in range(2):
                pool.wait_ge(ss_out[j], 16 * 4)
                pool.wait_ge(nat_out[j], 64)
                pool.wait_ge(y_out[j], 32)

        @block.tensor
        def _(pe):
            T = Tally()

            def split():
                pe.wait_ge(split_done, T.at("slot", 1))

            def slabs(kn, width):
                b = T.n.get("slot", 0) % RAW
                return (w_hi[:, b, 0:kn * width].rearrange("p (k n) -> p k n", k=kn),
                        w_lo[b][:, 0:kn * width].rearrange("p (k n) -> p k n", k=kn))

            def tile(out, wh, wl, xh, xl, start, stop):
                for t in range(2):
                    c = slice(t * HT, (t + 1) * HT)
                    pe.matmul(out[:, t, :], wh, xh[:, c], start=start, stop=False)
                    pe.matmul(out[:, t, :], wh, xl[:, c], start=False, stop=False)
                    mm = pe.matmul(out[:, t, :], wl, xh[:, c], start=False, stop=stop)
                return mm

            def chunk(out, hi, lo, col, xh, xl, kn, fresh=False):
                for k in range(kn):
                    if fresh:
                        pe.wait_ge(hn_done, T.at("hn", k + 1))
                    mm = tile(out, hi[:, k, col:col + P], lo[:, k, col:col + P], xh[:, k, :], xl[:, k, :],
                              k == 0, k == kn - 1)
                return mm

            def ada():
                hi, lo = slabs(KD, ADA_W)
                if T.n.get("ada", 0) or T.i is not None:
                    pe.wait_ge(rows_copied, T.at("ada"))
                split()
                for k in range(KD):
                    pe.matmul(ps[0:18, 6, 0:ADA_W], sc18[:, k, :], hi[:, k, :], start=(k == 0), stop=False)
                    mm = pe.matmul(ps[0:18, 6, 0:ADA_W], sc18[:, k, :], lo[:, k, :], start=False, stop=(k == 7))
                mm.then_inc(slot_used, 1)
                T.add("slot")
                T.add("ada")

            def ada_comb():
                pe.wait_ge(rows_copied, T.at("ada"))
                if T.n.get("comb", 0) or T.i is not None:
                    pe.wait_ge(mods_added, T.at("comb"))
                for j in range(2):
                    mm = pe.matmul(ps[:, 7, j * SEQS:(j + 1) * SEQS], rows[:, j * P:(j + 1) * P], comb,
                                   start=True, stop=True)
                mm.then_inc(comb_done, 1)
                T.add("comb")

            def ada_run(n):
                for j in range(min(4, n)):
                    ada()
                    ada_comb()
                full = max(0, n - 4) // 4
                if full:
                    with T.loop(pe, full, {"slot": 4, "ada": 4, "comb": 4}):
                        for j in range(4):
                            ada()
                            ada_comb()
                for j in range(4 + 4 * full, n):
                    ada()
                    ada_comb()

            def sum_squares(n, out=2):
                for c in range(n):
                    pe.wait_ge(sq_done, T.at("sq", c + 1))
                    for t in range(2):
                        mm = pe.matmul(pair[out][:, t, :], ones[:], sq[:, c % 2, t * HT:(t + 1) * HT],
                                       start=(c == 0), stop=(c == n - 1))
                    mm.then_inc(stats_done, 1)
                T.add("sq", n)
                T.add("root")

            def x_squares():
                pe.wait_ge(xsq_added, T.at("xn", KD - 1, KD - 1))
                for t in range(2):
                    pe.matmul(pair[2][:, t, :], ones[:], rstd[:, t * HT:(t + 1) * HT], start=True, stop=False)
                pe.wait_ge(xsq_done, T.at("xn", KD, KD))
                for t in range(2):
                    mm = pe.matmul(pair[2][:, t, :], ones[:], sq[:, (KD - 1) % 2, t * HT:(t + 1) * HT], start=False, stop=True)
                mm.then_inc(x_stats, 1)
                T.add("xn")

            def fresh_pair(hi, lo):
                for k in range(KD):
                    pe.wait_ge(hn_done, T.at("hn", k + 1))
                    ends = []
                    for m in range(2):
                        c = slice(m * P, (m + 1) * P)
                        ends.append(tile(pair[m], hi[:, k, c], lo[:, k, c], hn_hi[:, k, :], hn_lo[:, k, :], k == 0,
                                         k == KD - 1))
                T.add("hn", KD)
                return ends

            def hidden(fresh=False, combine=False, first=False):
                hi, lo = slabs(KD, 2 * P)
                split()
                pe.wait_ge(gate_read, T.at("up", 1))
                if first:
                    pe.wait_ge(x_upd, T.at("res", 1))
                if fresh:
                    pe.wait_ge(x_upd, T.at("res", 2))
                    pe.wait_ge(up_read, T.at("up", 1))
                    gate_end, up_end = fresh_pair(hi, lo)
                    gate_end.then_inc(gate_done, 1)
                    up_end.then_inc(slot_used, 1)
                    T.add("up")
                    T.add("slot")
                    return
                chunk(pair[0], hi, lo, 0, hn_hi, hn_lo, KD).then_inc(gate_done, 1)
                if combine:
                    ada_comb()
                pe.wait_ge(up_read, T.at("up", 1))
                if first:
                    pe.wait_ge(x_upd, T.at("res", 2))
                chunk(pair[1], hi, lo, P, hn_hi, hn_lo, KD).then_inc(slot_used, 1)
                T.add("up")
                T.add("slot")

            def down(kn):
                with T.loop(pe, 2, {"slot": 4, "res": 4}):
                    for q in range(2):
                        for s in range(2):
                            hi, lo = slabs(kn, 256)
                            split()
                            if q == 0:
                                pe.wait_ge(hid_done, T.n["hid"] - (0 if s else kn))
                            for m in range(2):
                                if s == 0:
                                    pe.wait_ge(x_upd, T.at("res", m + 1))
                                    if q == 0:
                                        pe.wait_ge(up_read if m else gate_read, T.at("up", 1))
                                for k in range(kn):
                                    c = slice(m * P, (m + 1) * P)
                                    mm = tile(pair[m], hi[:, k, c], lo[:, k, c], hid_hi[:, s * kn + k, :],
                                              hid_lo[:, s * kn + k, :], s == 0 and k == 0, s == 1 and k == kn - 1)
                                if s == 1 and m == 0:
                                    mm.then_inc(res_done, 1)
                            mm.then_inc(slot_used, 1)
                            T.add("slot")
                        T.add("res", 2)

            def ffn(with_ada):
                for half, mn in ((0, MFA), (1, MFB)):
                    by_hand = 2 if with_ada else mn % 4 or 4
                    for m in range(by_hand):
                        hidden(half == 0 and m == 0, with_ada and (half or m), m == 0)
                        if with_ada:
                            ada()
                    if with_ada:
                        with T.loop(pe, (mn - 2) // 2, {"slot": 4, "up": 2, "ada": 2, "comb": 2}):
                            for q in range(2):
                                hidden(False, True)
                                ada()
                    else:
                        with T.loop(pe, (mn - by_hand) // 4, {"slot": 4, "up": 4}):
                            for q in range(4):
                                hidden()
                    T.add("hid", mn)
                    down(mn // 2)
                if with_ada:
                    ada_comb()

            def out_projection(fresh):
                for s in range(4):
                    hi, lo = slabs(KD, 256)
                    split()
                    if fresh and s == 0:
                        pe.wait_ge(x_upd, T.at("res", 2))
                        ends = fresh_pair(hi, lo)
                    for m in range(2):
                        if fresh and s == 0:
                            mm = ends[m]
                        else:
                            pe.wait_ge(x_upd, T.at("res", m + 1))
                            mm = chunk(pair[m], hi, lo, m * P, hn_hi, hn_lo, KD)
                        mm.then_inc(slot_used if m else res_done, 1)
                    T.add("slot")
                    T.add("res", 2)

            def hgrn_step(events, q, first):
                def att():
                    b = T.n.get("att", 0) % 2
                    pe.wait_ge(att_read[b], T.at(f"att{b}", 1))
                    T.add("att")
                    T.add(f"att{b}")
                    return ps[:, 4 + b, :], att_done[b]

                for kind, j, n in events:
                    if kind == "fresh":
                        split()
                        i_end, f_end = fresh_pair(*slabs(KD, 2 * P))
                        i_end.then_inc(proj_mid, 1)
                        f_end.then_inc(slot_used, 1)
                        T.add("slot")
                    elif kind == "tiles":
                        for idx in range(j, j + n):
                            c, k = divmod(idx, KD)
                            hi, lo = slabs(KD, 2 * P)
                            if k == 0:
                                if c == 0:
                                    split()
                                    if not first:
                                        pe.wait_ge(i_read, T.at("proj"))
                                elif c == 1:
                                    if not first:
                                        pe.wait_ge(g_read, T.at("proj"))
                                elif c == 2:
                                    split()
                                    pe.wait_ge(q_read, T.at("proj", 1))
                                else:
                                    pe.wait_ge(f_read, T.at("proj", 1))
                            col = (c % 2) * P
                            mm = tile(pair[c % 2], hi[:, k, col:col + P], lo[:, k, col:col + P], hn_hi[:, k, :],
                                      hn_lo[:, k, :], k == 0, k == 7)
                            if k == 7:
                                mm.then_inc(slot_used if c % 2 else proj_mid, 1)
                                if c % 2:
                                    T.add("slot")
                                if c == 3:
                                    T.add("proj")
                    elif kind == "norm":
                        hgrn_norm(j)
                    elif kind == "ada":
                        ada()
                    elif kind == "comb":
                        ada_comb()
                    elif kind == "vt":
                        out, done = att()
                        pe.wait_ge(i_read, T.at("head", 1))
                        pe.wait_ge(fk_done, T.at("head", 1))
                        pe.wait_ge(q_read, T.at("head", 1))
                        for c in range(4):
                            mm = pe.transpose(out[:, c * P:(c + 1) * P], vv[:, q, c * P:(c + 1) * P], ident)
                        mm.then_inc(done, 1)
                    elif kind == "level":
                        if j:
                            pe.wait_ge(level_ready, T.at("level", j))
                        out, done = att()
                        for c in range(4):
                            s = slice(c * P, (c + 1) * P)
                            mm = pe.matmul(out[:, s], kk[:, q, s], qs[:, q, s], start=True, stop=True)
                        mm.then_inc(done, 1)
                    elif kind == "outer":
                        out, done = att()
                        for b in range(4):
                            v = vv[:, q, NP + 4 * j + b:NP + 4 * j + b + 1].broadcast_to([P, P])
                            mm = pe.matmul(out[:, b * P:(b + 1) * P], v, ident, start=True, stop=True)
                        mm.then_inc(done, 1)
                    elif kind == "kt":
                        pe.wait_ge(level_ready, T.at("level", 8))
                        T.add("level", 8)
                        out, done = att()
                        for c in range(4):
                            mm = pe.transpose(out[:, c * P:(c + 1) * P], kk[:, q, c * P:(c + 1) * P], ident)
                        mm.then_inc(done, 1)
                    elif kind == "state":
                        out, done = att()
                        other = T.n["att"] % 2
                        pe.wait_ge(att_read[other], T.at(f"att{other}", 1))
                        for c in range(4):
                            mm = pe.matmul(out[:, c * P:(c + 1) * P], kn_n[:, c, :], vn[:, c, :], start=True, stop=True)
                        mm.then_inc(done, 1)
                    elif kind == "out":
                        out, done = att()
                        for c in range(4):
                            s = slice(c * P, (c + 1) * P)
                            if c == 1:
                                pe.wait_ge(st_done, T.at("head", 1))
                            mm = pe.matmul(out[:, s], vn[:, c, :], attn[:, s], start=True, stop=(c == 0))
                            if c:
                                mm = pe.matmul(out[:, s], st[:, c - 1, :], qs[:, q, s], start=False, stop=True)
                        mm.then_inc(done, 1)
                    elif kind == "outs":
                        out, done = att()
                        pe.wait_ge(ss_done, T.at("head", 3, 2))
                        for b in range(NS):
                            mm = pe.matmul(out[:, b:b + 1], ss[:, q, b, :], qs[:, q, NP + b:NP + b + 1],
                                           start=True, stop=True)
                        mm.then_inc(done, 1)
                        T.add("head")

            def hgrn_norm(h):
                if h == H:
                    pe.wait_ge(root_done, T.at("root"))
                    return
                pe.wait_ge(sq_done, T.at("sq", 1))
                if h == 0:
                    pe.wait_ge(i_read, T.at("proj"))
                    pe.wait_ge(g_read, T.at("proj"))
                if h >= 2:
                    pe.wait_ge(root_done, T.at("root", -1))
                for t in range(2):
                    mm = pe.matmul(pair[h % 2][:, t, :], ones[:], sq[:, h % 2, t * HT:(t + 1) * HT], start=True, stop=True)
                mm.then_inc(stats_done, 1)
                T.add("sq")
                T.add("root")
                if h < ADA_TAIL:
                    ada()
                    ada_comb()

            pe.wait_ge(s_in, 16 * 13)
            for c in range(KD):
                pe.transpose(ps[:, 4, c * SEQS:(c + 1) * SEQS], cr[:, c * P:(c + 1) * P], ident[0:SEQS, 0:SEQS])
            pe.transpose(ps[:, 5, 0:NVEC], vrow[:], ident[0:NVEC, 0:NVEC])
            pe.transpose(ps[:, 5, 128:128 + C_L1], brow0[:], ident[0:C_L1, 0:C_L1])
            pe.transpose(ps[:, 5, 256:256 + NMOD - C_L1], brow1[:], ident[0:NMOD - C_L1, 0:NMOD - C_L1]
                         ).then_inc(start_t, 1)
            pe.wait_ge(s_xin, 16 * 5)
            for c in range(KD):
                if c >= 4:
                    pe.wait_ge(x_placed, c - 3)
                for t in range(4):
                    mm = pe.transpose(ps[:, c % 4, t * P:(t + 1) * P], xr[:, t, c * P:(c + 1) * P], ident)
                mm.then_inc(x_t, 1)
            for c in range(KD):
                mm = pe.transpose(ps[:, 7, c * NS:(c + 1) * NS], xs[:, c * P:(c + 1) * P], ident[0:NS, 0:NS])
            mm.then_inc(x_t, 1)
            pe.wait_ge(x_placed, KD + 1)
            pe.wait_ge(sc_done, 1)
            ada_run(ADA_FIRST)
            x_squares()
            ffn(True)
            x_squares()
            hgrn_step(project_events(), 1, True)
            per = {"slot": 8, "ada": 4, "comb": 4, "proj": 2, "att": 30, "att0": 15, "att1": 15, "level": 16, "head": 2}
            with T.loop(pe, 3, per):
                for q in range(2):
                    hgrn_step(hgrn_events(True), q, False)
            hgrn_step(hgrn_events(True), 0, False)
            hgrn_step(last_events(), 1, False)
            out_projection(True)
            x_squares()
            ffn(True)

            x_squares()
            hi, lo = slabs(KD, 256)
            split()
            z_end, slot_end = fresh_pair(hi, lo)
            z_end.then_inc(z_done, 1)
            slot_end.then_inc(slot_used, 1)
            T.add("slot")
            hi, lo = slabs(KD, P)
            split()
            pe.wait_ge(z_read, 1)
            chunk(pair[0], hi, lo, 0, hn_hi, hn_lo, KD).then_inc(slot_used, 1)
            T.add("slot")
            pe.wait_ge(z_read, 2)
            sum_squares(RK, 1)
            pe.wait_ge(z_read, 3)
            for t in range(2):
                mm = pe.matmul(pair[0][:, t, :], rot, zr[:, t * HT:(t + 1) * HT], start=True, stop=True)
            mm.then_inc(z_done, 1)
            pe.wait_ge(lat_done, 1)
            pe.wait_ge(rope_done, 1)
            for t in range(5):
                b = 6 + t % 2
                if t >= 2:
                    pe.wait_ge(nat_read, t - 1)
                s, n = (slice(t * P, (t + 1) * P), P) if t < 4 else (slice(NP, NT), NS)
                for r in range(RK):
                    pe.transpose(ps[0:n, b, r * P:(r + 1) * P], z[:, r, s], ident)
                pe.transpose(ps[0:n, b, KV:KV + ROPE], kr2[0:ROPE, s], ident[0:ROPE, 0:ROPE]).then_inc(nat_t, 1)

            ffn(False)

            x_squares()
            for s, n in ((0, 2), (1, 1)):
                hi, lo = slabs(KD, 256 if s == 0 else P)
                split()
                if s == 0:
                    z_end, slot_end = fresh_pair(hi, lo)
                    z_end.then_inc(z_done, 1)
                else:
                    pe.wait_ge(z_read, 4)
                    slot_end = chunk(pair[0], hi, lo, 0, hn_hi, hn_lo, KD)
                slot_end.then_inc(slot_used, 1)
                T.add("slot")
            pe.wait_ge(z_read, 5)
            sum_squares(QK, 1)
            pe.wait_ge(lat_done, 2)
            for hp in range(4):
                hi, lo = slabs(QK, 384)
                split()
                if hp:
                    pe.wait_ge(o_read, 2 * hp - 1)
                chunk(pair[0], hi, lo, 0, qc_hi, qc_lo, QK).then_inc(q_done, 1)
                if hp:
                    pe.wait_ge(o_read, 2 * hp)
                chunk(pair[1], hi, lo, P, qc_hi, qc_lo, QK).then_inc(q_done, 1)
                pe.wait_ge(q_copied, 6 * hp + 1)
                chunk(pair[0], hi, lo, 2 * P, qc_hi, qc_lo, QK).then_inc(slot_used, 1)
                T.add("slot")
                pe.wait_ge(q_copied, 6 * hp + 3)
                for t in range(2):
                    mm = pe.matmul(pair[1][:, t, :], rot, qrz[:, t * HT:(t + 1) * HT], start=True, stop=True)
                mm.then_inc(q_done, 1)
                hi, lo = slabs(RK, 256)
                split()
                for s in range(2):
                    for r in range(RK):
                        wh, wl = hi[:, r, s * P:(s + 1) * P], lo[:, r, s * P:(s + 1) * P]
                        pe.matmul(ps[:, s, :], wh, ck_hi[:, r, 0:NP], start=(r == 0), stop=False)
                        pe.matmul(ps[:, s, :], wh, ck_lo[:, r, 0:NP], start=False, stop=False)
                        mm = pe.matmul(ps[:, s, :], wl, ck_hi[:, r, 0:NP], start=False, stop=(r == 1))
                mm.then_inc(q_done, 1)
                b = T.n.get("att", 0) % 2
                pe.wait_ge(att_read[b], T.at(f"att{b}", 1))
                for s in range(2):
                    for r in range(RK):
                        o = ps[:, 4 + b, (2 * s + r) * P:(2 * s + r + 1) * P]
                        pe.matmul(o, hi[:, r, s * P:(s + 1) * P], ident_r[:], start=True, stop=False)
                        mm = pe.matmul(o, lo[:, r, s * P:(s + 1) * P], ident_r[:], start=False, stop=True)
                mm.then_inc(att_done[b], 1)
                T.add("att")
                T.add(f"att{b}")
                b = T.n["att"] % 2
                pe.wait_ge(att_read[b], T.at(f"att{b}", 1))
                pe.wait_ge(q_copied, 6 * hp + 5)
                pe.wait_ge(rope_done, hp + 2)
                for s in range(2):
                    for r in range(RK):
                        mm = pe.matmul(ps[:, 4 + b, (2 * s + r) * NS:(2 * s + r + 1) * NS], ukt[:, s, r, :],
                                       qn[:, s, NP:NT], start=True, stop=True)
                mm.then_inc(slot_used, 1)
                T.add("slot")
                pe.matmul(ps[0:ROPE, 4 + b, 4 * NS:5 * NS], ident[:, ROPE:P], qr[:, 1, NP:NT], start=True, stop=True
                          ).then_inc(att_done[b], 1)
                T.add("att")
                T.add(f"att{b}")
                hi, lo = slabs(RK, 256)
                split()
                for c in range(4):
                    o = ps[:, 2 + c // 2, (c % 2) * 256:(c % 2) * 256 + 256]
                    for r in range(RK):
                        th, tl = ck_hi[:, r, c * P:(c + 1) * P], ck_lo[:, r, c * P:(c + 1) * P]
                        pe.matmul(o, th, hi[:, r, :], start=(r == 0), stop=False)
                        pe.matmul(o, tl, hi[:, r, :], start=False, stop=False)
                        mm = pe.matmul(o, th, lo[:, r, :], start=False, stop=(r == 1))
                mm.then_inc(slot_used, 1)
                T.add("slot")
                pe.wait_ge(q_copied, 6 * hp + 6)
                units = [(s, t) for s in range(2) for t in range(4)]
                for u in range(len(units) + 3):
                    if u < 8:
                        s, t = units[u]
                        n = (t + 1) * P
                        b = T.n["att"] % 2
                        pe.wait_ge(att_read[b], T.at(f"att{b}", 1))
                        pe.matmul(ps[:, 4 + b, 0:n], qn[:, s, t * P:(t + 1) * P], kn[:, s, 0:n], start=True, stop=False)
                        pe.matmul(ps[:, 4 + b, 0:n], qr[:, s, t * P:(t + 1) * P], kr2[:, 0:n], start=False, stop=True
                                  ).then_inc(att_done[b], 1)
                        T.add("att")
                        T.add(f"att{b}")
                    if 2 <= u <= 9:
                        s, t = units[u - 2]
                        w = 8 * hp + u - 2
                        pe.wait_ge(p_done, w + 1)
                        if w >= 2:
                            pe.wait_ge(pt_copied, w - 1)
                        for c in range(t + 1):
                            mm = pe.transpose(ps[:, 6 + w % 2, c * P:(c + 1) * P], pp[:, w % 3, c * P:(c + 1) * P], ident)
                        mm.then_inc(pt_t, 1)
                    if u >= 3:
                        s, t = units[u - 3]
                        w = 8 * hp + u - 3
                        pe.wait_ge(pt_copied, w + 1)
                        for c in range(t + 1):
                            mm = pe.matmul(ps[:, 2 * s, t * P:(t + 1) * P], vh[:, c, s * P:(s + 1) * P],
                                           ppt[:, w % 2, c * P:(c + 1) * P], start=(c == 0), stop=(c == t))
                        if t == 3:
                            mm.then_inc(o_done, 1)

            pe.wait_ge(o_read, H)
            per = {"seq": 2, "seq0": 1, "seq1": 1, "ct": 8}
            def turn(g, q):
                b = 4 * (g % 2)
                pe.wait_ge(ct_copied_a, T.at("ct", g + 1))
                pe.wait_ge(ct_copied_d, T.at("ct", g + 1))
                for p in range(4):
                    for r in range(RK):
                        pe.transpose(ps[:, b + r, p * P:(p + 1) * P], pg[q][:, 4 * g + p, r * P:(r + 1) * P], ident)
                    mm = pe.transpose(ps[0:ROPE, b + 2, p * P:(p + 1) * P], pgk[q][:, 4 * g + p, :], ident)
                mm.then_inc(ct_t, 1)

            def scores(g, q):
                pe.wait_ge(ct_copied_a, T.at("ct", g + 3))
                pe.wait_ge(ct_copied_d, T.at("ct", g + 3))
                if g >= 2:
                    pe.wait_ge(sc_copied, T.at("ct", g - 1))
                o = ps[0:H, 3 + 4 * (g % 2), :]
                for r in range(RK):
                    pe.matmul(o, qsamp[:, q, r, :], cts[g % 2][:, r, :], start=(r == 0), stop=False)
                pe.matmul(o, qsamp[0:ROPE, q, 2, :], cts[g % 2][0:ROPE, 2, :], start=False, stop=True
                          ).then_inc(sc_mul, 1)

            def first_turns(q):
                pe.wait_ge(pages_in[q][0], T.at(f"seq{q}", 16 * NPG, 16 * NPG))
                T.add(f"seq{q}")
                turn(0, q)
                turn(1, q)

            def sequence(q, more):
                pe.wait_ge(qs_ready, T.at("seq", 1))
                scores(0, q)
                pe.wait_ge(pages_in[q][1], T.at(f"seq{q}", 0, 16 * NPG))
                turn(2, q)
                pe.wait_ge(ols_done, T.at("seq", 1))
                scores(1, q)
                turn(3, q)
                scores(2, q)
                scores(3, q)
                T.add("ct", 4)
                pe.wait_ge(sc_copied, T.at("ct", -1))
                for r in range(RK):
                    pe.matmul(ps[0:H, 3, 0:NS], qsamp[:, q, r, :], cnew[:, r, :], start=(r == 0), stop=False)
                pe.matmul(ps[0:H, 3, 0:NS], qsamp[0:ROPE, q, 2, :], kr2[0:ROPE, NP:NT], start=False, stop=True
                          ).then_inc(new_mul, 1)
                if more:
                    first_turns(1 - q)
                pe.wait_ge(exp_done, T.at("seq", 1))
                pe.wait_ge(sc_copied, T.at("ct"))
                pe.nop(nofuse=True)
                for p in range(NPG):
                    pe.transpose(ps[:, 7, p * H:(p + 1) * H], srow[:, p * P:(p + 1) * P], ident[0:H, 0:H])
                pe.transpose(ps[0:NS, 7, NPG * H:(NPG + 1) * H], srow[:, PAST:PAST + NS], ident[0:H, 0:H]
                             ).then_inc(pts_t, 1)
                pe.wait_ge(pts_copied, T.at("seq", 1))
                for p in range(NPG):
                    pe.matmul(ps[0:H, 3, 0:KV], pts[:, p, :], pg[q][:, p, :], start=(p == 0), stop=False)
                pe.matmul(ps[0:H, 3, 0:KV], pts[0:NS, NPG, :], ckn[:, 0:KV], start=False, stop=True
                          ).then_inc(pages_used, 1)
                pe.wait_ge(ol_done, T.at("seq", 1))
                pe.nop(nofuse=True)
                for r in range(RK):
                    mm = pe.transpose(ps[:, 7, r * H:(r + 1) * H], ol[:, r * P:(r + 1) * P], ident[0:H, 0:H])
                mm.then_inc(olt_done, 1)
                T.add("seq")

            first_turns(0)
            with T.loop(pe, NS // 2 - 1, per):
                sequence(0, True)
                sequence(1, True)
            sequence(0, True)
            sequence(1, False)
            pe.wait_ge(olsplit, 1)
            split()
            hi, lo = slabs(RK, D)
            for h in range(H):
                o = ps[:, 0, h * NS:(h + 1) * NS]
                for r in range(RK):
                    wh, wl = hi[:, r, h * P:(h + 1) * P], lo[:, r, h * P:(h + 1) * P]
                    pe.matmul(o, wh, ol_hi[:, r, :, h], start=(r == 0), stop=False)
                    pe.matmul(o, wh, ol_lo[:, r, :, h], start=False, stop=False)
                    mm = pe.matmul(o, wl, ol_hi[:, r, :, h], start=False, stop=(r == 1))
            mm.then_inc(slot_used, 1)
            T.add("slot")
            pe.wait_ge(os_split, 1)
            out_projection(False)
            x_squares()
            ffn(False)

            x_squares()
            for t in range(5):
                s, n = (slice(t * P, (t + 1) * P), P) if t < 4 else (slice(NP, NT), NS)
                for half in range(2):
                    w = 2 * t + half
                    if t == 0:
                        pe.wait_ge(y_done, KD // 2 * (half + 1))
                    if w >= 4:
                        pe.wait_ge(y_copied, w - 3)
                    for c in range(4):
                        mm = pe.transpose(ps[0:n, 4 + w % 4, c * P:(c + 1) * P], yt[:, 4 * half + c, s], ident)
                    mm.then_inc(y_t, 1)


        @block.scalar
        def _(act):
            T = Tally()

            def split_hi():
                k = T.n.get("split", 0)
                if k == SLOTS:
                    return
                r = k % RAW
                turns = LAND * (k // RAW + 1)
                if T.i is not None:
                    turns = T.i * (LAND * T.per["split"] // RAW) + turns
                act.wait_ge(landed[r], turns)
                n = T.words(k)
                act.activation(w_hi[:, r, 0:n], raw[r][:, 0:n], ACT.Copy).then_inc(hi_done, 1)
                T.add("split")

            def ada():
                split_hi()
                act.wait_ge(slot_used, T.at("slot", 1))
                if T.n.get("ada", 0):
                    act.wait_ge(comb_done, T.at("ada"))
                act.activation(rows[:], ps[0:2 * SEQS, 6, 0:ADA_W], ACT.Copy).then_inc(rows_copied, 1)
                T.add("slot")
                T.add("ada")

            def ada_run(n):
                for j in range(min(4, n)):
                    ada()
                full = max(0, n - 4) // 4
                if full:
                    with T.loop(act, full, {"slot": 4, "split": 4, "ada": 4}):
                        for j in range(4):
                            ada()
                for j in range(4 + 4 * full, n):
                    ada()

            def squares(n, source):
                for c in range(n):
                    src = source(c)
                    if T.n.get("sq", 0) + c >= 2:
                        act.wait_ge(stats_done, T.at("sq", c - 1))
                    act.activation(sq[:, c % 2, :], src, ACT.Square).then_inc(sq_done, 1)
                T.add("sq", n)

            def take_root(n, out=2):
                act.wait_ge(stats_done, T.at("sq"))
                act.activation(two(root[:]), pair[out], ACT.Sqrt, scale=1.0 / (n * P), bias=eps[:, 0:1]
                               ).then_inc(root_done, 1)

            def x_square(c, wait=None):
                if wait is not None:
                    act.wait_ge(*wait)
                if c >= 2:
                    act.wait_ge(xsq_added, T.at("xn", c - 1, KD - 1))
                act.activation(sq[:, c % 2, :], x[:, c, :], ACT.Square).then_inc(xsq_done, 1)

            def updated(c):
                return x_upd, T.at("res", 3 + c)

            def x_root_of():
                act.wait_ge(x_stats, T.at("xn", 1))
                act.activation(two(root[:]), pair[2], ACT.Sqrt, scale=1.0 / D, bias=eps[:, 0:1]).then_inc(x_root, 1)
                T.add("xn")

            def norm(base, fresh=True):
                if fresh:
                    x_root_of()
                for c in range(KD):
                    act.wait_ge(tn_done, T.at("hn", c + 1))
                    if c >= 2:
                        act.wait_ge(hn_done, T.at("hnd", c - 1))
                    mod = dict(scale=amod[:, c, 0:1], bias=mods[:, base + c, 0:1])
                    act.activation(tt[:, c % 2, 0:NP], tn[:, c % 2, 0:NP], ACT.Identity, **mod)
                    act.activation(hn_hi[:, c, 0:NP], tn[:, c % 2, 0:NP], ACT.Identity, **mod).then_inc(aff_done, 1)
                T.add("hn", KD)
                T.add("hnd", KD)

            def hidden():
                split_hi()
                act.wait_ge(gate_done, T.at("up", 1))
                if T.n.get("up", 0) >= 2:
                    act.wait_ge(up_read, T.at("up"))
                act.activation(two(sg[:, T.n.get("up", 0) % 2, :]), pair[0], ACT.Silu).then_inc(gate_read, 1)
                T.add("up")
                T.add("slot")

            def ffn(with_ada):
                for half, mn in ((0, MFA), (1, MFB)):
                    by_hand = 2 if with_ada else mn
                    for m in range(by_hand):
                        hidden()
                        if with_ada:
                            ada()
                    if with_ada:
                        with T.loop(act, (mn - 4) // 2, {"slot": 4, "split": 4, "up": 2, "ada": 2}):
                            for q in range(2):
                                hidden()
                                ada()
                        for m in range(2):
                            hidden()
                            ada()
                    for c in range(KD):
                        split_hi()
                        T.add("slot")
                        if half and c % 2:
                            x_square(c - 1, updated(c - 1))
                            x_square(c, updated(c))
                    T.add("res", KD)

            def out_projection():
                for c in range(0, KD, 2):
                    split_hi()
                    T.add("slot")
                    x_square(c, updated(c))
                    x_square(c + 1, updated(c + 1))
                T.add("res", KD)

            def hgrn_step(events, q, h):
                def att():
                    b = T.n.get("att", 0) % 2
                    T.add("att")
                    T.add(f"att{b}")
                    return ps[:, 4 + b, :], att_done[b], T.at(f"att{b}"), att_read[b]

                for kind, j, n in events:
                    if kind in ("tiles", "fresh"):
                        if j % 16 == 0:
                            split_hi()
                        for c in range(4):
                            if not j < 8 * (c + 1) <= j + n:
                                continue
                            if c == 0:
                                act.wait_ge(proj_mid, T.at("proj", 1, 2))
                                act.activation(two(sgq[:]), pair[0], ACT.Sigmoid).then_inc(act_part, 1)
                            elif c == 1:
                                act.wait_ge(slot_used, T.at("slot", 1))
                                act.activation(two(s1[:]), pair[1], ACT.Sigmoid)
                                act.activation(two(s2[:]), pair[1], ACT.Sigmoid, scale=-1.0).then_inc(f_read, 1)
                                T.add("slot")
                            elif c == 2:
                                act.wait_ge(proj_mid, T.at("proj", 2, 2))
                                act.activation(two(vv[:, 1 - q, :]), pair[0], ACT.Copy).then_inc(i_read, 1)
                            else:
                                act.wait_ge(slot_used, T.at("slot", 1))
                                act.activation(two(sgg[:]), pair[1], ACT.Sigmoid).then_inc(act_part, 1)
                                T.add("slot")
                                T.add("proj")
                    elif kind == "norm":
                        hgrn_norm(j)
                    elif kind == "ada":
                        ada()
                    elif kind == "vt":
                        src, done, count, read = att()
                        act.wait_ge(done, count)
                        act.activation(vn[:].rearrange("p c k -> p (c k)"), src, ACT.Copy).then_inc(read, 1)
                    elif kind == "kt":
                        src, done, count, read = att()
                        act.wait_ge(done, count)
                        act.activation(kn_n[:].rearrange("p c k -> p (c k)"), src, ACT.Copy).then_inc(read, 1)
                    elif kind == "outer":
                        src, done, count, read = att()
                        act.wait_ge(done, count)
                        act.wait_ge(ss_done, T.at("head", j + 1, 2))
                        for b in range(4):
                            t = NP + 4 * j + b
                            mm = act.activation(kvo[:, b, :], src[:, b * P:(b + 1) * P], ACT.Copy, scale=kk[:, q, t:t + 1])
                        mm.then_inc(read, 1)
                    elif kind == "out":
                        src, done, count, read = att()
                        act.wait_ge(done, count)
                        act.activation(og[:, bass.ds(h, 1), 0:NP], src.unsqueeze(1), ACT.Copy).then_inc(read, 1)
                    elif kind == "outs":
                        src, done, count, read = att()
                        act.wait_ge(done, count)
                        act.activation(og[:, bass.ds(h, 1), NP:NT], src[:, 0:NS].unsqueeze(1), ACT.Copy).then_inc(read, 1)
                        b0 = (T.n["att"] - 1) % 2
                        act.wait_ge(read, T.at(f"att{b0}", 1))
                        act.sem_inc(outs_read, 1)
                        T.add("head")
                    elif kind in ("level", "state"):
                        att()

            def hgrn_norm(h):
                if h in (0, H - 1):
                    act.wait_ge(att_read[0], T.at("att0", 1))
                    act.wait_ge(att_read[1], T.at("att1", 1))
                if h == 0:
                    act.wait_ge(g_read, T.at("proj"))
                if h < H:
                    if h >= 2:
                        act.wait_ge(stats_done, T.at("sq", -1))
                    act.activation(sq[:, h % 2, :], og[:, h, :], ACT.Square).then_inc(sq_done, 1)
                    T.add("sq")
                if h >= 1:
                    g = h - 1
                    act.wait_ge(stats_done, T.at("sq", 0 if h == H else -1))
                    if g >= 2:
                        act.wait_ge(hn_done, T.at("hnd", g - 1))
                    act.activation(two(norm_root[g % 2]), pair[g % 2], ACT.Sqrt, scale=1.0 / P, bias=eps[:, 0:1]
                                   ).then_inc(root_done, 1)
                if h < ADA_TAIL:
                    ada()
                if h == H:
                    T.add("hnd", H)

            act.sem_inc(gate_read, 1)
            act.sem_inc(ct_copied_a, 2)
            for j in range(2):
                act.sem_inc(att_read[j], 1)
            for _ in range(AHEAD):
                split_hi()
            act.wait_ge(start_t, 1)
            act.activation(scf[:].rearrange("p k s -> p (k s)"), ps[:, 4, 0:KD * SEQS], ACT.Silu).then_inc(start_c, 1)
            act.activation(vec[:], ps[:, 5, 0:NVEC], ACT.Copy).then_inc(start_c, 1)
            act.activation(bias[:, 0:C_L1], ps[:, 5, 128:128 + C_L1], ACT.Copy).then_inc(start_c, 1)
            act.activation(bias[:, C_L1:NMOD], ps[:, 5, 256:256 + NMOD - C_L1], ACT.Copy).then_inc(start_c, 1)
            act.wait_ge(low_ready, 1)
            act.activation(low[:, 1, :], low[:, 0, :], ACT.Sigmoid, scale=-1.0).then_inc(low_done, 1)
            act.wait_ge(low_done, 1)
            act.activation(low[:, 0, :], low[:, 0, :], ACT.Sigmoid).then_inc(low_done, 1)
            ada_run(ADA_FIRST)
            for c in range(KD):
                x_square(c, (x_placed, KD + 1))
            norm(C_L0)
            ffn(True)
            norm(C_L0 + 24)
            hgrn_step(project_events(), 1, 0)
            per = {"slot": 8, "split": 8, "ada": 4, "proj": 2, "att": 30, "att0": 15, "att1": 15, "head": 2}
            with T.loop(act, 3, per) as i:
                for q in range(2):
                    hgrn_step(hgrn_events(True), q, i * 2 + q)
            hgrn_step(hgrn_events(True), 0, 6)
            hgrn_step(last_events(), 1, 7)
            out_projection()
            norm(C_L0 + 48)
            ffn(True)

            norm(C_KV)
            split_hi()
            act.wait_ge(z_done, 1)
            act.activation(two(z[:, 0, :]), pair[0], ACT.Copy).then_inc(z_read, 1)
            act.wait_ge(slot_used, T.at("slot", 1))
            act.activation(two(z[:, 1, :]), pair[1], ACT.Copy).then_inc(z_read, 1)
            T.add("slot")
            split_hi()
            act.wait_ge(slot_used, T.at("slot", 1))
            act.activation(two(zr[:]), pair[0], ACT.Copy).then_inc(z_read, 1)
            T.add("slot")
            act.wait_ge(z_read, 2)
            squares(RK, lambda c: z[:, c, :])
            take_root(RK, 1)
            for t in range(5):
                act.wait_ge(nat_t, t + 1)
                if t in (2, 3):
                    act.wait_ge(nat_out[t % 2], 32)
                n = P if t < 4 else NS
                dst = nat[:, t % 2, :] if t < 4 else ckn[:]
                act.activation(dst, ps[0:n, 6 + t % 2, 0:KV + ROPE], ACT.Copy).then_inc(nat_read, 1)
            norm(C_L1, False)
            ffn(False)

            norm(C_L1 + 24)
            split_hi()
            act.wait_ge(z_done, 3)
            act.activation(two(qz[:, 0, :]), pair[0], ACT.Copy).then_inc(z_read, 1)
            act.wait_ge(slot_used, T.at("slot", 1))
            act.activation(two(qz[:, 1, :]), pair[1], ACT.Copy).then_inc(z_read, 1)
            T.add("slot")
            split_hi()
            act.wait_ge(slot_used, T.at("slot", 1))
            act.activation(two(qz[:, 2, :]), pair[0], ACT.Copy).then_inc(z_read, 1)
            T.add("slot")
            act.wait_ge(z_read, 6)
            squares(QK, lambda c: qz[:, c, :])
            take_root(QK, 1)

            def att():
                b = T.n.get("att", 0) % 2
                T.add("att")
                T.add(f"att{b}")
                return ps[:, 4 + b, :], att_done[b], T.at(f"att{b}"), att_read[b]

            for hp in range(4):
                split_hi()
                act.wait_ge(q_done, 4 * hp + 1)
                if hp:
                    act.wait_ge(o_done, 2 * hp)
                act.activation(two(qn[:, 0, :]), pair[0], ACT.Copy).then_inc(q_copied, 1)
                act.wait_ge(q_done, 4 * hp + 2)
                act.activation(two(qn[:, 1, :]), pair[1], ACT.Copy).then_inc(q_copied, 1)
                act.wait_ge(slot_used, T.at("slot", 1))
                if hp:
                    act.wait_ge(rope_done, hp + 1)
                act.activation(two(qrz[:]), pair[0], ACT.Copy).then_inc(q_copied, 1)
                T.add("slot")
                split_hi()
                act.wait_ge(q_done, 4 * hp + 4)
                act.activation(kn[:], ps[:, 0:2, :], ACT.Copy).then_inc(q_copied, 1)
                src, done, count, read = att()
                act.wait_ge(done, count)
                act.activation(ukt[:].rearrange("p s r k -> p (s r k)"), src, ACT.Copy).then_inc(q_copied, 1)
                act.wait_ge(q_copied, 6 * hp + 5)
                act.sem_inc(read, 1)
                att()
                T.add("slot")
                split_hi()
                act.wait_ge(slot_used, T.at("slot", 1))
                act.activation(vh[:].rearrange("p (a c) n -> p a (c n)", a=2), ps[:, 2:4, :], ACT.Copy).then_inc(q_copied, 1)
                T.add("slot")
                for u in range(10):
                    if u < 8:
                        w = 8 * hp + u
                        n = (u % 4 + 1) * P
                        if w >= 3:
                            act.wait_ge(pt_t, w - 2)
                        src, done, count, read = att()
                        act.wait_ge(nb_done, w + 1)
                        act.activation(pp[:, w % 3, 0:n], src[:, 0:n], ACT.Exp, bias=nb[:, w:w + 1], scale=SM_SCALE,
                                       accum_out=rsum[:, w:w + 1]).then_inc(read, 1)
                    if u >= 2:
                        w = 8 * hp + u - 2
                        n = ((u - 2) % 4 + 1) * P
                        act.wait_ge(pt_t, w + 1)
                        act.activation(ppt[:, w % 2, 0:n], ps[:, 6 + w % 2, 0:n], ACT.Copy).then_inc(pt_copied, 1)

            split_hi()
            per = {"seq": 2, "ct": 8}

            def copy_pages(g):
                b = 4 * (g % 2)
                act.wait_ge(ct_t, T.at("ct", g + 1))
                act.activation(cts[g % 2][:, 0:2, :], ps[:, b:b + 2, :], ACT.Copy).then_inc(ct_copied_a, 1)

            def copy_scores(g):
                act.wait_ge(sc_mul, T.at("ct", g + 1))
                act.activation(srow[:, g * 512:(g + 1) * 512], ps[0:H, 3 + 4 * (g % 2), :], ACT.Copy
                               ).then_inc(sc_copied, 1)

            def sequence(more):
                copy_scores(0)
                copy_pages(2)
                copy_scores(1)
                copy_pages(3)
                copy_scores(2)
                copy_scores(3)
                T.add("ct", 4)
                act.wait_ge(smax_done, T.at("seq", 1))
                act.activation(srow[:], srow[:], ACT.Exp, bias=smx[:, 1:2], scale=SM_SCALE, accum_out=smx[:, 2:3]
                               ).then_inc(exp_done, 1)
                act.wait_ge(pts_t, T.at("seq", 1))
                act.activation(pts[:, 0:NPG, :].rearrange("p a h -> p (a h)"), ps[:, 7, 0:NPG * H], ACT.Copy)
                act.activation(pts[0:NS, NPG, :], ps[0:NS, 7, NPG * H:(NPG + 1) * H], ACT.Copy).then_inc(pts_copied, 1)
                T.add("seq")
                if more:
                    copy_pages(0)
                    copy_pages(1)

            copy_pages(0)
            copy_pages(1)
            with T.loop(act, NS // 2 - 1, per):
                sequence(True)
                sequence(True)
            sequence(True)
            sequence(False)
            T.add("slot")
            out_projection()
            norm(C_L1 + 48)
            ffn(False)

            x_root_of()
            for w in range(10):
                t, half = divmod(w, 2)
                act.wait_ge(y_t, w + 1)
                if t in (2, 3) and half == 0:
                    act.wait_ge(y_out[t % 2], 16)
                n = P if t < 4 else NS
                dst = ynat[:, t % 2, half * 512:(half + 1) * 512] if t < 4 else yns[:, half * 512:(half + 1) * 512]
                act.activation(dst, ps[0:n, 4 + w % 4, :], ACT.Copy).then_inc(y_copied, 1)

        @block.vector
        def _(dve):
            T = Tally()

            def link(ins):
                ins.then_inc(chain, 1)
                T.add("chain")
                dve.wait_ge(chain, T.at("chain"))

            def split_lo(part=None):
                k = T.n.get("split", 0)
                if k == SLOTS:
                    return
                r = k % RAW
                dve.wait_ge(hi_done, T.at("split", 1))
                n = T.words(k)
                c = {None: slice(0, n), 0: slice(0, n // 2), 1: slice(n // 2, n)}[part]
                ins = dve.tensor_tensor(w_lo[r][:, c], raw[r][:, c], w_hi[:, r, c], ALU.subtract)
                if part != 0:
                    ins.then_inc(split_done, 1)
                    T.add("split")

            def add_mods(col):
                dve.wait_ge(comb_done, T.at("comb", 1))
                dve.tensor_tensor(mods[:, bass.ds(col, 2), :], ps[:, 7, 0:2 * SEQS].rearrange("p (c s) -> p c s", c=2),
                                  bias[:, bass.ds(col, 2)].unsqueeze(2).broadcast_to([P, 2, SEQS]), ALU.add
                                  ).then_inc(mods_added, 1)
                T.add("comb")

            def ada(col):
                split_lo()
                T.add("slot")
                add_mods(col)

            def ada_run(first, n):
                for j in range(min(4, n)):
                    ada(2 * (first + j))
                full = max(0, n - 4) // 4
                if full:
                    with T.loop(dve, full, {"slot": 4, "split": 4, "comb": 4}) as i:
                        for j in range(4):
                            ada(i * 8 + 2 * (first + 4 + j))
                for j in range(4 + 4 * full, n):
                    ada(2 * (first + j))

            def split_act(src, hi, lo, done=None):
                link(dve.tensor_copy(hi, src))
                ins = dve.tensor_tensor(lo, src, hi, ALU.subtract)
                if done is not None:
                    ins.then_inc(done, 1)

            def add_square(c):
                dve.wait_ge(xsq_done, T.at("xn", c + 1, KD))
                if c == 0:
                    return
                if c >= 2:
                    dve.wait_ge(xsq_added, T.at("xn", c, KD - 1))
                first = sq[:, 0, :] if c == 1 else rstd[:]
                dve.tensor_tensor(rstd[:], first, sq[:, c % 2, :], ALU.add).then_inc(xsq_added, 2 if c == 1 else 1)

            def norm(base, gain, gate_base, factor, fresh=True):
                dve.wait_ge(mods_added, T.at("comb"))
                dve.scalar_tensor_tensor(amod[:], mods[:, base + KD:base + 2 * KD, :], 1.0,
                                         vec[:, gain:gain + KD].unsqueeze(2).broadcast_to([P, KD, SEQS]), ALU.add, ALU.mult)
                if gate_base is not None:
                    if T.n.get("res", 0):
                        dve.wait_ge(x_upd, T.at("res", 2, 2))
                    dve.tensor_scalar(gate[:], mods[:, gate_base:gate_base + KD, :].rearrange("p c s -> p (c s)"),
                                      factor, None, ALU.mult)
                if fresh:
                    T.add("xn")
                    dve.wait_ge(x_root, T.at("xn"))
                    link(dve.reciprocal(rstd[:], root[:]))
                for c in range(KD + 1):
                    if c < KD:
                        if c >= 2:
                            dve.wait_ge(aff_done, T.at("hn", c - 1))
                        dve.tensor_tensor(tn[:, c % 2, 0:NP], x[:, c, 0:NP], rstd[:, 0:NP], ALU.mult).then_inc(tn_done, 1)
                    if c == 0:
                        link(dve.tensor_tensor(ts[:], x[:, :, NP:NT], rstd[:, NP:NT].unsqueeze(1).broadcast_to([P, KD, NS]),
                                               ALU.mult))
                        link(dve.tensor_tensor(ts[:], ts[:], amod[:, :, 1:SEQS], ALU.mult))
                        link(dve.tensor_tensor(ts[:], ts[:], mods[:, base:base + KD, 1:SEQS], ALU.add))
                        split_act(ts[:], hn_hi[:, :, NP:NT], hn_lo[:, :, NP:NT])
                    else:
                        dve.wait_ge(aff_done, T.at("hn", c))
                        dve.tensor_tensor(hn_lo[:, c - 1, 0:NP], tt[:, (c - 1) % 2, 0:NP], hn_hi[:, c - 1, 0:NP],
                                          ALU.subtract).then_inc(hn_done, 1)
                T.add("hn", KD)

            def hidden(m, col=None):
                split_lo()
                if col is not None:
                    add_mods(col)
                dve.wait_ge(slot_used, T.at("slot", 1))
                dve.wait_ge(gate_read, T.at("up", 2))
                if T.n.get("up", 0):
                    dve.wait_ge(hid_done, T.at("up"))
                dve.tensor_tensor(two(hf[:]), pair[1], two(sg[:, T.n.get("up", 0) % 2, :]), ALU.mult).then_inc(up_read, 1)
                dve.wait_ge(up_read, T.at("up", 2))
                split_act(hf[:].unsqueeze(1), hid_hi[:, bass.ds(m, 1), :], hid_lo[:, bass.ds(m, 1), :], hid_done)
                T.add("up")
                T.add("slot")

            def residual(c, m):
                if m == 0:
                    dve.wait_ge(res_done, T.at("res", 1))
                else:
                    dve.wait_ge(slot_used, T.at("slot", 1))
                xc = x[:, bass.ds(c, 1), :]
                g0 = gate[:, bass.ds(c * SEQS, 1)]
                link(dve.tensor_tensor(t9[:, m, 0:NS], pair[m][:, 1, HT - NS:HT], gate[:, bass.ds(c * SEQS + 1, NS)],
                                       ALU.mult))
                for lo, hi, t in ((0, HT, 0), (HT, NP, 1)):
                    dve.scalar_tensor_tensor(xc[:, :, lo:hi], pair[m][:, t, 0:hi - lo].unsqueeze(1), g0,
                                             xc[:, :, lo:hi], ALU.mult, ALU.add)
                dve.tensor_tensor(xc[:, :, NP:NT], xc[:, :, NP:NT], t9[:, m, 0:NS].unsqueeze(1), ALU.add
                                  ).then_inc(x_upd, 1)

            def down(squares):
                for c in range(0, KD, 2):
                    split_lo()
                    T.add("slot")
                    split_lo()
                    for m in range(2):
                        residual(c + m, m)
                        if squares and c + m >= 2:
                            add_square(c + m - 1)
                    T.add("slot")
                    T.add("res")

            def ffn(col=None):
                done = 0

                def with_ada(m):
                    hidden(m, col + 2 * (done - 1) if done else None)
                    split_lo()
                    T.add("slot")

                for half, mn in ((0, MFA), (1, MFB)):
                    if col is None:
                        for m in range(mn):
                            hidden(m)
                    else:
                        for m in range(2):
                            with_ada(m)
                            done += 1
                        with T.loop(dve, (mn - 4) // 2, {"slot": 4, "split": 4, "up": 2, "comb": 2, "chain": 2}) as i:
                            for q in range(2):
                                hidden(i * 2 + (2 + q), i * 4 + (col + 2 * (done - 1 + q)))
                                split_lo()
                                T.add("slot")
                        done += mn - 4
                        for m in range(mn - 2, mn):
                            with_ada(m)
                            done += 1
                    down(half == 1)
                if col is not None:
                    add_mods(col + 2 * (done - 1))

            def out_projection():
                for s in range(4):
                    split_lo()
                    for m in range(2):
                        residual(2 * s + m, m)
                        if 2 * s + m >= 2:
                            add_square(2 * s + m - 1)
                    T.add("slot")
                    T.add("res")

            def hgrn_step(events, q, h, hnext, ada_cols):
                def att():
                    b = T.n.get("att", 0) % 2
                    T.add("att")
                    T.add(f"att{b}")
                    return ps[:, 4 + b, :], att_done[b], T.at(f"att{b}"), att_read[b]

                for kind, j, n in events:
                    if kind in ("tiles", "fresh"):
                        if j == 16 or kind == "fresh":
                            split_lo()
                        elif j in (6, 9):
                            split_lo(j // 9)
                        for c in range(4):
                            if not j < 8 * (c + 1) <= j + n:
                                continue
                            if c == 0:
                                dve.wait_ge(act_part, T.at("proj", 1, 2))
                                dve.tensor_tensor(two(qs[:, 1 - q, :]), pair[0], two(sgq[:]), ALU.mult).then_inc(q_read, 1)
                            elif c == 1:
                                dve.wait_ge(f_read, T.at("proj", 1))
                                lb, ub = low[:, 0, bass.ds(hnext, 1)], low[:, 1, bass.ds(hnext, 1)]
                                dve.tensor_scalar(fg[:, 1 - q, :], s1[:], ub, lb, ALU.mult, ALU.add)
                                dve.tensor_scalar(kk[:, 1 - q, :], s2[:], ub, None, ALU.mult).then_inc(fk_done, 1)
                                T.add("slot")
                            elif c == 3:
                                dve.wait_ge(act_part, T.at("proj", 2, 2))
                                dve.tensor_tensor(gg[:, bass.ds(hnext, 1), :].rearrange("p a (h n) -> p (a h) n", h=2),
                                                  pair[1], two(sgg[:]), ALU.mult).then_inc(g_read, 1)
                                T.add("slot")
                                T.add("proj")
                    elif kind == "norm":
                        hgrn_norm(j)
                    elif kind == "ada":
                        split_lo()
                        T.add("slot")
                    elif kind == "comb":
                        add_mods(ada_cols[j])
                    elif kind == "level":
                        src, done, count, read = att()
                        dve.wait_ge(done, count)
                        qh, kh, fh = qs[:, q, 0:NP], kk[:, q, 0:NP], fg[:, q, 0:NP]
                        if j == 0:
                            link(dve.memset(attn[:], 0.0))
                            dve.tensor_tensor(qh, qh, fh, ALU.mult).then_inc(level_ready, 1)
                        else:
                            m = 2 ** (j - 1)
                            blocks = NP // (2 * m)
                            t_in = fh if j == 1 else tot[:, NP - 4 * blocks:NP - 2 * blocks]
                            t_in = t_in.rearrange("p (b t) -> p b t", t=2)
                            kb = kh.rearrange("p (b t m) -> p b t m", t=2, m=m)
                            qb = qh.rearrange("p (b t m) -> p b t m", t=2, m=m)
                            link(dve.tensor_tensor(tot[:, NP - 2 * blocks:NP - blocks], t_in[:, :, 0], t_in[:, :, 1],
                                                   ALU.mult))
                            dve.tensor_tensor(kb[:, :, 0, :], kb[:, :, 0, :], t_in[:, :, 1:2].broadcast_to([P, blocks, m]),
                                              ALU.mult)
                            dve.tensor_tensor(qb[:, :, 1, :], qb[:, :, 1, :], t_in[:, :, 0:1].broadcast_to([P, blocks, m]),
                                              ALU.mult).then_inc(level_ready, 1)
                        dve.copy_predicated(attn[:].rearrange("p (c t) -> p c t", c=4),
                                            lmask[:, j, :].unsqueeze(1).broadcast_to([P, 4, P]),
                                            src.rearrange("p (c t) -> p c t", c=4)).then_inc(read, 1)
                    elif kind == "state":
                        src, done, count, read = att()
                        dve.wait_ge(done, count)
                        dve.wait_ge(st_free, T.at("head", 1))
                        link(dve.tensor_copy(st[:, 0, :], src[:, 0:P]))
                        for c in range(1, 4):
                            ins = dve.scalar_tensor_tensor(st[:, c, :], st[:, c - 1, :], tot[:, NP - 8 + c:NP - 7 + c],
                                                           src[:, c * P:(c + 1) * P], ALU.mult, ALU.add)
                            if c < 3:
                                link(ins)
                        ins.then_inc(st_done, 1)
                        dve.wait_ge(st_done, T.at("head", 1))
                        dve.sem_inc(read, 1)
                    elif kind == "outer":
                        src, done, count, read = att()
                        b0 = (T.n["att"] - 1) % 2
                        dve.wait_ge(read, T.at(f"att{b0}", 1))
                        if j == 0:
                            dve.wait_ge(ss_in[q], T.at(f"head{q}", 16, 16))
                        for b in range(4):
                            t = 4 * j + b
                            ins = dve.scalar_tensor_tensor(ss[:, q, t, :], ss[:, q, t, :], fg[:, q, NP + t:NP + t + 1],
                                                           kvo[:, b, :], ALU.mult, ALU.add)
                        ins.then_inc(ss_done, 1)
                    elif kind in ("vt", "kt", "out", "outs"):
                        att()
                        if kind == "outs":
                            T.add("head")
                            T.add(f"head{q}")

            def hgrn_norm(h):
                if h < ADA_TAIL:
                    split_lo()
                    T.add("slot")
                if h >= 1:
                    g = h - 1
                    dve.wait_ge(root_done, T.at("root", g + 1))
                    link(dve.reciprocal(rstd[:], norm_root[g % 2]))
                    link(dve.tensor_tensor(norm_t[0], og[:, g, :], rstd[:], ALU.mult))
                    link(dve.scalar_tensor_tensor(norm_t[1], norm_t[0], vec[:, V_HG + g:V_HG + g + 1],
                                                  gg[:, g, :], ALU.mult, ALU.mult))
                    split_act(norm_t[1], hn_hi[:, g, :], hn_lo[:, g, :], hn_done)
                if h < ADA_TAIL:
                    add_mods(C_L1 + 2 * (H + h))
                if h == H:
                    T.add("root", H)

            def small_norm(chunks, n, gain, hi, lo):
                dve.wait_ge(root_done, T.at("root", 1))
                T.add("root")
                link(dve.reciprocal(tn[:, 1, :], root[:]))
                for c in range(n):
                    link(dve.scalar_tensor_tensor(chunks[:, c, :], chunks[:, c, :], vec[:, gain + c:gain + c + 1],
                                                  tn[:, 1, :], ALU.mult, ALU.mult))
                    split_act(chunks[:, c, :], hi[:, c, :], lo[:, c, :])

            dve.sem_inc(up_read, 1)
            dve.sem_inc(x_upd, 2)
            dve.sem_inc(ss_done, 1)
            dve.sem_inc(ct_copied_d, 2)
            dve.sem_inc(ols_done, 1)
            dve.memset(ones[:], 1.0)
            dve.memset(eps[:], EPS)
            for _ in range(AHEAD):
                split_lo()
            dve.wait_ge(s_in, 16 * 13)
            dve.tensor_copy(ident_r[:], ident)
            dve.wait_ge(start_c, 1)
            scv = scf[:]
            link(dve.tensor_copy(sc18[:, :, 0:SEQS], scv))
            dve.tensor_tensor(sc18[:, :, SEQS:], scv, sc18[:, :, 0:SEQS], ALU.subtract).then_inc(sc_done, 1)
            dve.wait_ge(start_c, 2)
            dve.tensor_tensor(low[:, 0, :], vec[:, V_LB:V_LB + H], vec[:, V_LB + H:V_LB + 2 * H], ALU.subtract
                              ).then_inc(low_ready, 1)
            for c in range(KD):
                dve.wait_ge(x_t, c + 1)
                dve.tensor_copy(x[:, c, 0:NP], ps[:, c % 4, :]).then_inc(x_placed, 1)
            dve.wait_ge(x_t, KD + 1)
            dve.tensor_copy(x[:, :, NP:NT], ps[:, 7, 0:KD * NS].rearrange("p (c s) -> p c s", c=KD)).then_inc(x_placed, 1)
            dve.wait_ge(start_c, 4)
            dve.wait_ge(s_tab, 16)
            ada_run(0, ADA_FIRST)
            for c in range(1, KD - 1):
                add_square(c)
            norm(C_L0, V_NORM, C_L0 + 16, 0.5)
            ffn(C_L0 + 2 * ADA_FIRST)
            norm(C_L0 + 24, V_NORM + 8, C_L0 + 40, 1.0)
            hgrn_step(project_events(), 1, None, 0, (C_KV, C_L1))
            per = {"slot": 8, "split": 8, "comb": 4, "proj": 2, "att": 30, "att0": 15, "att1": 15, "head": 2,
                   "head0": 1, "head1": 1, "chain": 22}
            with T.loop(dve, 3, per) as i:
                for q in range(2):
                    hgrn_step(hgrn_events(True), q, i * 2 + q, i * 2 + (q + 1),
                              (i * 4 + (C_KV + 2 + 2 * q), i * 4 + (C_L1 + 2 + 2 * q)))
            hgrn_step(hgrn_events(True), 0, 6, 7, (C_KV + 14, C_L1 + 14))
            hgrn_step(last_events(), 1, 7, None, None)
            out_projection()
            norm(C_L0 + 48, V_NORM + 16, C_L0 + 64, 0.5)
            ffn(C_L1 + 2 * (H + ADA_TAIL))

            norm(C_KV, V_KVN, None, None)
            split_lo()
            T.add("slot")
            split_lo()
            T.add("slot")
            dve.wait_ge(st_out, 16 * H)
            for j in range(2):
                dve.wait_ge(ss_out[j], 16 * H // 2)
            small_norm(z, RK, V_LAT, ck_hi, ck_lo)
            dve.tensor_copy(cnew[:], z[:, 0:RK, NP:NT]).then_inc(lat_done, 1)
            dve.wait_ge(s_tab, 32)
            cos, sin = cossin[:, 0, :], cossin[:, 1, :]
            dve.wait_ge(z_read, 3)
            dve.tensor_tensor(kr2[:], zr[:], cos, ALU.mult)
            dve.wait_ge(z_done, 2)
            link(dve.tensor_tensor(two(tn[:, 0, :]), pair[0], two(sin), ALU.mult))
            dve.tensor_tensor(kr2[:], kr2[:], tn[:, 0, :], ALU.add).then_inc(rope_done, 1)
            dve.wait_ge(rope_done, 1)
            norm(C_L1, V_NORM + 24, C_L1 + 16, 0.5, False)
            for j in range(2):
                dve.wait_ge(nat_out[j], 64)
            ffn()

            norm(C_L1 + 24, V_NORM + 32, C_L1 + 40, 1.0)
            split_lo()
            T.add("slot")
            split_lo()
            T.add("slot")
            link(dve.memset(qr[:], 0.0))
            small_norm(qz, QK, V_Q, qc_hi, qc_lo)
            dve.memset(t9[:, 1, 0:1], 0.0).then_inc(lat_done, 1)

            def att():
                b = T.n.get("att", 0) % 2
                T.add("att")
                T.add(f"att{b}")
                return ps[:, 4 + b, :], att_done[b], T.at(f"att{b}"), att_read[b]

            for hp in range(4):
                split_lo()
                T.add("slot")
                dve.wait_ge(q_copied, 6 * hp + 3)
                dve.wait_ge(q_done, 4 * hp + 3)
                for s in range(2):
                    rp = slice(s * ROPE, (s + 1) * ROPE)
                    dve.tensor_tensor(qr[rp, s, :], qrz[rp, :], cos[rp, :], ALU.mult)
                link(dve.tensor_tensor(two(tn_m[:]), pair[1], two(sin), ALU.mult))
                for s in range(2):
                    rp = slice(s * ROPE, (s + 1) * ROPE)
                    ins = dve.tensor_tensor(qr[rp, s, :], qr[rp, s, :], tn_m[rp, :], ALU.add)
                ins.then_inc(rope_done, 1)
                split_lo()
                T.add("slot")
                att()
                src, done, count, read = att()
                dve.wait_ge(done, count)
                for s in range(2):
                    for r in range(RK):
                        dve.tensor_copy(ql[:, r, :, 2 * hp + s], src[:, (2 * s + r) * NS:(2 * s + r + 1) * NS])
                dve.tensor_copy(qrs[:, :, 2 * hp], qr[0:ROPE, 0, NP:NT])
                dve.tensor_copy(qrs[:, :, 2 * hp + 1], src[0:ROPE, 4 * NS:5 * NS]).then_inc(read, 1)
                split_lo()
                T.add("slot")
                for u in range(9):
                    if u < 8:
                        w = 8 * hp + u
                        t = u % 4
                        src, done, count, read = att()
                        dve.wait_ge(done, count)
                        diag = src[:, t * P:(t + 1) * P]
                        link(dve.tensor_tensor(diag, diag, causal, ALU.add))
                        link(dve.tensor_reduce(mx[:, w:w + 1], src[:, 0:(t + 1) * P], AX_X, ALU.max))
                        dve.tensor_scalar(nb[:, w:w + 1], mx[:, w:w + 1], -SM_SCALE, None, ALU.mult).then_inc(nb_done, 1)
                        exp_bank = read, count + 1
                    if u >= 1:
                        w = 8 * hp + u - 1
                        n = ((u - 1) % 4 + 1) * P
                        dve.wait_ge(*last_bank)
                        link(dve.reciprocal(rinv[:, w:w + 1], rsum[:, w:w + 1]))
                        dve.tensor_scalar(pp[:, w % 3, 0:n], pp[:, w % 3, 0:n], rinv[:, w:w + 1], None, ALU.mult
                                          ).then_inc(p_done, 1)
                    if u < 8:
                        last_bank = exp_bank
                    if u in (7, 8):
                        s = 0 if u == 7 else 1
                        h = 2 * hp + s
                        dve.wait_ge(o_done, h + 1)
                        link(dve.tensor_copy(hn_hi[:, h, 0:NP], ps[:, 2 * s, :]))
                        dve.tensor_tensor(hn_lo[:, h, 0:NP], ps[:, 2 * s, :], hn_hi[:, h, 0:NP], ALU.subtract
                                          ).then_inc(o_read, 1)

            split_lo()
            per = {"seq": 2, "ct": 8, "chain": 10}

            def copy_rope(g):
                dve.wait_ge(ct_t, T.at("ct", g + 1))
                dve.tensor_copy(cts[g % 2][0:ROPE, 2, :], ps[0:ROPE, 4 * (g % 2) + 2, :]).then_inc(ct_copied_d, 1)

            def queries(seq, q):
                for r in range(RK):
                    dve.tensor_copy(qsamp[:, q, r, :].unsqueeze(1), ql[:, r, bass.ds(seq, 1), :])
                dve.tensor_copy(qsamp[0:ROPE, q, RK, :].unsqueeze(1), qrs[:, bass.ds(seq, 1), :]).then_inc(qs_ready, 1)

            def maximum(g, extra=0):
                dve.wait_ge(sc_copied, T.at("ct", g + 1))
                return dve.tensor_reduce(smx[:, 4 + g:5 + g], srow[:, g * 512:(g + 1) * 512 + extra], AX_X, ALU.max)

            def sequence(seq, q, more):
                copy_rope(2)
                maximum(0)
                copy_rope(3)
                maximum(1)
                maximum(2)
                dve.wait_ge(new_mul, T.at("seq", 1))
                link(dve.tensor_tensor(srow[:, PAST:PAST + NS], ps[0:H, 3, 0:NS], newmask[:, bass.ds(seq * NS, NS)], ALU.add))
                link(maximum(3, NS))
                T.add("ct", 4)
                link(dve.tensor_reduce(smx[:, 0:1], smx[:, 4:8], AX_X, ALU.max))
                dve.tensor_scalar(smx[:, 1:2], smx[:, 0:1], -SM_SCALE, None, ALU.mult).then_inc(smax_done, 1)
                if more:
                    queries(seq + 1, 1 - q)
                    copy_rope(0)
                    copy_rope(1)
                dve.wait_ge(exp_done, T.at("seq", 1))
                link(dve.reciprocal(smx[:, 3:4], smx[:, 2:3]))
                dve.wait_ge(pages_used, T.at("seq", 3))
                dve.tensor_scalar(ol[:], ps[0:H, 3, 0:KV], smx[:, 3:4], None, ALU.mult).then_inc(ol_done, 1)
                dve.wait_ge(olt_done, T.at("seq", 1))
                link(dve.tensor_copy(ols[:, :, bass.ds(seq, 1), :].rearrange("p r a h -> p r (a h)"),
                                     ps[:, 7, 0:RK * H].rearrange("p (r h) -> p r h", r=RK)))
                dve.sem_inc(ols_done, 1)
                T.add("seq")

            queries(0, 0)
            copy_rope(0)
            copy_rope(1)
            with T.loop(dve, NS // 2 - 1, per) as i:
                sequence(i * 2, 0, True)
                sequence(i * 2 + 1, 1, True)
            sequence(NS - 2, 0, True)
            sequence(NS - 1, 1, False)
            olf = ols[:].rearrange("p r b h -> p (r b h)")
            split_act(olf, ol_hi[:].rearrange("p r b h -> p (r b h)"), ol_lo[:].rearrange("p r b h -> p (r b h)"), olsplit)
            dve.wait_ge(slot_used, T.at("slot", 1))
            T.add("slot")
            heads = ps[:, 0, 0:H * NS].rearrange("p (h s) -> p h s", h=H)
            link(dve.tensor_copy(hn_hi[:, :, NP:NT], heads))
            dve.tensor_tensor(hn_lo[:, :, NP:NT], heads, hn_hi[:, :, NP:NT], ALU.subtract).then_inc(os_split, 1)
            out_projection()
            norm(C_L1 + 48, V_NORM + 40, C_L1 + 64, 0.5)
            ffn()

            dve.wait_ge(x_root, T.at("xn", 1))
            link(dve.reciprocal(rstd[:], root[:]))
            for c in range(KD):
                dve.scalar_tensor_tensor(yt[:, c, :], x[:, c, :], vec[:, V_FINAL + c:V_FINAL + c + 1], rstd[:],
                                         ALU.mult, ALU.mult).then_inc(y_done, 1)


_INS = ["x_prompt", "x_sample", "c_prompt", "c_sample", "state_hgrn", "cache_ckv", "cache_krope", "page_table", "w_ada",
        "b_ada", "g_norm", "w_ffn_gu", "w_ffn_down", "hg_w_in", "hg_lb", "hg_g_out", "hg_w_out", "kv_w_ada",
        "kv_b_ada", "kv_g_norm", "kv_w_down", "kv_g_latent", "kv_w_uk", "kv_w_uv", "q_w_down", "q_g_norm", "q_w_up",
        "attn_w_out", "g_final"]
_OUTS = [(1, NP, D), (NS, 1, D), (1, 1, H, P, P), (1, NS, H, P, P), (1, NP, KV), (1, NP, ROPE), (NS, 1, KV),
         (NS, 1, ROPE)]


def _tables():
    import numpy as np
    c = np.zeros((P, K_END), np.float32)
    c[:, K_ID:K_ID + P] = np.eye(P)
    half = ROPE // 2
    for base in (0, ROPE):
        for n in range(half):
            c[base + n + half, K_ROT + base + n] = -1.0
            c[base + n, K_ROT + base + n + half] = 1.0
    c[:, K_CAUS:K_CAUS + P] = np.triu(np.full((P, P), NEG, np.float32), 1)
    for n in range(SEQS):
        c[n, K_COMB + n] = c[SEQS + n, K_COMB + n] = 1.0
    new = np.full((NS, NS), NEG, np.float32)
    np.fill_diagonal(new, 0.0)
    c[0:H, K_NEW:K_NEW + 64] = new.reshape(1, 64)
    masks = np.zeros((P, 8, P), np.uint32)
    for s in range(P):
        for t in range(s, P):
            masks[s, (s ^ t).bit_length(), t] = 1
    pos = np.concatenate([np.arange(NP), np.full(NS, PAST)]).astype(np.float32)
    freq = (np.float32(10000.0) ** (np.float32(-2.0) * np.arange(half, dtype=np.float32) / np.float32(ROPE))).astype(np.float32)
    ang = (pos[None, :] * np.tile(freq, 4)[:, None]).astype(np.float32)
    rotary = np.stack([np.cos(ang), np.sin(ang)], axis=1).astype(np.float32)
    return {"consts": c, "level_masks": masks, "rotary": rotary}


def kernel(**inputs):
    import numpy as _np
    import concourse.bacc as _bacc
    from concourse import mybir as _mybir
    from concourse.bass_utils import run_bass_kernel_spmd as _run

    nc = _bacc.Bacc("TRN2", target_bir_lowering=False, num_devices=1)
    arrays, aps = {}, {}
    given = {n: _np.ascontiguousarray(inputs[n]) for n in _INS}
    given.update(_tables())
    for name, a in given.items():
        arrays[f"in_{name}"] = a
        aps[name] = nc.dram_tensor(f"in_{name}", a.shape, _mybir.dt.from_np(a.dtype), kind="ExternalInput").ap()
    outs = [nc.dram_tensor(f"out_{i}", s, _mybir.dt.float32, kind="ExternalOutput").ap() for i, s in enumerate(_OUTS)]
    build(nc, aps, *outs)
    r = _run(nc, [arrays], core_ids=[0])
    return tuple(r.results[0][f"out_{i}"] for i in range(len(_OUTS)))
```
